# Optimizing a Trainium2 kernel written in Bass

```python
import math
import jax
import jax.numpy as jnp
from jax import lax
import numpy as np

D_MODEL = 1024
BATCH = 1
SEQ = 1024
DEPTH = 1
DEC_BATCH = 8
DEC_SEQ = 1
PAST_LEN = 1024
PAGE_SIZE = 128

D_RNN = D_MODEL
LRU_BLOCKS = 4
LRU_BW = D_RNN // LRU_BLOCKS
CONV_W = 4
LRU_C = 8.0
NSA_HEADS = 8
NSA_KV = 2
NSA_GRP = NSA_HEADS // NSA_KV
NSA_HD = 64
CMP_STRIDE = 16
CMP_LEN = 2 * CMP_STRIDE
CMP_HID = 2 * NSA_HD
SEL_BLK = 64
TOP_N = 16
WINDOW = 512
Q_BLOCK = 128
MEM_HEADS = 4
MEM_HD = 128
N_MEM = 256
REL_BUCKETS = 32
REL_MAX_DIST = 128
D_FF = -(-8 * D_MODEL // (3 * 256)) * 256
N_BRANCH = 3
EPS = 1e-6
NEG = -1e30
FORCE_SCORE = 1e6
SPLITS = (D_RNN, D_RNN, NSA_HEADS * NSA_HD, 3 * 2 * NSA_KV * NSA_HD, 3 * NSA_HEADS, MEM_HEADS * MEM_HD, N_BRANCH * D_MODEL)
N_IN = sum(SPLITS)

kernel_name = 'griffin_nsa_memory_hybrid_step'

def rmsnorm(x, g):
    xf = x.astype(jnp.float32)
    return xf * lax.rsqrt(jnp.mean(xf * xf, axis=-1, keepdims=True) + EPS) * g.astype(jnp.float32)

def masked_softmax(logits, mask):
    z = jnp.where(mask, logits.astype(jnp.float32), NEG)
    z = jnp.exp(z - jnp.max(z, axis=-1, keepdims=True)) * mask
    return z / jnp.maximum(jnp.sum(z, axis=-1, keepdims=True), 1e-30)

def t5_bucket(dist):
    n = jnp.maximum(dist, 0)
    exact = REL_BUCKETS // 2
    nf = jnp.maximum(n, 1).astype(jnp.float32)
    large = exact + (jnp.log(nf / exact) / math.log(REL_MAX_DIST / exact) * (REL_BUCKETS - exact)).astype(jnp.int32)
    return jnp.where(n < exact, n, jnp.minimum(large, REL_BUCKETS - 1))

def bias_qk(qpos, kpos, table):
    b = table.astype(jnp.float32)[t5_bucket(qpos[:, None] - kpos[None, :])]
    return b.reshape(b.shape[0], b.shape[1], NSA_KV, NSA_GRP).transpose(0, 2, 3, 1)

def compress(rows, pe, w1, w2):
    B, L, G, D = rows.shape
    n_ch = L // CMP_STRIDE
    ch = rows[:, :n_ch * CMP_STRIDE].reshape(B, n_ch, CMP_STRIDE, G, D)
    ch = ch.transpose(0, 1, 3, 2, 4).reshape(B, n_ch, G, CMP_STRIDE * D)
    half = CMP_STRIDE * D
    pos_term = pe.reshape(-1) @ w1
    h = ch[:, :-1] @ w1[:half] + ch[:, 1:] @ w1[half:] + pos_term
    return jax.nn.gelu(h) @ w2

def overlap_matrix(n_cmp, n_sel):
    cs = jnp.arange(n_cmp)[:, None] * CMP_STRIDE
    ss = jnp.arange(n_sel)[None, :] * SEL_BLK
    return ((cs < ss + SEL_BLK) & (cs + CMP_LEN > ss)).astype(jnp.float32)

def nsa_attend(q, qpos, kc, vc, ks, vs, kw, vw, wpos, gates, table):
    B, Q = q.shape[:2]
    G, R, D = NSA_KV, NSA_GRP, NSA_HD
    scale = D ** -0.5
    qg = q.reshape(B, Q, G, R, D)
    NC = kc.shape[1]
    cpos = jnp.arange(NC, dtype=jnp.int32) * CMP_STRIDE + (CMP_LEN - 1)
    lc = jnp.einsum('bqgrd,bcgd->bqgrc', qg, kc) * scale + bias_qk(qpos, cpos, table)[None]
    pc = masked_softmax(lc, (cpos[None, :] <= qpos[:, None])[None, :, None, None, :])
    oc = jnp.einsum('bqgrc,bcgd->bqgrd', pc, vc)
    NS = ks.shape[2]
    ssum = jnp.einsum('bqgrc,cs->bqgs', pc, overlap_matrix(NC, NS))
    blk = jnp.arange(NS, dtype=jnp.int32)[None, :]
    cur = (qpos // SEL_BLK)[:, None]
    forced = ((blk == 0) | (blk == cur) | (blk == cur - 1))[None, :, None, :]
    valid = (blk <= cur)[None, :, None, :]
    score = jnp.where(forced, FORCE_SCORE, jnp.where(valid, ssum, -1.0))
    n_top = min(TOP_N, NS)
    _, idx = lax.top_k(score, n_top)
    idx_t = idx.transpose(0, 2, 1, 3)
    take = jax.vmap(jax.vmap(lambda blocks, ids: blocks[ids]))
    ksel = take(ks, idx_t)
    vsel = take(vs, idx_t)
    spos = idx_t[..., None] * SEL_BLK + jnp.arange(SEL_BLK, dtype=jnp.int32)
    tg = table.astype(jnp.float32).reshape(REL_BUCKETS, G, R).transpose(1, 0, 2)
    sb = tg[jnp.arange(G)[None, :, None, None, None], t5_bucket(qpos[None, None, :, None, None] - spos)]
    ls = jnp.einsum('bqgrd,bgqnsd->bgqrns', qg, ksel) * scale + sb.transpose(0, 1, 2, 5, 3, 4)
    smask = (spos <= qpos[None, None, :, None, None])[:, :, :, None]
    ps = masked_softmax(ls.reshape(B, G, Q, R, n_top * SEL_BLK), smask.reshape(B, G, Q, 1, n_top * SEL_BLK))
    osel = jnp.einsum('bgqrm,bgqmd->bqgrd', ps, vsel.reshape(B, G, Q, n_top * SEL_BLK, D))
    lw = jnp.einsum('bqgrd,bwgd->bqgrw', qg, kw) * scale + bias_qk(qpos, wpos, table)[None]
    dw = qpos[:, None] - wpos[None, :]
    wmask = (dw >= 0) & (dw < WINDOW) & (wpos[None, :] >= 0)
    pw = masked_softmax(lw, wmask[None, :, None, None, :])
    ow = jnp.einsum('bqgrw,bwgd->bqgrd', pw, vw)
    g = gates.reshape(B, Q, G, R, 3)
    o = g[..., 0:1] * oc + g[..., 1:2] * osel + g[..., 2:3] * ow
    return o.reshape(B, Q, G * R * D)

def project(x, p):
    B, T, _ = x.shape
    z = rmsnorm(x, p['norm_mix']) @ p['w_in']
    bounds, acc = [], 0
    for width in SPLITS[:-1]:
        acc += width
        bounds.append(acc)
    lru_x, lru_gate, q, kv, ng, mq, mg = jnp.split(z, bounds, axis=-1)
    q = rmsnorm(q.reshape(B, T, NSA_HEADS, NSA_HD), p['g_nsa_q'])
    kv = kv.reshape(B, T, 3, 2, NSA_KV, NSA_HD)
    cmp_kv = kv[:, :, 0]
    sel_kv = jnp.stack([rmsnorm(kv[:, :, 1, 0], p['g_nsa_k'][1]), kv[:, :, 1, 1]], axis=2)
    win_kv = jnp.stack([rmsnorm(kv[:, :, 2, 0], p['g_nsa_k'][2]), kv[:, :, 2, 1]], axis=2)
    nsa_gates = jax.nn.sigmoid(ng.reshape(B, T, NSA_HEADS, 3))
    mem_q = rmsnorm(mq.reshape(B, T, MEM_HEADS, MEM_HD), p['g_mem_q'])
    merge = jax.nn.sigmoid(mg.reshape(B, T, N_BRANCH, D_MODEL))
    return lru_x, lru_gate, q, cmp_kv, sel_kv, win_kv, nsa_gates, mem_q, merge

def lru_branch(xb, gate, conv_prev, h0, p):
    B, T, W = xb.shape
    xp = jnp.concatenate([conv_prev.astype(xb.dtype), xb], axis=1)
    xc = p['conv_b'] + xp[:, 0:T] * p['conv_w'][0]
    for k in range(1, CONV_W):
        xc = xc + xp[:, k:k + T] * p['conv_w'][k]
    xr = xc.reshape(B, T, LRU_BLOCKS, LRU_BW)
    r = jax.nn.sigmoid(jnp.einsum('btnc,ncd->btnd', xr, p['w_lru_a']).reshape(B, T, W).astype(jnp.float32) + p['b_lru_a'])
    i = jax.nn.sigmoid(jnp.einsum('btnc,ncd->btnd', xr, p['w_lru_i']).reshape(B, T, W).astype(jnp.float32) + p['b_lru_i'])
    log_a = -LRU_C * r * jax.nn.softplus(-p['lru_lambda'].astype(jnp.float32))
    a = jnp.exp(log_a)
    b = jnp.sqrt(-jnp.expm1(2.0 * log_a)) * (i * xc.astype(jnp.float32))
    b = b.at[:, 0].add(a[:, 0] * h0.astype(jnp.float32))
    _, h = lax.associative_scan(lambda e1, e2: (e1[0] * e2[0], e2[0] * e1[1] + e2[1]), (a, b), axis=1)
    return h * jax.nn.gelu(gate.astype(jnp.float32)), xp[:, T:], h[:, -1]

def mem_kv_proj(mem, p):
    B, M, _ = mem.shape
    kv = (rmsnorm(mem, p['norm_mem']) @ p['w_mem_kv']).reshape(B, M, 2, MEM_HEADS, MEM_HD)
    return jnp.stack([rmsnorm(kv[:, :, 0], p['g_mem_k']), kv[:, :, 1]], axis=2)

def mem_attend(mq, mkv):
    B, T = mq.shape[:2]
    logits = jnp.einsum('bthd,bmhd->bhtm', mq, mkv[:, :, 0].astype(jnp.float32)) * MEM_HD ** -0.5
    o = jnp.einsum('bhtm,bmhd->bthd', jax.nn.softmax(logits, axis=-1), mkv[:, :, 1].astype(jnp.float32))
    return o.reshape(B, T, MEM_HEADS * MEM_HD)

def merge_ffn(x, o_lru, o_nsa, o_mem, merge, p):
    z = (merge[:, :, 0] * (o_lru @ p['w_up_a']) + merge[:, :, 1] * (o_nsa @ p['w_up_b'])
         + merge[:, :, 2] * (o_mem @ p['w_up_m']))
    h = x + z @ p['w_o']
    f = rmsnorm(h, p['norm_ffn'])
    return h + (jax.nn.silu(f @ p['w_ffn_gate']) * (f @ p['w_ffn_up'])) @ p['w_ffn_down']

def prompt_layer(x, mem, table, p):
    B, T, _ = x.shape
    lru_x, lru_gate, q, cmp_kv, sel_kv, win_kv, ngate, mq, merge = project(x, p)
    o_lru, conv_new, h_new = lru_branch(lru_x, lru_gate, jnp.zeros((B, CONV_W - 1, D_RNN), lru_x.dtype),
                                        jnp.zeros((B, D_RNN), jnp.float32), p)
    kc = rmsnorm(compress(cmp_kv[:, :, 0], p['pe_cmp_k'], p['w_cmp_k1'], p['w_cmp_k2']), p['g_nsa_k'][0])
    vc = compress(cmp_kv[:, :, 1], p['pe_cmp_v'], p['w_cmp_v1'], p['w_cmp_v2'])
    ns = T // SEL_BLK
    ks = sel_kv[:, :, 0].reshape(B, ns, SEL_BLK, NSA_KV, NSA_HD).transpose(0, 3, 1, 2, 4)
    vs = sel_kv[:, :, 1].reshape(B, ns, SEL_BLK, NSA_KV, NSA_HD).transpose(0, 3, 1, 2, 4)
    w_pad = jnp.pad(win_kv, ((0, 0), (WINDOW, 0), (0, 0), (0, 0), (0, 0)))

    def block(bi):
        q0 = bi * Q_BLOCK
        qpos = q0 + jnp.arange(Q_BLOCK, dtype=jnp.int32)
        qb = lax.dynamic_slice_in_dim(q, q0, Q_BLOCK, axis=1)
        gb = lax.dynamic_slice_in_dim(ngate, q0, Q_BLOCK, axis=1)
        wkv = lax.dynamic_slice_in_dim(w_pad, q0, WINDOW + Q_BLOCK, axis=1)
        wpos = q0 - WINDOW + jnp.arange(WINDOW + Q_BLOCK, dtype=jnp.int32)
        return nsa_attend(qb, qpos, kc, vc, ks, vs, wkv[:, :, 0], wkv[:, :, 1], wpos, gb, table)

    o_nsa = lax.map(block, jnp.arange(T // Q_BLOCK, dtype=jnp.int32))
    o_nsa = o_nsa.transpose(1, 0, 2, 3).reshape(B, T, NSA_HEADS * NSA_HD)
    mkv = mem_kv_proj(mem, p)
    o_mem = mem_attend(mq, mkv)
    y = merge_ffn(x, o_lru, o_nsa, o_mem, merge, p)
    return y, cmp_kv, sel_kv, win_kv[:, -min(WINDOW, T):], mkv, h_new, conv_new

def sample_layer(x, cmp_pool, sel_pool, page_table, win_buf, mem_kv, h0, conv0, table, p):
    DB, S, _ = x.shape
    past = page_table.shape[1] * cmp_pool.shape[1]
    L = past + S
    lru_x, lru_gate, q, cmp_kv, sel_kv, win_kv, ngate, mq, merge = project(x, p)
    o_lru, conv_new, h_new = lru_branch(lru_x, lru_gate, conv0, h0, p)

    def gather_past(pool):
        return pool[page_table].reshape(DB, past, 2, NSA_KV, NSA_HD)

    cmp_all = jnp.concatenate([gather_past(cmp_pool), cmp_kv], axis=1)
    kc = rmsnorm(compress(cmp_all[:, :, 0], p['pe_cmp_k'], p['w_cmp_k1'], p['w_cmp_k2']), p['g_nsa_k'][0])
    vc = compress(cmp_all[:, :, 1], p['pe_cmp_v'], p['w_cmp_v1'], p['w_cmp_v2'])
    ns = -(-L // SEL_BLK)
    sel_all = jnp.concatenate([gather_past(sel_pool), sel_kv], axis=1)
    sel_all = jnp.pad(sel_all, ((0, 0), (0, ns * SEL_BLK - L), (0, 0), (0, 0), (0, 0)))
    ks = sel_all[:, :, 0].reshape(DB, ns, SEL_BLK, NSA_KV, NSA_HD).transpose(0, 3, 1, 2, 4)
    vs = sel_all[:, :, 1].reshape(DB, ns, SEL_BLK, NSA_KV, NSA_HD).transpose(0, 3, 1, 2, 4)
    wb = win_buf.shape[1]
    win_all = jnp.concatenate([win_buf, win_kv], axis=1)
    wpos = past - wb + jnp.arange(wb + S, dtype=jnp.int32)
    qpos = past + jnp.arange(S, dtype=jnp.int32)
    o_nsa = nsa_attend(q, qpos, kc, vc, ks, vs, win_all[:, :, 0], win_all[:, :, 1], wpos, ngate, table)
    o_mem = mem_attend(mq, mem_kv)
    y = merge_ffn(x, o_lru, o_nsa, o_mem, merge, p)
    return y, cmp_kv, sel_kv, win_all[:, -wb:], h_new, conv_new

def setup_inputs(seed: int = 0) -> dict:
    key = jax.random.key(seed)
    keys = iter(jax.random.split(key, 64))

    def nrm(shape, scale):
        return jax.random.normal(next(keys), shape, jnp.float32) * scale

    def gain(shape):
        return 1.0 + nrm(shape, 0.02)

    n_pages = PAST_LEN // PAGE_SIZE
    n_pool = (DEC_BATCH * n_pages * 5) // 4
    wb = min(WINDOW, PAST_LEN)
    page_table = jax.random.permutation(next(keys), n_pool)[:DEC_BATCH * n_pages].reshape(DEC_BATCH, n_pages).astype(jnp.int32)
    u = jax.random.uniform(next(keys), (DEPTH, D_RNN), jnp.float32, 0.9, 0.999)
    a0 = u ** (1.0 / LRU_C)
    lru_lambda = jnp.log(a0) - jnp.log1p(-a0)
    return {
        'x_prompt': nrm((BATCH, SEQ, D_MODEL), 1.0),
        'x_sample': nrm((DEC_BATCH, DEC_SEQ, D_MODEL), 1.0),
        'mem_prompt': nrm((BATCH, N_MEM, D_MODEL), 1.0),
        'cache_cmp_kv': nrm((DEPTH, n_pool, PAGE_SIZE, 2, NSA_KV, NSA_HD), 1.0),
        'cache_sel_kv': nrm((DEPTH, n_pool, PAGE_SIZE, 2, NSA_KV, NSA_HD), 1.0),
        'page_table': page_table,
        'cache_win_kv': nrm((DEPTH, DEC_BATCH, wb, 2, NSA_KV, NSA_HD), 1.0),
        'cache_mem_kv': nrm((DEPTH, DEC_BATCH, N_MEM, 2, MEM_HEADS, MEM_HD), 1.0),
        'state_lru_h': nrm((DEPTH, DEC_BATCH, D_RNN), 0.5),
        'state_conv': nrm((DEPTH, DEC_BATCH, CONV_W - 1, D_RNN), 1.0),
        'rel_bias': nrm((REL_BUCKETS, NSA_HEADS), 0.5),
        'norm_mix': gain((DEPTH, D_MODEL)),
        'w_in': nrm((DEPTH, D_MODEL, N_IN), D_MODEL ** -0.5),
        'conv_w': nrm((DEPTH, CONV_W, D_RNN), CONV_W ** -0.5),
        'conv_b': nrm((DEPTH, D_RNN), 0.01),
        'w_lru_a': nrm((DEPTH, LRU_BLOCKS, LRU_BW, LRU_BW), LRU_BW ** -0.5),
        'b_lru_a': nrm((DEPTH, D_RNN), 0.01),
        'w_lru_i': nrm((DEPTH, LRU_BLOCKS, LRU_BW, LRU_BW), LRU_BW ** -0.5),
        'b_lru_i': nrm((DEPTH, D_RNN), 0.01),
        'lru_lambda': lru_lambda,
        'g_nsa_q': gain((DEPTH, NSA_HD)),
        'g_nsa_k': gain((DEPTH, 3, NSA_HD)),
        'pe_cmp_k': nrm((DEPTH, CMP_LEN, NSA_HD), 0.5),
        'w_cmp_k1': nrm((DEPTH, CMP_LEN * NSA_HD, CMP_HID), (CMP_LEN * NSA_HD) ** -0.5),
        'w_cmp_k2': nrm((DEPTH, CMP_HID, NSA_HD), CMP_HID ** -0.5),
        'pe_cmp_v': nrm((DEPTH, CMP_LEN, NSA_HD), 0.5),
        'w_cmp_v1': nrm((DEPTH, CMP_LEN * NSA_HD, CMP_HID), (CMP_LEN * NSA_HD) ** -0.5),
        'w_cmp_v2': nrm((DEPTH, CMP_HID, NSA_HD), CMP_HID ** -0.5),
        'norm_mem': gain((DEPTH, D_MODEL)),
        'w_mem_kv': nrm((DEPTH, D_MODEL, 2 * MEM_HEADS * MEM_HD), D_MODEL ** -0.5),
        'g_mem_q': gain((DEPTH, MEM_HD)),
        'g_mem_k': gain((DEPTH, MEM_HD)),
        'w_up_a': nrm((DEPTH, D_RNN, D_MODEL), D_RNN ** -0.5),
        'w_up_b': nrm((DEPTH, NSA_HEADS * NSA_HD, D_MODEL), (NSA_HEADS * NSA_HD) ** -0.5),
        'w_up_m': nrm((DEPTH, MEM_HEADS * MEM_HD, D_MODEL), (MEM_HEADS * MEM_HD) ** -0.5),
        'w_o': nrm((DEPTH, D_MODEL, D_MODEL), D_MODEL ** -0.5),
        'norm_ffn': gain((DEPTH, D_MODEL)),
        'w_ffn_gate': nrm((DEPTH, D_MODEL, D_FF), D_MODEL ** -0.5),
        'w_ffn_up': nrm((DEPTH, D_MODEL, D_FF), D_MODEL ** -0.5),
        'w_ffn_down': nrm((DEPTH, D_FF, D_MODEL), D_FF ** -0.5),
    }

def reference(x_prompt, x_sample, mem_prompt, cache_cmp_kv, cache_sel_kv, page_table, cache_win_kv,
              cache_mem_kv, state_lru_h, state_conv, rel_bias, norm_mix, w_in, conv_w, conv_b, w_lru_a,
              b_lru_a, w_lru_i, b_lru_i, lru_lambda, g_nsa_q, g_nsa_k, pe_cmp_k, w_cmp_k1, w_cmp_k2,
              pe_cmp_v, w_cmp_v1, w_cmp_v2, norm_mem, w_mem_kv, g_mem_q, g_mem_k, w_up_a, w_up_b, w_up_m,
              w_o, norm_ffn, w_ffn_gate, w_ffn_up, w_ffn_down):
    yp, ys = x_prompt, x_sample
    cmp_p, cmp_s, sel_p, sel_s, win_p, win_s, mem_p, h_p, h_s, cv_p, cv_s = [], [], [], [], [], [], [], [], [], [], []
    for l in range(DEPTH):
        p = dict(norm_mix=norm_mix[l], w_in=w_in[l], conv_w=conv_w[l], conv_b=conv_b[l], w_lru_a=w_lru_a[l],
                 b_lru_a=b_lru_a[l], w_lru_i=w_lru_i[l], b_lru_i=b_lru_i[l], lru_lambda=lru_lambda[l],
                 g_nsa_q=g_nsa_q[l], g_nsa_k=g_nsa_k[l], pe_cmp_k=pe_cmp_k[l], w_cmp_k1=w_cmp_k1[l],
                 w_cmp_k2=w_cmp_k2[l], pe_cmp_v=pe_cmp_v[l], w_cmp_v1=w_cmp_v1[l], w_cmp_v2=w_cmp_v2[l],
                 norm_mem=norm_mem[l], w_mem_kv=w_mem_kv[l], g_mem_q=g_mem_q[l], g_mem_k=g_mem_k[l],
                 w_up_a=w_up_a[l], w_up_b=w_up_b[l], w_up_m=w_up_m[l], w_o=w_o[l], norm_ffn=norm_ffn[l],
                 w_ffn_gate=w_ffn_gate[l], w_ffn_up=w_ffn_up[l], w_ffn_down=w_ffn_down[l])
        yp, c1, s1, w1, m1, h1, v1 = prompt_layer(yp, mem_prompt, rel_bias, p)
        ys, c2, s2, w2, h2, v2 = sample_layer(ys, cache_cmp_kv[l], cache_sel_kv[l], page_table, cache_win_kv[l],
                                              cache_mem_kv[l], state_lru_h[l], state_conv[l], rel_bias, p)
        cmp_p.append(c1)
        cmp_s.append(c2)
        sel_p.append(s1)
        sel_s.append(s2)
        win_p.append(w1)
        win_s.append(w2)
        mem_p.append(m1)
        h_p.append(h1)
        h_s.append(h2)
        cv_p.append(v1)
        cv_s.append(v2)
    return (yp, ys, jnp.stack(cmp_p), jnp.stack(cmp_s), jnp.stack(sel_p), jnp.stack(sel_s),
            jnp.stack(win_p), jnp.stack(win_s), jnp.stack(mem_p), jnp.stack(h_p), jnp.stack(h_s),
            jnp.stack(cv_p), jnp.stack(cv_s))


_drawn_inputs = setup_inputs


def setup_inputs(seed=0):
    import zlib

    import numpy as np

    out = dict(_drawn_inputs(seed))
    spreads = {}
    factors = {'cache_sel_kv': 3.58,
     'norm_mix': 2.858,
     'b_lru_a': 33.015,
     'b_lru_i': 26.17,
     'g_nsa_q': 8.0,
     'g_nsa_k': 3.684,
     'pe_cmp_k': 4.142,
     'norm_mem': 2.729,
     'g_mem_q': 8.0,
     'g_mem_k': 3.922,
     'norm_ffn': 3.743}
    for name, (base, spread) in spreads.items():
        noise = np.random.default_rng([zlib.crc32(name.encode()), seed]).standard_normal(out[name].shape)
        drawn = base * np.exp(spread * noise) if base else spread * noise
        out[name] = jnp.asarray(drawn.astype(out[name].dtype))
    for name, factor in factors.items():
        out[name] = (out[name] * factor).astype(out[name].dtype)
    return out
```

```python
from contextlib import ExitStack
import math

import numpy as np
import concourse.bass as bass
from concourse import mybir

F32 = mybir.dt.float32
F32R = mybir.dt.float32r
I32 = mybir.dt.int32
ACT = mybir.ActivationFunctionType
ALU = mybir.AluOpType
AX = mybir.AxisListType.X

P = 128
D = 1024
KT = D // P
NP_ = 1024
NS = 8
T = NP_ + NS
NCH, CW = 3, T // 3
NMEM = 256
XC = T + NMEM
G, R, HD = 2, 4, 64
MH = 4
QT = NP_ // P
PAGES = 8
NCMP = 63
NCK = 64
WIN = 512
FFG = 11
EPS = 1e-6
NEGV = -1e30
RLEN, RMAX = 512, 360
CU = 120

U_CMPK, U_CMPV, U_SELV, U_WINV, U_SELK, U_WINK, U_Q, U_MQ, U_LX, U_LG, U_MG = 0, 1, 2, 3, 4, 5, 6, 10, 14, 22, 30
NU_IN = 54
NHN = 10
V_MIX, V_MEM, V_FFN, V_GMK, V_PEK, V_PEV, NV = 0, 8, 16, 24, 25, 41, 57
L_CW, L_CB, L_BA, L_BI, L_LAM, NL = 0, 4, 5, 6, 7, 8


def sb_of(nc, ctx, tag):
    return lambda name, shape, dt=F32: ctx.enter_context(nc.sbuf_tensor(f"{tag}_{name}", shape, dt))


def ps_of(nc, ctx, tag):
    return lambda name, shape: ctx.enter_context(nc.psum_tensor(f"{tag}_{name}", shape, F32))


PHASE_SEMS = {"last": [], "now": []}


def sem_of(nc, ctx, tag):
    PHASE_SEMS["last"], PHASE_SEMS["now"] = PHASE_SEMS["now"], []

    def sem(name):
        s = ctx.enter_context(nc.semaphore(f"{tag}_{name}"))
        PHASE_SEMS["now"].append(s)
        return s

    return sem


def clear_last(sp):
    for s in PHASE_SEMS["last"]:
        sp.sem_clear(s)


def normalise(nc, d, per, h_hi, h_lo):
    with ExitStack() as ctx:
        sb, ps, sem = sb_of(nc, ctx, "nrm"), ps_of(nc, ctx, "nrm"), sem_of(nc, ctx, "nrm")
        x = sb("x", [P, KT, XC])
        sq = sb("sq", [P, 2, XC])
        rstd = sb("rstd", [P, XC])
        nrm = sb("nrm", [P, 2, XC])
        ss = ps("ss", [P, 4, 512])
        w = XC // 4
        x_in, c_in, sq_done, ss_done = sem("x_in"), sem("c_in"), sem("sq_done"), sem("ss_done")
        sum_done, rt_done, rs_done, n_done, hi_done, lo_done = (sem("sum_done"), sem("rt_done"), sem("rs_done"), sem("n_done"),
                                                      sem("hi_done"), sem("lo_done"))
        eps_done = sem("eps_done")
        block = ctx.enter_context(nc.Block())

        @block.sync
        def _(sp):
            clear_last(sp)
            sp.dma_start(per["ones"][:], d["ones"]).then_inc(c_in, 16)
            sp.dma_start(per["vec"][:], d["vec"]).then_inc(c_in, 16)
            for k in range(KT):
                sp.dma_start(x[:, k, :], d["xT"][:, k, :]).then_inc(x_in, 16)
            sp.dma_start(per["ident"][:], d["ident"]).then_inc(c_in, 16)
            sp.wait_ge(c_in, 48)

        @block.scalar
        def _(act):
            act.wait_ge(x_in, 16 * KT)
            for k in range(KT):
                if k >= 2:
                    act.wait_ge(ss_done, k - 1)
                act.activation(sq[:, k % 2, :], x[:, k, :], ACT.Square).then_inc(sq_done, 1)
            act.wait_ge(ss_done, KT)
            act.wait_ge(eps_done, 1)
            act.activation(rstd[:].rearrange("p (c n) -> p c n", c=4), ss[:, :, 0:w], ACT.Sqrt,
                           bias=per["eps"][:, 0:1], scale=1.0 / D).then_inc(rt_done, 1)
            for k in range(KT):
                act.wait_ge(n_done, 2 * k + 2)
                act.activation(h_hi[:, k, :], nrm[:, k % 2, :], ACT.Copy).then_inc(hi_done, 1)

        @block.tensor
        def _(pe):
            pe.wait_ge(c_in, 32)
            for k in range(KT):
                pe.wait_ge(sq_done, k + 1)
                for c in range(4):
                    mm = pe.matmul(ss[:, c, 0:w], per["ones"][:], sq[:, k % 2, c * w:c * w + w],
                                   start=(k == 0), stop=(k == KT - 1))
                mm.then_inc(ss_done, 1)

        @block.vector
        def _(dve):
            dve.memset(per["eps"][:], EPS).then_inc(eps_done, 1)
            dve.wait_ge(rt_done, 1)
            dve.reciprocal(rstd[:], rstd[:]).then_inc(rs_done, 1)
            dve.wait_ge(rs_done, 1)
            dve.wait_ge(c_in, 32)
            dve.wait_ge(x_in, 16 * KT)
            for k in range(KT):
                if k >= 2:
                    dve.wait_ge(lo_done, k - 1)
                dve.scalar_tensor_tensor(nrm[:, k % 2, 0:T], x[:, k, 0:T], per["vec"][:, V_MIX + k:V_MIX + k + 1],
                                         rstd[:, 0:T], ALU.mult, ALU.mult).then_inc(n_done, 1)
                dve.scalar_tensor_tensor(nrm[:, k % 2, T:XC], x[:, k, T:XC], per["vec"][:, V_MEM + k:V_MEM + k + 1],
                                         rstd[:, T:XC], ALU.mult, ALU.mult).then_inc(n_done, 1)

        @block.gpsimd
        def _(pool):
            for k in range(KT):
                pool.wait_ge(hi_done, k + 1)
                pool.tensor_tensor(h_lo[:, k, :], nrm[:, k % 2, :], h_hi[:, k, :].bitcast(F32),
                                   ALU.subtract).then_inc(lo_done, 1)


def project(nc, tag, units, n_units, h_hi, h_lo, col, chunks, cw, out):
    cols = chunks * cw
    with ExitStack() as ctx:
        sb, ps, sem = sb_of(nc, ctx, tag), ps_of(nc, ctx, tag), sem_of(nc, ctx, tag)
        raw = sb("raw", [P, 2, KT, P])
        w_hi = sb("w_hi", [P, 2, KT, P], F32R)
        w_lo = sb("w_lo", [P, 2, KT, P], F32R)
        z = sb("z", [P, 2, cols])
        acc = [ps(f"acc{s}", [P, chunks, 512]) for s in range(2)]
        raw_in = [sem("raw_in0"), sem("raw_in1")]
        z_out = [sem("z_out0"), sem("z_out1")]
        hi_done, lo_done, mm_done, ev_done = sem("hi_done"), sem("lo_done"), sem("mm_done"), sem("ev_done")
        block = ctx.enter_context(nc.Block())
        pairs = n_units // 2

        @block.sync
        def _(sp):
            clear_last(sp)
            sp.sem_inc(z_out[0], 16)
            sp.sem_inc(z_out[1], 16)
            for s in range(2):
                sp.dma_start(raw[:, s], units[s]).then_inc(raw_in[s], 16)

            def store(s, row, n):
                sp.wait_ge(ev_done, n + 2)
                sp.dma_start(out[row], z[:, s]).then_inc(z_out[s], 16)

            with sp.Fori(0, pairs - 1) as i:
                for s in range(2):
                    nxt = sp.snap(i * 2 + (s + 2))
                    cur = sp.snap(i * 2 + s)
                    sp.wait_ge(lo_done, i * 2 + (s + 1))
                    sp.dma_start(raw[:, s], units[bass.ds(nxt, 1)].rearrange("a p k m -> p (a k) m")).then_inc(raw_in[s], 16)
                    sp.wait_ge(ev_done, i * 2 + (s + 3))
                    sp.dma_start(out[bass.ds(cur, 1)].rearrange("a p n -> p (a n)"), z[:, s]).then_inc(z_out[s], 16)
            for s in range(2):
                store(s, n_units - 2 + s, n_units - 1 + s)
            for s in range(2):
                sp.wait_ge(z_out[s], 16 * (pairs + 1))

        @block.scalar
        def _(act):
            with act.Fori(0, pairs) as i:
                for s in range(2):
                    act.wait_ge(raw_in[s], i * 16 + 16)
                    act.wait_ge(mm_done, i * 2 + (s + 1))
                    act.activation(w_hi[:, s], raw[:, s], ACT.Copy).then_inc(hi_done, 1)

        @block.gpsimd
        def _(pool):
            with pool.Fori(0, pairs) as i:
                for s in range(2):
                    pool.wait_ge(hi_done, i * 2 + (s + 1))
                    pool.tensor_tensor(w_lo[:, s], raw[:, s], w_hi[:, s].bitcast(F32), ALU.subtract).then_inc(lo_done, 1)

        @block.tensor
        def _(pe):
            pe.sem_inc(mm_done, 2)
            with pe.Fori(0, pairs) as i:
                for s in range(2):
                    pe.wait_ge(lo_done, i * 2 + (s + 1))
                    pe.wait_ge(ev_done, i * 2 + (s + 1))
                    for k in range(KT):
                        for n, (w, h) in enumerate(((w_hi, h_hi), (w_hi, h_lo), (w_lo, h_hi))):
                            for c in range(chunks):
                                mm = pe.matmul(acc[s][:, c, 0:cw], w[:, s, k, :],
                                               h[:, k, col + c * cw:col + (c + 1) * cw],
                                               start=(k + n == 0), stop=(k == KT - 1 and n == 2))
                    mm.then_inc(mm_done, 1)

        @block.vector
        def _(dve):
            dve.sem_inc(ev_done, 2)
            with dve.Fori(0, pairs) as i:
                for s in range(2):
                    dve.wait_ge(z_out[s], i * 16 + 16)
                    dve.wait_ge(mm_done, i * 2 + (s + 3))
                    dve.tensor_copy(z[:, s].rearrange("p (c n) -> p c n", c=chunks), acc[s][:, :, 0:cw]).then_inc(ev_done, 1)


def gates(nc, d, per, h_hi, h_lo):
    with ExitStack() as ctx:
        sb, ps, sem = sb_of(nc, ctx, "gat"), ps_of(nc, ctx, "gat"), sem_of(nc, ctx, "gat")
        raw = sb("raw", [P, KT, 24])
        hi = sb("hi", [P, KT, 24], F32R)
        lo = sb("lo", [P, KT, 24], F32R)
        gs = sb("gs", [NS, 24])
        acc = ps("acc", [P, QT + 1, 32])
        w_in, hi_done, lo_done, mm_done, sig_done, g_out = (sem("w_in"), sem("hi_done"), sem("lo_done"), sem("mm_done"),
                                                      sem("sig_done"), sem("g_out"))
        block = ctx.enter_context(nc.Block())

        @block.sync
        def _(sp):
            clear_last(sp)
            sp.dma_start(raw[:], d["w_ng"]).then_inc(w_in, 16)
            sp.wait_ge(sig_done, 2)
            sp.dma_start(d["gate_s"].rearrange("(b n) c -> b (n c)", b=NS), gs[:]).then_inc(g_out, 16)
            sp.wait_ge(g_out, 16)

        @block.vector
        def _(dve):
            dve.wait_ge(w_in, 16)
            dve.tensor_copy(hi[:], raw[:]).then_inc(hi_done, 1)
            dve.wait_ge(hi_done, 1)
            dve.tensor_tensor(lo[:], raw[:], hi[:].bitcast(F32), ALU.subtract).then_inc(lo_done, 1)

        @block.tensor
        def _(pe):
            pe.wait_ge(lo_done, 1)
            for t in range(QT + 1):
                m = P if t < QT else NS
                for k in range(KT):
                    for n, (h, w) in enumerate(((h_hi, hi), (h_lo, hi), (h_hi, lo))):
                        mm = pe.matmul(acc[0:m, t, 0:24], h[:, k, t * P:t * P + m], w[:, k, :],
                                       start=(k + n == 0), stop=(k == KT - 1 and n == 2))
            mm.then_inc(mm_done, 1)

        @block.scalar
        def _(act):
            act.wait_ge(mm_done, 1)
            act.activation(per["gate"][:], acc[:, 0:QT, 0:24], ACT.Sigmoid).then_inc(sig_done, 1)
            act.activation(gs[:], acc[0:NS, QT, 0:24], ACT.Sigmoid).then_inc(sig_done, 1)


def head_norm(nc, tag, d, src, row0, n, cols, chunks, mats, gains, dst):
    cw = cols // chunks
    with ExitStack() as ctx:
        sb, ps, sem = sb_of(nc, ctx, tag), ps_of(nc, ctx, tag), sem_of(nc, ctx, tag)
        z = sb("z", [P, 2, cols])
        m = sb("m", [P, 2, P + 1])
        g = sb("g", [P, 2, 1])
        sq = sb("sq", [P, 2, cols])
        o = sb("o", [P, 2, cols])
        ms = [ps(f"ms{s}", [P, chunks, 512]) for s in range(2)]
        t_in = [sem("t_in0"), sem("t_in1")]
        t_out = [sem("t_out0"), sem("t_out1")]
        sq_done, mm_done, rt_done, rc_done, n_done = sem("sq_done"), sem("mm_done"), sem("rt_done"), sem("rc_done"), sem("n_done")
        block = ctx.enter_context(nc.Block())

        @block.sync
        def _(sp):
            clear_last(sp)
            sp.sem_inc(t_out[0], 16)
            sp.sem_inc(t_out[1], 16)
            sp.sem_inc(n_done, 2)
            with sp.Fori(0, n // 2) as i:
                for s in range(2):
                    j = sp.snap(i * 2 + s)
                    jr = sp.snap(i * 2 + (s + row0))
                    sp.wait_ge(n_done, i * 2 + (s + 1))
                    sp.dma_start(z[:, s], src[bass.ds(jr, 1)].rearrange("a p n -> p (a n)")).then_inc(t_in[s], 16)
                    sp.dma_start(m[:, s], mats[bass.ds(j, 1)].rearrange("a p n -> p (a n)")).then_inc(t_in[s], 16)
                    sp.dma_start(g[:, s], gains[bass.ds(j, 1)].rearrange("a p n -> p (a n)")).then_inc(t_in[s], 16)

        @block.scalar
        def _(act):
            with act.Fori(0, n // 2) as i:
                for s in range(2):
                    j = act.snap(i * 2 + s)
                    act.wait_ge(t_in[s], i * 48 + 48)
                    act.activation(sq[:, s], z[:, s], ACT.Square).then_inc(sq_done, 1)
                    act.wait_ge(mm_done, i * 2 + (s + 1))
                    act.activation(sq[:, s].rearrange("p (c n) -> p c n", c=chunks), ms[s][:, :, 0:cw], ACT.Sqrt,
                                   bias=m[:, s, P:P + 1]).then_inc(rt_done, 1)
                    act.wait_ge(n_done, i * 2 + (s + 3))
                    act.dma_start(dst[bass.ds(j, 1)].rearrange("a p n -> p (a n)"), o[:, s]).then_inc(t_out[s], 16)
            act.wait_ge(t_out[0], 16 * (n // 2 + 1))
            act.wait_ge(t_out[1], 16 * (n // 2 + 1))

        @block.tensor
        def _(pe):
            with pe.Fori(0, n // 2) as i:
                for s in range(2):
                    pe.wait_ge(sq_done, i * 2 + (s + 1))
                    for c in range(chunks):
                        mm = pe.matmul(ms[s][:, c, 0:cw], m[:, s, 0:P], sq[:, s, c * cw:(c + 1) * cw], start=True, stop=True)
                    mm.then_inc(mm_done, 1)

        @block.vector
        def _(dve):
            with dve.Fori(0, n // 2) as i:
                for s in range(2):
                    dve.wait_ge(rt_done, i * 2 + (s + 1))
                    dve.reciprocal(sq[:, s], sq[:, s]).then_inc(rc_done, 1)
                    dve.wait_ge(t_out[s], i * 16 + 16)
                    dve.wait_ge(rc_done, i * 2 + (s + 1))
                    dve.scalar_tensor_tensor(o[:, s], z[:, s], g[:, s], sq[:, s], ALU.mult, ALU.mult).then_inc(n_done, 1)


def to_tokens(nc, tag, per, src, row0, n, cols, dst):
    nt = cols // P
    with ExitStack() as ctx:
        sb, ps, sem = sb_of(nc, ctx, tag), ps_of(nc, ctx, tag), sem_of(nc, ctx, tag)
        z = sb("z", [P, 2, cols])
        o = sb("o", [P, 2, cols])
        tp = [ps(f"tp{s}", [P, nt, P]) for s in range(2)]
        t_in = [sem("t_in0"), sem("t_in1")]
        t_out = [sem("t_out0"), sem("t_out1")]
        tp_done, ev_done = sem("tp_done"), sem("ev_done")
        block = ctx.enter_context(nc.Block())

        def store(sp, j):
            sp.wait_ge(ev_done, j + 1)
            sp.dma_start(dst[j].rearrange("t p n -> p t n"), o[:, j % 2].rearrange("p (t n) -> p t n", n=P)).then_inc(t_out[j % 2], 16)

        @block.sync
        def _(sp):
            clear_last(sp)
            for j in range(n):
                s = j % 2
                if j >= 2:
                    sp.wait_ge(tp_done, j - 1)
                sp.dma_start(z[:, s], src[row0 + j][:, 0:cols]).then_inc(t_in[s], 16)
                if j >= 1:
                    store(sp, j - 1)
            store(sp, n - 1)
            for s in range(2):
                sp.wait_ge(t_out[s], 16 * ((n - s + 1) // 2))

        @block.tensor
        def _(pe):
            for j in range(n):
                s = j % 2
                pe.wait_ge(t_in[s], 16 * (j // 2 + 1))
                if j >= 2:
                    pe.wait_ge(ev_done, j - 1)
                for t in range(nt):
                    mm = pe.transpose(tp[s][:, t, :], z[:, s, t * P:(t + 1) * P], per["ident"][:])
                mm.then_inc(tp_done, 1)

        @block.vector
        def _(dve):
            for j in range(n):
                s = j % 2
                dve.wait_ge(tp_done, j + 1)
                if j >= 2:
                    dve.wait_ge(t_out[s], 16 * (j // 2))
                dve.tensor_copy(o[:, s].rearrange("p (t n) -> p t n", n=P), tp[s][:]).then_inc(ev_done, 1)


def recurrence(nc, d, per):
    CWD = 4
    with ExitStack() as ctx:
        sb, ps, sem = sb_of(nc, ctx, "lru"), ps_of(nc, ctx, "lru"), sem_of(nc, ctx, "lru")
        xp = sb("xp", [P, 2, CWD - 1 + T])
        st = sb("st", [P, 2, 4 * NS])
        par = sb("par", [P, 2, NL])
        wa = sb("wa", [P, 2, 256])
        wi = sb("wi", [P, 2, 256])
        gate = sb("gate", [P, 2, T])
        xc = sb("xc", [P, 2, T])
        r = sb("r", [P, 2, T])
        ig = sb("ig", [P, 2, T])
        a = sb("a", [P, 2, T])
        th = sb("th", [P, 2, T])
        h = sb("h", [P, 2, T])
        lam = sb("lam", [P, 8, 2])
        ps_r = ps("ps_r", [P, NCH, 512])
        ps_i = ps("ps_i", [P, NCH, 512])
        b_in, b_out, z_done, ch, xc_done, mm_done, sig_done = (sem("b_in"), sem("b_out"), sem("z_done"), sem("ch"), sem("xc_done"),
                                                         sem("mm_done"), sem("sig_done"))
        lam_done, act_done, sq_in, rt_done, o_done, ex_done = (sem("lam_done"), sem("act_done"), sem("sq_in"), sem("rt_done"),
                                                     sem("o_done"), sem("ex_done"))
        block = ctx.enter_context(nc.Block())
        NBLK = 4
        LOADS = 9

        @block.sync
        def _(sp):
            clear_last(sp)
            sp.sem_inc(b_out, 80)
            with sp.Fori(0, NBLK) as n:
                u = sp.snap(n * 2 + U_LX)
                ug = sp.snap(n * 2 + U_LG)
                t2 = sp.snap(n * 2)
                nn = sp.snap(n * 1)
                sp.wait_ge(b_out, n * 80 + 80)
                sp.dma_start(xp[:, :, CWD - 1:], d["z"][bass.ds(u, 2)].rearrange("a p n -> p a n")).then_inc(b_in, 16)
                sp.dma_start(gate[:], d["z"][bass.ds(ug, 2)].rearrange("a p n -> p a n")).then_inc(b_in, 16)
                sp.dma_start(st[:], d["st"][:, bass.ds(t2, 2), :]).then_inc(b_in, 16)
                sp.dma_start(par[:], d["par"][:, bass.ds(t2, 2), :]).then_inc(b_in, 16)
                sp.dma_start(wa[:], d["w_a"][bass.ds(nn, 1)].rearrange("a p k n -> p (a k) n")).then_inc(b_in, 16)
                sp.dma_start(wi[:], d["w_i"][bass.ds(nn, 1)].rearrange("a p k n -> p (a k) n")).then_inc(b_in, 16)
                sp.wait_ge(o_done, n * 2 + 2)
                sp.dma_start(d["o_lru"][bass.ds(t2, 2)].rearrange("a p n -> p a n"), xc[:]).then_inc(b_out, 16)
                sp.dma_start(d["hT"][bass.ds(t2, 2)].rearrange("a p n -> p a n"), h[:, :, NP_ - 1:T]).then_inc(b_out, 16)
                sp.dma_start(d["cvT"][bass.ds(t2, 2)].rearrange("a p n -> p a n"), xp[:, :, NP_:NP_ + 3]).then_inc(b_out, 16)
                sp.dma_start(d["cvsT"][bass.ds(t2, 2), :, 0:2 * NS].rearrange("a p n -> p a n"), st[:, :, NS:3 * NS]).then_inc(b_out, 16)
                sp.dma_start(d["cvsT"][bass.ds(t2, 2), :, 2 * NS:].rearrange("a p n -> p a n"),
                             xp[:, :, CWD - 1 + NP_:]).then_inc(b_out, 16)
            sp.wait_ge(b_out, 80 * (NBLK + 1))

        @block.vector
        def _(dve):
            per_block = [0]

            def chain(ins, n):
                per_block[0] += 1
                ins.then_inc(ch, 1)
                dve.wait_ge(ch, n * CH + per_block[0])

            dve.memset(xp[:, :, 0:CWD - 1], 0.0).then_inc(z_done, 1)
            dve.wait_ge(z_done, 1)
            CH = 52
            with dve.Fori(0, NBLK) as n:
                dve.wait_ge(b_in, n * 96 + 96)
                L = par[:, :, L_LAM]
                chain(dve.tensor_scalar(lam[:, 0], L, -1.0, None, ALU.mult), n)
                chain(dve.tensor_tensor(lam[:, 1], L, lam[:, 0], ALU.max), n)
                dve.tensor_scalar(lam[:, 2], lam[:, 0], 0.0, None, ALU.max).then_inc(lam_done, 1)
                dve.wait_ge(ex_done, n + 1)
                chain(dve.tensor_scalar(lam[:, 4], lam[:, 3], 2.0, None, ALU.add), n)
                chain(dve.reciprocal(lam[:, 4], lam[:, 4]), n)
                chain(dve.tensor_tensor(lam[:, 4], lam[:, 3], lam[:, 4], ALU.mult), n)
                chain(dve.tensor_tensor(lam[:, 5], lam[:, 4], lam[:, 4], ALU.mult), n)
                chain(dve.memset(lam[:, 6], 1.0 / 19), n)
                for q in range(17, 0, -2):
                    chain(dve.tensor_tensor(lam[:, 6], lam[:, 6], lam[:, 5], ALU.mult), n)
                    chain(dve.tensor_scalar(lam[:, 6], lam[:, 6], 1.0 / q, None, ALU.add), n)
                chain(dve.tensor_tensor(lam[:, 6], lam[:, 6], lam[:, 4], ALU.mult), n)
                chain(dve.scalar_tensor_tensor(lam[:, 6], lam[:, 6], 2.0, lam[:, 2], ALU.mult, ALU.add), n)
                chain(dve.tensor_scalar(lam[:, 6], lam[:, 6], -8.0, None, ALU.mult), n)
                dve.tensor_scalar(lam[:, 7], lam[:, 6], -1.0, None, ALU.mult).then_inc(lam_done, 1)
                for t in range(2):
                    w = [par[:, t, L_CW + j:L_CW + j + 1] for j in range(CWD)]
                    chain(dve.tensor_scalar(xc[:, t, 0:NP_], xp[:, t, 0:NP_], w[0], par[:, t, L_CB:L_CB + 1],
                                            ALU.mult, ALU.add), n)
                    chain(dve.tensor_scalar(xc[:, t, NP_:T], st[:, t, 0:NS], w[0], par[:, t, L_CB:L_CB + 1],
                                            ALU.mult, ALU.add), n)
                    for j in range(1, CWD):
                        x_s = st[:, t, j * NS:(j + 1) * NS] if j < CWD - 1 else xp[:, t, CWD - 1 + NP_:]
                        p = dve.scalar_tensor_tensor(xc[:, t, 0:NP_], xp[:, t, j:j + NP_], w[j], xc[:, t, 0:NP_],
                                                     ALU.mult, ALU.add)
                        if j < CWD - 1:
                            chain(p, n)
                        else:
                            p.then_inc(xc_done, 1)
                        p = dve.scalar_tensor_tensor(xc[:, t, NP_:T], x_s, w[j], xc[:, t, NP_:T], ALU.mult, ALU.add)
                        if j < CWD - 1:
                            chain(p, n)
                        else:
                            p.then_inc(xc_done, 1)
                for t in range(2):
                    dve.wait_ge(xc_done, n * 4 + (2 * t + 2))
                    dve.wait_ge(act_done, n * 2 + (t + 1))
                    chain(dve.tensor_tensor(r[:, t], a[:, t], a[:, t], ALU.mult), n)
                    dve.scalar_tensor_tensor(th[:, t], r[:, t], 1.0, th[:, t], ALU.add, ALU.mult).then_inc(sq_in, 1)
                    chain(dve.tensor_tensor(ig[:, t], ig[:, t], xc[:, t], ALU.mult), n)
                    dve.wait_ge(rt_done, n * 2 + (t + 1))
                    chain(dve.tensor_tensor(ig[:, t], ig[:, t], th[:, t], ALU.mult), n)
                    chain(dve.tensor_tensor(h[:, t, NP_:T], a[:, t, NP_:T], st[:, t, 3 * NS:4 * NS], ALU.mult), n)
                    chain(dve.tensor_tensor(h[:, t, NP_:T], h[:, t, NP_:T], ig[:, t, NP_:T], ALU.add), n)
                    chain(dve.tensor_tensor_scan(h[:, t, 0:NP_], a[:, t, 0:NP_], ig[:, t, 0:NP_], 0.0, ALU.mult, ALU.add), n)
                    dve.tensor_tensor(xc[:, t], h[:, t], gate[:, t], ALU.mult).then_inc(o_done, 1)
                assert per_block[0] == CH, per_block[0]

        @block.scalar
        def _(act):
            with act.Fori(0, NBLK) as n:
                act.wait_ge(lam_done, n * 2 + 1)
                act.activation(lam[:, 3], lam[:, 1], ACT.Exp, scale=-1.0).then_inc(ex_done, 1)
                act.activation(gate[:], gate[:], ACT.Gelu_apprx_tanh)
                for t in range(2):
                    act.wait_ge(mm_done, n * 2 + (t + 1))
                    act.activation(r[:, t].rearrange("p (c n) -> p c n", c=NCH), ps_r[:, :, 0:CW], ACT.Sigmoid,
                                   bias=par[:, t, L_BA:L_BA + 1]).then_inc(sig_done, 1)
                    act.activation(ig[:, t].rearrange("p (c n) -> p c n", c=NCH), ps_i[:, :, 0:CW], ACT.Sigmoid,
                                   bias=par[:, t, L_BI:L_BI + 1]).then_inc(sig_done, 1)
                act.wait_ge(lam_done, n * 2 + 2)
                act.wait_ge(sig_done, n * 4 + 4)
                for t in range(2):
                    act.activation(th[:, t], r[:, t], ACT.Tanh, scale=lam[:, 7, t:t + 1])
                    act.activation(a[:, t], r[:, t], ACT.Exp, scale=lam[:, 6, t:t + 1]).then_inc(act_done, 1)
                for t in range(2):
                    act.wait_ge(sq_in, n * 2 + (t + 1))
                    act.activation(th[:, t], th[:, t], ACT.Sqrt).then_inc(rt_done, 1)

        @block.tensor
        def _(pe):
            with pe.Fori(0, NBLK) as n:
                pe.wait_ge(xc_done, n * 4 + 4)
                for t in range(2):
                    if t == 1:
                        pe.wait_ge(sig_done, n * 4 + 2)
                    for w, o in ((wa, ps_r), (wi, ps_i)):
                        for k in range(2):
                            for c in range(NCH):
                                mm = pe.matmul(o[:, c, 0:CW], w[:, k, t * P:(t + 1) * P], xc[:, k, c * CW:(c + 1) * CW],
                                               start=(k == 0), stop=(k == 1))
                    mm.then_inc(mm_done, 1)


def distance_bias(nc, d):
    with ExitStack() as ctx:
        sb, ps, sem = sb_of(nc, ctx, "dst"), ps_of(nc, ctx, "dst"), sem_of(nc, ctx, "dst")
        rel = sb("rel", [33, 8, P])
        hot = sb("hot", [33, RLEN])
        f = sb("f", [P, 8, RLEN])
        acc = ps("acc", [P, 8, RLEN])
        r_in, mm_done, ev_done, f_out = sem("r_in"), sem("mm_done"), sem("ev_done"), sem("f_out")
        block = ctx.enter_context(nc.Block())

        @block.sync
        def _(sp):
            clear_last(sp)
            sp.dma_start(rel[:], d["rel"]).then_inc(r_in, 16)
            sp.dma_start(hot[:], d["hot"]).then_inc(r_in, 16)
            sp.wait_ge(ev_done, 8)
            sp.dma_start(d["dist"].rearrange("p h n -> p (h n)"), f[:].rearrange("p h n -> p (h n)")).then_inc(f_out, 16)
            sp.wait_ge(f_out, 16)

        @block.tensor
        def _(pe):
            pe.wait_ge(r_in, 32)
            for h in range(8):
                pe.matmul(acc[:, h, :], rel[:, h, :], hot[:], start=True, stop=True).then_inc(mm_done, 1)

        @block.vector
        def _(dve):
            for h in range(8):
                dve.wait_ge(mm_done, h + 1)
                dve.tensor_copy(f[:, h, :], acc[:, h, :]).then_inc(ev_done, 1)


def compress(nc, d, per):
    SEQ = NS + 1
    with ExitStack() as ctx:
        sb, ps, sem = sb_of(nc, ctx, "cmp"), ps_of(nc, ctx, "cmp"), sem_of(nc, ctx, "cmp")
        pt = sb("pt", [1, NS * PAGES], I32)
        pool_x = sb("pool_x", [P, NS * PAGES, 256])
        zc = sb("zc", [P, 2, NP_])
        zr = sb("zr", [P, 2, 2, 8 * NCK])
        cp = sb("cp", [P, 2, 2, 8, NCK])
        w1 = sb("w1", [P, 2, 16, P])
        w2 = sb("w2", [P, 2, HD])
        pos = sb("pos", [P, 2])
        lo = sb("lo", [P, 2, SEQ, NCK])
        hd = sb("hd", [P, 2, SEQ, NCK])
        kc = sb("kc", [P, SEQ * NCK])
        sq = sb("sq", [P, SEQ * NCK])
        vc = sb("vc", [NCK, SEQ, P])
        nm = sb("nm", [P, P + 2])
        ps_lo = [ps(f"lo{s}", [P, NS, NCK]) for s in range(2)]
        ps_hi = [ps(f"hi{s}", [P, NS, NCK]) for s in range(2)]
        ps_pr = [ps(f"pr{s}", [P, 8, NCK]) for s in range(2)]
        ps_o = ps("o", [P, NS * NCK])
        ps_p = ps("p", [P, 8, NCK])
        pt_in, pg_in, zc_in, zr_done, cp_in, w_in, pos_mm, pos_done = (sem("pt_in"), sem("pg_in"), sem("zc_in"), sem("zr_done"),
                                                              sem("cp_in"), sem("w_in"), sem("pos_mm"), sem("pos_done"))
        mm_done, lo_ev, sum_done, act_done, o_mm, o_ev, z_done, c_out = (sem("mm_done"), sem("lo_ev"), sem("sum_done"),
                                                                 sem("act_done"), sem("o_mm"), sem("o_ev"), sem("z_done"),
                                                                 sem("c_out"))
        sq_done, ms_mm, rt_done, rc_done, kc_done = sem("sq_done"), sem("ms_mm"), sem("rt_done"), sem("rc_done"), sem("kc_done")
        block = ctx.enter_context(nc.Block())
        COMBOS = [(kv, g) for kv in range(2) for g in range(2)]

        @block.sync
        def _(sp):
            clear_last(sp)
            sp.dma_start(pt[:], d["page_table"]).then_inc(pt_in, 16)
            sp.dma_start(zc[:, 0, :], d["z"][U_CMPK][:, 0:NP_]).then_inc(zc_in, 16)
            sp.dma_start(zc[:, 1, :], d["z"][U_CMPV][:, 0:NP_]).then_inc(zc_in, 16)
            for kv in range(2):
                sp.dma_start(w1[:, kv], d["w_c1"][kv]).then_inc(w_in, 16)
                sp.dma_start(w2[:, kv], d["w_c2"][kv]).then_inc(w_in, 16)
            sp.dma_start(nm[:], d["nm_kc"]).then_inc(w_in, 16)
            sp.wait_ge(pt_in, 16)
            with sp.Fori(0, NS * PAGES) as i:
                page = sp.value_load(pt[0:1, bass.ds(i, 1)], min_val=0, max_val=d["cmp_pool"].shape[0] - 1)
                sp.dma_start(pool_x[:, bass.ds(i, 1), :].rearrange("p a n -> p (a n)"),
                             d["cmp_pool"][bass.ds(page, 1)].rearrange("a p n -> p (a n)")).then_inc(pg_in, 16)
            sp.wait_ge(zr_done, 2)
            for g in range(2):
                for s in range(2):
                    sp.dma_start(cp[s * HD:(s + 1) * HD, :, g].rearrange("p k a c -> p k (a c)"),
                                 zr[g * HD:(g + 1) * HD, :, s]).then_inc(cp_in, 16)
            sp.wait_ge(kc_done, 1)
            sp.dma_start(d["kcT"], kc[:]).then_inc(c_out, 16)
            sp.wait_ge(o_ev, 6)
            sp.dma_start(d["vc"], vc[:]).then_inc(c_out, 16)
            sp.wait_ge(c_out, 32)

        @block.vector
        def _(dve):
            dve.memset(hd[:], 0.0).then_inc(z_done, 1)
            dve.wait_ge(zc_in, 32)
            for kv in range(2):
                dve.tensor_copy(zr[:, kv].rearrange("p s (a c) -> p s a c", a=8),
                                zc[:, kv].rearrange("p (c a s) -> p s a c", a=8, s=2)).then_inc(zr_done, 1)
            dve.wait_ge(pos_mm, 1)
            dve.tensor_copy(pos[:], ps_p[:, 0, 0:2]).then_inc(pos_done, 1)
            dve.wait_ge(z_done, 1)
            for n, (kv, g) in enumerate(COMBOS):
                s = n % 2
                dve.wait_ge(lo_ev, 2 * n + 2)
                dve.tensor_tensor(hd[:, s, 0:NS, 0:NCMP], lo[:, s, 0:NS, 0:NCMP], ps_hi[s][:, :, 1:NCK], ALU.add).then_inc(sum_done, 1)
                dve.tensor_tensor(hd[:, s, NS, 0:NCMP], lo[:, s, NS, 0:NCMP], ps_pr[s][:, 1, 1:NCK], ALU.add).then_inc(sum_done, 1)
                if kv == 0:
                    if g == 1:
                        dve.wait_ge(o_mm, 2)
                        dve.tensor_copy(kc[:, 0:NS * NCK], ps_o[:]).then_inc(o_ev, 1)
                        dve.tensor_copy(kc[:, NS * NCK:], ps_p[:, 0, :]).then_inc(o_ev, 1)
                        dve.wait_ge(rt_done, 1)
                        dve.reciprocal(sq[:], sq[:]).then_inc(rc_done, 1)
                        dve.wait_ge(rc_done, 1)
                        dve.scalar_tensor_tensor(kc[:], kc[:], nm[:, P + 1:P + 2], sq[:], ALU.mult, ALU.mult).then_inc(kc_done, 1)
                else:
                    dve.wait_ge(o_mm, n + 1)
                    dve.tensor_copy(vc[:, 0:NS, g * HD:(g + 1) * HD], ps_o[0:NCK, :].rearrange("p (b n) -> p b n", b=NS)).then_inc(o_ev, 1)
                    dve.tensor_copy(vc[:, NS, g * HD:(g + 1) * HD], ps_p[0:NCK, 0, :]).then_inc(o_ev, 1)
                    if n == 3:
                        dve.wait_ge(o_ev, 6)

        @block.scalar
        def _(act):
            act.wait_ge(pos_done, 1)
            for n, (kv, g) in enumerate(COMBOS):
                s = n % 2
                act.wait_ge(mm_done, n + 1)
                if n >= 2:
                    act.wait_ge(sum_done, 2 * (n - 1))
                act.activation(lo[:, s, 0:NS], ps_lo[s][:], ACT.Identity, bias=pos[:, kv:kv + 1]).then_inc(lo_ev, 1)
                act.activation(lo[:, s, NS], ps_pr[s][:, 0], ACT.Identity, bias=pos[:, kv:kv + 1]).then_inc(lo_ev, 1)
                act.wait_ge(sum_done, 2 * n + 2)
                act.activation(hd[:, s, :, 0:NCMP], hd[:, s, :, 0:NCMP], ACT.Gelu_apprx_tanh).then_inc(act_done, 1)
                if n == 1:
                    act.wait_ge(o_ev, 2)
                    act.activation(sq[:], kc[:], ACT.Square).then_inc(sq_done, 1)
                    act.wait_ge(ms_mm, 1)
                    act.activation(sq[:, 0:NS * NCK], ps_o[:], ACT.Sqrt, bias=nm[:, P:P + 1])
                    act.activation(sq[:, NS * NCK:], ps_p[:, 0, :], ACT.Sqrt, bias=nm[:, P:P + 1]).then_inc(rt_done, 1)

        @block.tensor
        def _(pe):
            pe.wait_ge(w_in, 80)
            for kv, v0 in enumerate((V_PEK, V_PEV)):
                for i in range(16):
                    mm = pe.matmul(ps_p[:, 0, kv:kv + 1], w1[:, kv, i, :], per["vec"][:, v0 + i:v0 + i + 1],
                                   start=(i == 0), stop=(i == 15))
            mm.then_inc(pos_mm, 1)
            pe.wait_ge(pg_in, 16 * NS * PAGES)
            pe.wait_ge(cp_in, 64)

            def hidden(n):
                kv, g = COMBOS[n]
                s = n % 2
                if n >= 2:
                    pe.wait_ge(sum_done, 2 * (n - 1))
                for half, o in ((0, ps_lo[s]), (1, ps_hi[s])):
                    for a in range(8):
                        c0 = ((kv * 2 + g) * 8 + a) * 8
                        pe.matmul(o[:].rearrange("p b c -> p (b c)").rearrange("p (i c) -> p i c", c=8),
                                  w1[:, kv, half * 8 + a, :], pool_x[:, :, c0:c0 + 8], start=(a == 0), stop=(a == 7))
                for half in range(2):
                    for a in range(8):
                        mm = pe.matmul(ps_pr[s][:, half, :], w1[:, kv, half * 8 + a, :], cp[:, kv, g, a, :],
                                       start=(a == 0), stop=(a == 7))
                mm.then_inc(mm_done, 1)

            def output(n):
                kv, g = COMBOS[n]
                s = n % 2
                pe.wait_ge(act_done, n + 1)
                if kv == 0:
                    pe.wait_ge(pos_done, 1)
                    pe.matmul(ps_o[g * HD:(g + 1) * HD, :], w2[:, 0, :], hd[:, s, 0:NS].rearrange("p b c -> p (b c)"),
                              start=True, stop=True)
                    mm = pe.matmul(ps_p[g * HD:(g + 1) * HD, 0, :], w2[:, 0, :], hd[:, s, NS], start=True, stop=True)
                else:
                    if n == 2:
                        pe.wait_ge(rt_done, 1)
                    else:
                        pe.wait_ge(o_ev, 4)
                    for b in range(NS):
                        pe.matmul(ps_o[0:NCK, b * HD:(b + 1) * HD], hd[:, s, b], w2[:, 1, :], start=True, stop=True)
                    mm = pe.matmul(ps_p[0:NCK, 0, :], hd[:, s, NS], w2[:, 1, :], start=True, stop=True)
                mm.then_inc(o_mm, 1)

            hidden(0)
            hidden(1)
            output(0)
            output(1)
            hidden(2)
            pe.wait_ge(sq_done, 1)
            pe.wait_ge(o_ev, 2)
            pe.matmul(ps_o[:], nm[:, 0:P], sq[:, 0:NS * NCK], start=True, stop=True)
            pe.matmul(ps_p[:, 0, :], nm[:, 0:P], sq[:, NS * NCK:], start=True, stop=True).then_inc(ms_mm, 1)
            hidden(3)
            output(2)
            output(3)


def prompt_attention(nc, d, per, h_hi, h_lo):
    with ExitStack() as ctx:
        sb, ps, sem = sb_of(nc, ctx, "att"), ps_of(nc, ctx, "att"), sem_of(nc, ctx, "att")
        k_sel = sb("k_sel", [P, NP_])
        k_win = sb("k_win", [P, NP_])
        k_cmp = sb("k_cmp", [P, NCK])
        v_sel = sb("v_sel", [P, QT, P])
        v_win = sb("v_win", [P, QT, P])
        v_cmp = sb("v_cmp", [NCK, P])
        near = sb("near", [P, G, R, 2 * P])
        wmask = sb("wmask", [P, P])
        cstrip = sb("cstrip", [P, G, R, CU])
        cmask = sb("cmask", [P, CU])
        q = sb("q", [P, 2, P])
        pr = sb("pr", [P, 2, NP_])
        ptr = sb("ptr", [P, 2, 4 * P])
        gsl = sb("gsl", [P, 2, G, 3])
        nmx = sb("nmx", [P, 2])
        rs = sb("rs", [P, 2])
        cf = sb("cf", [P, 4])
        oacc = sb("oacc", [P, 2, P])
        oT = sb("oT", [P, 2, P])
        S = [ps(f"S{s}", [P, NP_]) for s in range(2)]
        tp = [ps(f"tp{s}", [P, 512]) for s in range(2)]
        O = ps("O", [P, 512])
        facc = ps("facc", [P, 512])
        raw = sb("raw", [P, KT, P])
        w_hi = sb("w_hi", [P, KT, P], F32R)
        w_lo = sb("w_lo", [P, KT, P], F32R)
        zf = sb("zf", [P, T])
        c_in, m_done = sem("c_in"), sem("m_done")
        f_in, f_hi, f_lo, f_mm, f_ev, f_out = (sem(x) for x in ("f_in", "f_hi", "f_lo", "f_mm", "f_ev", "f_out"))
        q_in = [sem("q_in0"), sem("q_in1")]
        o_out = [sem("o_out0"), sem("o_out1")]
        s_mm, s_exp, s_max, s_pm, s_tp, s_te, s_pvg, s_acc, s_ch = (
            sem(x) for x in ("s_mm", "s_exp", "s_max", "s_pm", "s_tp", "s_te", "s_pvg", "s_acc", "s_ch"))
        block = ctx.enter_context(nc.Block())
        HALF = [(g, br) for g in range(G) for br in ("sel", "win", "cmp")]
        NH = len(HALF)
        NJ = 2 * NH

        def tiles(qt, br):
            return {"sel": (0, qt + 1), "win": (max(0, qt - 4), min(qt + 1, 5)), "cmp": (0, 1)}[br]

        def groups(qt, j):
            return -(-tiles(qt, HALF[j % NH][1])[1] // 4)

        def before(qt, j):
            return sum(groups(qt, x) for x in range(j))

        def vbase(qt):
            return sum(2 * before(x, NJ) for x in range(qt))

        def tbase(qt):
            return vbase(qt) + 4 * qt

        def turn_at(qt, s):
            return before(qt, 7) if s == 0 else before(qt, NJ) + 1

        def tgroup(qt, j, a):
            return before(qt, j) + a + (1 if j > 6 else 0)

        @block.sync
        def _(sp):
            clear_last(sp)
            sp.dma_start(raw[:], d["w_in"][U_LX]).then_inc(f_in, 16)
            sp.sem_inc(f_out, 16)
            sp.dma_start(k_sel[:], d["zn"][0][:, 0:NP_]).then_inc(c_in, 16)
            sp.dma_start(k_win[:], d["zn"][1][:, 0:NP_]).then_inc(c_in, 16)
            sp.dma_start(k_cmp[:], d["kcT"][:, NS * NCK:]).then_inc(c_in, 16)
            sp.dma_start(v_sel[:], d["vtok"][0].rearrange("t p n -> p t n")).then_inc(c_in, 16)
            sp.dma_start(v_win[:], d["vtok"][1].rearrange("t p n -> p t n")).then_inc(c_in, 16)
            sp.dma_start(v_cmp[:], d["vc"][:, NS, :]).then_inc(c_in, 16)
            sp.dma_start(near[:].rearrange("p g r n -> p (g r) n"),
                         bass.AP(d["dist"].tensor, RMAX - P, [[8 * RLEN - 1, P], [RLEN, 8], [1, 2 * P]])).then_inc(c_in, 16)
            sp.dma_start(wmask[:], d["wmask"]).then_inc(c_in, 16)
            sp.dma_start(cmask[:], d["cmask"]).then_inc(c_in, 16)
            sp.wait_ge(m_done, 2)
            for h in range(8):
                sp.dma_start(cstrip[:, h // R, h % R, 40:64],
                             bass.AP(d["dist"].tensor, h * RLEN + 16 * 40 - 505, [[8 * RLEN - 1, P], [16, 24]]), allow_slow_non_contiguous=True).then_inc(c_in, 16)

            def load_q(b, s):
                sp.dma_start(q[:, s], d["zn"][2 + 2 * (b % 2) + s][:, (b // 2) * P:(b // 2 + 1) * P]).then_inc(q_in[s], 16)

            sp.sem_inc(o_out[0], 16)
            sp.sem_inc(o_out[1], 16)
            load_q(0, 0)
            load_q(0, 1)
            for b in range(2 * QT):
                qt = b // 2
                sp.wait_ge(f_lo, b + 1)
                sp.dma_start(raw[:], d["w_in"][U_LX + b + 1]).then_inc(f_in, 16)
                if b >= 1:
                    sp.wait_ge(f_ev, 3 * b + 1)
                    sp.dma_start(d["z"][U_LX + b - 1], zf[:]).then_inc(f_out, 16)
                for s in range(2):
                    if b + 1 < 2 * QT:
                        sp.wait_ge(s_mm, NJ * b + NH * s + NH)
                        load_q(b + 1, s)
                    sp.wait_ge(s_te, tbase(qt) + (b % 2) * (before(qt, NJ) + 2) + turn_at(qt, s) + 3)
                    sp.dma_start(d["o_nsa"][2 * (b % 2) + s][:, qt * P:(qt + 1) * P], oT[:, s]).then_inc(o_out[s], 16)
            sp.wait_ge(f_ev, 3 * 2 * QT + 1)
            sp.dma_start(d["z"][U_LX + 2 * QT - 1], zf[:]).then_inc(f_out, 16)
            sp.wait_ge(f_out, 16 * (2 * QT + 1))
            sp.wait_ge(f_in, 16 * (2 * QT + 1))
            sp.wait_ge(o_out[0], 16 * (2 * QT + 1))
            sp.wait_ge(o_out[1], 16 * (2 * QT + 1))

        @block.gpsimd
        def _(pool):
            pool.memset(cstrip[:, :, :, 0:64], 0.0).then_inc(m_done, 1)
            pool.memset(cstrip[:, :, :, 64:CU], NEGV).then_inc(m_done, 1)
            pool.memset(pr[:, :, 0:P], 0.0).then_inc(m_done, 1)

            pool.wait_ge(f_hi, 1)
            pool.tensor_tensor(w_lo[:], raw[:], w_hi[:].bitcast(F32), ALU.subtract).then_inc(f_lo, 1)
            with pool.Fori(0, 2 * QT) as i:
                pool.wait_ge(f_hi, i * 1 + 2)
                pool.tensor_tensor(w_lo[:], raw[:], w_hi[:].bitcast(F32), ALU.subtract).then_inc(f_lo, 1)

        @block.tensor
        def _(pe):
            pe.sem_inc(s_pvg, 2)
            pe.wait_ge(c_in, 16 * 17)
            for qt in range(QT):
                nv = before(qt, NJ)
                nt = nv + 2
                with pe.Fori(0, 2) as i:

                    def scores(j):
                        s, (g, br) = j // NH, HALF[j % NH]
                        k0, nk = tiles(qt, br)
                        keys = {"sel": k_sel, "win": k_win, "cmp": k_cmp}[br]
                        n = NCMP if br == "cmp" else nk * P
                        if j % NH == 0:
                            pe.wait_ge(q_in[s], i * 16 + (32 * qt + 16))
                        pe.wait_ge(s_exp, i * NJ + (2 * NJ * qt + j + 1))
                        for c in range(0, n, 512):
                            w = min(512, n - c)
                            mm = pe.matmul(S[j % 2][:, c:c + w], q[g * HD:(g + 1) * HD, s, :],
                                           keys[g * HD:(g + 1) * HD, k0 * P + c:k0 * P + c + w], start=True, stop=True)
                        mm.then_inc(s_mm, 1)

                    def values(j):
                        s, (g, br) = j // NH, HALF[j % NH]
                        k0, nk = tiles(qt, br)
                        vals = {"sel": v_sel, "win": v_win}.get(br)
                        if br == "cmp":
                            pe.wait_ge(s_pm, i * 4 + (8 * qt + 2 * s + g + 1))
                        else:
                            pe.wait_ge(s_exp, i * NJ + (2 * NJ * qt + j + 3))
                        for a in range(groups(qt, j)):
                            tg = tgroup(qt, j, a)
                            pe.wait_ge(s_te, i * nt + (tbase(qt) + tg + 1))
                            for t in range(4 * a, min(4 * a + 4, nk)):
                                mm = pe.transpose(tp[tg % 2][:, (t % 4) * P:(t % 4 + 1) * P],
                                                  pr[:, j % 2, t * P:(t + 1) * P], per["ident"][:])
                            mm.then_inc(s_tp, 1)
                        pe.wait_ge(s_acc, i * NJ + (2 * NJ * qt + j + 2))
                        for a in range(groups(qt, j)):
                            vg = before(qt, j) + a
                            pe.wait_ge(s_te, i * nt + (tbase(qt) + tgroup(qt, j, a) + 3))
                            for t in range(4 * a, min(4 * a + 4, nk)):
                                if br == "cmp":
                                    lhs, rhs = ptr[0:NCMP, vg % 2, 0:P], v_cmp[0:NCMP, g * HD:(g + 1) * HD]
                                else:
                                    lhs = ptr[:, vg % 2, (t % 4) * P:(t % 4 + 1) * P]
                                    rhs = vals[:, k0 + t, g * HD:(g + 1) * HD]
                                mm = pe.matmul(O[:, 0:HD], lhs, rhs, start=(t == 0), stop=(t == nk - 1))
                            mm.then_inc(s_pvg, 1)

                    def turn(s):
                        tg = turn_at(qt, s)
                        pe.wait_ge(s_te, i * nt + (tbase(qt) + tg + 1))
                        pe.wait_ge(s_acc, i * NJ + (2 * NJ * qt + NH * s + NH + 2))
                        pe.transpose(tp[tg % 2][:, 0:P], oacc[:, s], per["ident"][:]).then_inc(s_tp, 1)

                    def filler(j):
                        c = j // 3
                        if j == 0:
                            pe.wait_ge(f_lo, i * 1 + (2 * qt + 1))
                        if j % 3 == 0:
                            pe.wait_ge(f_ev, i * 3 + (6 * qt + c + 1))
                        for x in range(8 * (j % 3), 8 * (j % 3) + 8):
                            k, n = x // 3, x % 3
                            w, h = ((w_hi, h_hi), (w_hi, h_lo), (w_lo, h_hi))[n]
                            mm = pe.matmul(facc[:, 0:CW], w[:, k, :], h[:, k, c * CW:(c + 1) * CW], start=(x == 0), stop=(x == 23))
                        if j % 3 == 2:
                            mm.then_inc(f_mm, 1)

                    scores(0)
                    for j in range(NJ):
                        if j + 1 < NJ:
                            scores(j + 1)
                        if j < 9:
                            filler(j)
                        values(j)
                        if j == NH:
                            turn(0)
                    turn(1)

        @block.scalar
        def _(act):
            act.sem_inc(s_exp, 2)
            act.sem_inc(s_te, 2)
            act.wait_ge(m_done, 3)
            act.wait_ge(f_in, 16)
            act.activation(w_hi[:], raw[:], ACT.Copy).then_inc(f_hi, 1)
            for qt in range(QT):
                nv = before(qt, NJ)
                nt = nv + 2
                with act.Fori(0, 2) as i:

                    def probs(j):
                        br = HALF[j % NH][1]
                        n = NCMP if br == "cmp" else tiles(qt, br)[1] * P
                        act.wait_ge(s_max, i * NJ + (2 * NJ * qt + j + 1))
                        act.wait_ge(s_pvg, i * nv + (vbase(qt) + (before(qt, j - 1) + 2 if j >= 1 else 1)))
                        act.activation(pr[:, j % 2, 0:n], S[j % 2][:, 0:n], ACT.Exp, bias=nmx[:, j % 2:j % 2 + 1],
                                       accum_out=rs[:, j % 2:j % 2 + 1]).then_inc(s_exp, 1)

                    def copies(j):
                        k0, nk = tiles(qt, HALF[j % NH][1])
                        cmp = HALF[j % NH][1] == "cmp"
                        for a in range(groups(qt, j)):
                            vg, tg = before(qt, j) + a, tgroup(qt, j, a)
                            m = min(4, nk - 4 * a) * P
                            w = NCMP if cmp else P
                            act.wait_ge(s_pvg, i * nv + (vbase(qt) + vg + 1))
                            act.wait_ge(s_tp, i * nt + (tbase(qt) + tg + 1))
                            act.activation(ptr[0:w, vg % 2, 0:m], tp[tg % 2][0:w, 0:m], ACT.Copy).then_inc(s_te, 1)

                    def turned(s):
                        tg = turn_at(qt, s)
                        act.wait_ge(o_out[s], i * 16 + (32 * qt + 16))
                        act.wait_ge(s_tp, i * nt + (tbase(qt) + tg + 1))
                        act.activation(oT[:, s], tp[tg % 2][:, 0:P], ACT.Copy).then_inc(s_te, 1)

                    probs(0)
                    for j in range(NJ):
                        if j + 1 < NJ:
                            probs(j + 1)
                        copies(j)
                        if j == NH:
                            turned(0)
                        if j == 10:
                            act.wait_ge(f_in, i * 16 + (32 * qt + 32))
                            act.wait_ge(f_mm, i * 3 + (6 * qt + 3))
                            act.activation(w_hi[:], raw[:], ACT.Copy).then_inc(f_hi, 1)
                    turned(1)

        @block.vector
        def _(dve):
            dve.sem_inc(s_acc, 2)
            dve.wait_ge(c_in, 16 * 17)
            dve.sem_inc(f_ev, 1)
            chb = 0
            for qt in range(QT):
                per_body = 46 + (4 if qt >= 4 else 0)
                with dve.Fori(0, 2) as i:
                    count = [0]

                    def chain(ins):
                        count[0] += 1
                        ins.then_inc(s_ch, 1)
                        dve.wait_ge(s_ch, i * per_body + (chb + count[0]))

                    def maxima(j):
                        s, (g, br) = j // NH, HALF[j % NH]
                        k0, nk = tiles(qt, br)
                        x = S[j % 2]
                        n = NCMP if br == "cmp" else nk * P
                        r = i * 2 + s
                        dve.wait_ge(s_mm, i * NJ + (2 * NJ * qt + j + 1))
                        if br == "cmp":
                            c0 = 56 - 8 * qt
                            chain(dve.tensor_tensor(x[:, 0:n], x[:, 0:n], cstrip[:, g, bass.ds(r, 1), c0:c0 + n].rearrange(
                                "p a n -> p (a n)"), ALU.add))
                        else:
                            m = min(nk, 2) * P
                            chain(dve.tensor_tensor(x[:, n - m:n], x[:, n - m:n], near[:, g, bass.ds(r, 1), 2 * P - m:].rearrange(
                                "p a n -> p (a n)"), ALU.add))
                            if br == "win" and qt >= 4:
                                chain(dve.tensor_tensor(x[:, 0:P], x[:, 0:P], wmask[:], ALU.add))
                        dve.tensor_reduce(nmx[:, j % 2:j % 2 + 1], x[:, 0:n], AX, ALU.max, negate=True).then_inc(s_max, 1)

                    def finish(j):
                        s, (g, br) = j // NH, HALF[j % NH]
                        bi = ("cmp", "sel", "win").index(br)
                        v = rs[:, j % 2:j % 2 + 1]
                        dve.wait_ge(s_exp, i * NJ + (2 * NJ * qt + j + 3))
                        if br == "cmp":
                            c0 = 56 - 8 * qt
                            pm = pr[:, j % 2, 0:NCMP]
                            dve.tensor_tensor(pm, pm, cmask[:, c0:c0 + NCMP], ALU.mult).then_inc(s_pm, 1)
                            dve.wait_ge(s_pm, i * 4 + (8 * qt + 2 * s + g + 1))
                            chain(dve.tensor_reduce(v, pm, AX, ALU.add))
                            chain(dve.tensor_scalar(v, v, 1e-30, None, ALU.max))
                        chain(dve.reciprocal(cf[:, 0:1], v))
                        chain(dve.tensor_tensor(cf[:, 1:2], cf[:, 0:1], gsl[:, s, g, bi:bi + 1], ALU.mult))
                        dve.wait_ge(s_pvg, i * before(qt, NJ) + (vbase(qt) + before(qt, j + 1) + 2))
                        o = oacc[:, s, g * HD:(g + 1) * HD]
                        if br == "sel":
                            dve.tensor_scalar(o, O[:, 0:HD], cf[:, 1:2], None, ALU.mult).then_inc(s_acc, 1)
                        else:
                            dve.wait_ge(s_acc, i * NJ + (2 * NJ * qt + j + 2))
                            dve.scalar_tensor_tensor(o, O[:, 0:HD], cf[:, 1:2], o, ALU.mult, ALU.add).then_inc(s_acc, 1)

                    for j in range(NJ + 1):
                        if j < NJ:
                            if j % NH == 0:
                                r = i * 2 + j // NH
                                gt = per["gate"][:, qt, :].rearrange("p (g r c) -> p g r c", g=G, r=R)
                                chain(dve.tensor_copy(gsl[:, j // NH], gt[:, :, bass.ds(r, 1), :].rearrange("p g a c -> p g (a c)")))
                            maxima(j)
                        if j >= 1:
                            finish(j - 1)
                        if j in (3, 6, 9):
                            c = j // 3 - 1
                            if c == 0:
                                dve.wait_ge(f_out, i * 16 + (32 * qt + 16))
                            dve.wait_ge(f_mm, i * 3 + (6 * qt + c + 1))
                            dve.tensor_copy(zf[:, c * CW:(c + 1) * CW], facc[:, 0:CW]).then_inc(f_ev, 1)
                    assert count[0] == per_body, count[0]
                chb += 2 * per_body


def memory_attention(nc, d, per):
    SC = P ** -0.5
    with ExitStack() as ctx:
        sb, ps, sem = sb_of(nc, ctx, "mat"), ps_of(nc, ctx, "mat"), sem_of(nc, ctx, "mat")
        km = sb("km", [P, MH, NMEM])
        vm = sb("vm", [P, MH, 2, P])
        q = sb("q", [P, 2, P])
        pr = sb("pr", [P, 2, NMEM])
        ptr = sb("ptr", [P, 2, NMEM])
        nmx = sb("nmx", [P, 2, 2])
        rs = sb("rs", [P, 2, 2])
        o = sb("o", [P, 2, P])
        oT = sb("oT", [P, 2, P])
        S = [ps(f"S{s}", [P, 512]) for s in range(2)]
        tp = [ps(f"tp{s}", [P, 512]) for s in range(2)]
        O = [ps(f"O{s}", [P, 512]) for s in range(2)]
        oTp = [ps(f"oTp{s}", [P, 512]) for s in range(2)]
        c_in = sem("c_in")
        q_in = [sem("q_in0"), sem("q_in1")]
        o_out = [sem("o_out0"), sem("o_out1")]
        s_mm, s_max, s_neg, s_exp, s_tp, s_te, s_pv, s_rc, s_on, s_ot, s_oe = (
            sem(x) for x in ("s_mm", "s_max", "s_neg", "s_exp", "s_tp", "s_te", "s_pv", "s_rc", "s_on", "s_ot", "s_oe"))
        block = ctx.enter_context(nc.Block())

        @block.sync
        def _(sp):
            clear_last(sp)
            sp.dma_start(km[:], d["memn"].rearrange("h p n -> p h n")).then_inc(c_in, 16)
            sp.dma_start(vm[:], d["memv"].rearrange("h t p n -> p h t n")).then_inc(c_in, 16)
            sp.sem_inc(o_out[0], 16)
            sp.sem_inc(o_out[1], 16)
            for n in range(MH * QT):
                s = n % 2
                if n >= 2:
                    sp.wait_ge(s_mm, n - 1)
                sp.dma_start(q[:, s], d["zn"][6 + n // QT][:, (n % QT) * P:(n % QT + 1) * P]).then_inc(q_in[s], 16)
                if n >= 1:
                    m = n - 1
                    sp.wait_ge(s_oe, m + 1)
                    sp.dma_start(d["o_mem"][m // QT][:, (m % QT) * P:(m % QT + 1) * P], oT[:, m % 2]).then_inc(o_out[m % 2], 16)
            m = MH * QT - 1
            sp.wait_ge(s_oe, m + 1)
            sp.dma_start(d["o_mem"][m // QT][:, (m % QT) * P:(m % QT + 1) * P], oT[:, m % 2]).then_inc(o_out[m % 2], 16)
            sp.wait_ge(o_out[0], 16 * (MH * QT // 2 + 1))
            sp.wait_ge(o_out[1], 16 * (MH * QT // 2 + 1))

        @block.tensor
        def _(pe):
            pe.wait_ge(c_in, 32)
            with pe.Fori(0, MH) as h:
                with pe.Fori(0, QT // 2) as i:
                    for s in range(2):
                        pe.wait_ge(q_in[s], h * (16 * QT // 2) + i * 16 + 16)
                        pe.wait_ge(s_exp, h * QT + i * 2 + (s + 1))
                        pe.matmul(S[s][:, 0:NMEM], q[:, s], km[:, bass.ds(h, 1), :].rearrange("p a n -> p (a n)"),
                                  start=True, stop=True).then_inc(s_mm, 1)
                        pe.wait_ge(s_exp, h * QT + i * 2 + (s + 3))
                        for t in range(2):
                            mm = pe.transpose(tp[s][:, t * P:(t + 1) * P], pr[:, s, t * P:(t + 1) * P], per["ident"][:])
                        mm.then_inc(s_tp, 1)
                        pe.wait_ge(s_te, h * QT + i * 2 + (s + 1))
                        for t in range(2):
                            mm = pe.matmul(O[s][:, 0:P], ptr[:, s, t * P:(t + 1) * P],
                                           vm[:, bass.ds(h, 1), t, :].rearrange("p a n -> p (a n)"), start=(t == 0), stop=(t == 1))
                        mm.then_inc(s_pv, 1)
                        pe.wait_ge(s_on, h * QT + i * 2 + (s + 1))
                        pe.transpose(oTp[s][:, 0:P], o[:, s], per["ident"][:]).then_inc(s_ot, 1)

        @block.vector
        def _(dve):
            with dve.Fori(0, MH) as h:
                with dve.Fori(0, QT // 2) as i:
                    for s in range(2):
                        dve.wait_ge(s_mm, h * QT + i * 2 + (s + 1))
                        dve.tensor_reduce(nmx[:, s, 0:1], S[s][:, 0:NMEM], AX, ALU.max).then_inc(s_neg, 1)
                        dve.wait_ge(s_neg, h * QT + i * 2 + (s + 1))
                        dve.tensor_scalar(nmx[:, s, 1:2], nmx[:, s, 0:1], -SC, None, ALU.mult).then_inc(s_max, 1)
                        dve.wait_ge(s_tp, h * QT + i * 2 + (s + 1))
                        dve.tensor_copy(ptr[:, s], tp[s][:, 0:NMEM]).then_inc(s_te, 1)
                        dve.reciprocal(rs[:, s, 1:2], rs[:, s, 0:1]).then_inc(s_rc, 1)
                        dve.wait_ge(s_rc, h * QT + i * 2 + (s + 1))
                        dve.wait_ge(s_pv, h * QT + i * 2 + (s + 1))
                        dve.tensor_scalar(o[:, s], O[s][:, 0:P], rs[:, s, 1:2], None, ALU.mult).then_inc(s_on, 1)

        @block.scalar
        def _(act):
            act.sem_inc(s_exp, 2)
            with act.Fori(0, MH) as h:
                with act.Fori(0, QT // 2) as i:
                    for s in range(2):
                        act.wait_ge(s_max, h * QT + i * 2 + (s + 1))
                        act.activation(pr[:, s], S[s][:, 0:NMEM], ACT.Exp, bias=nmx[:, s, 1:2], scale=SC,
                                       accum_out=rs[:, s, 0:1]).then_inc(s_exp, 1)
                        act.wait_ge(s_ot, h * QT + i * 2 + (s + 1))
                        act.wait_ge(o_out[s], h * (16 * QT // 2) + i * 16 + 16)
                        act.activation(oT[:, s], oTp[s][:, 0:P], ACT.Copy).then_inc(s_oe, 1)


def sample_attention(nc, d, per):
    RW = NS * 8
    LS = NP_ + 1
    LW = WIN + 1
    NB = 16
    with ExitStack() as ctx:
        sb, ps, sem = sb_of(nc, ctx, "sat"), ps_of(nc, ctx, "sat"), sem_of(nc, ctx, "sat")
        pt = sb("pt", [1, NS * PAGES], I32)
        qs = sb("qs", [P, R, NS])
        qb = sb("qb", [P, NS, RW])
        knew = sb("knew", [P, NS, 2])
        vnew = sb("vnew", [1, NS, 2, P])
        kc = sb("kc", [P, NS, NCK])
        ks = sb("ks", [P, 2, PAGES, P])
        kw = sb("kw", [P, 2, WIN])
        vs = sb("vs", [P, 2, PAGES, P])
        vw = sb("vw", [P, 2, WIN // P, P])
        vc = sb("vc", [NCK, 2, P])
        b_far = sb("b_far", [RW, P + 1])
        b_cmp = sb("b_cmp", [RW, 23])
        gt = sb("gt", [RW, 3])
        grp = sb("grp", [RW, RW])
        blk = sb("blk", [RW, NB])
        ls = sb("ls", [RW, LS + 7])
        lw = sb("lw", [RW, LW + 7])
        lc = sb("lc", [RW, NCK])
        sc = sb("sc", [RW, 16])
        sel = sb("sel", [RW, 4, NB])
        keep = sb("keep", [RW, NCK])
        pT = sb("pT", [P, 13, RW])
        nT = sb("nT", [1, 2, RW])
        oT = sb("oT", [P, R, NS])
        S0, S1, S2, S3, S4 = (ps(f"S{n}", [P, 512]) for n in range(5))
        S5, S6, S7 = (ps(f"S{n}", [P, 512]) for n in range(5, 8))
        c_in, b_in, z_done, qb_done, vn_in, pt_in = sem("c_in"), sem("b_in"), sem("z_done"), sem("qb_done"), sem("vn_in"), sem("pt_in")
        k_in = [sem("k_in0"), sem("k_in1")]
        v_in = [sem("v_in0"), sem("v_in1")]
        s_mm, ch, e_done, a_done, g_mm, tp_done, te_done, o_mm, o_done, o_out, s_all, m_done = (
            sem(x) for x in ("s_mm", "ch", "e_done", "a_done", "g_mm", "tp_done", "te_done", "o_mm", "o_done", "o_out",
                             "s_all", "m_done"))
        block = ctx.enter_context(nc.Block())
        dist = d["dist"].tensor

        @block.sync
        def _(sp):
            clear_last(sp)
            sp.dma_start(pt[:], d["page_table"]).then_inc(pt_in, 16)
            sp.dma_start(qs[:], d["zn"][2:6][:, :, NP_:T].rearrange("r p b -> p r b")).then_inc(c_in, 16)
            sp.dma_start(knew[:, :, 0], d["zn"][0][:, NP_:T], allow_slow_non_contiguous=True).then_inc(c_in, 16)
            sp.dma_start(knew[:, :, 1], d["zn"][1][:, NP_:T], allow_slow_non_contiguous=True).then_inc(c_in, 16)
            sp.dma_start(kc[:].rearrange("p b c -> p (b c)"), d["kcT"][:, 0:NS * NCK]).then_inc(c_in, 16)
            sp.dma_start(grp[:], d["grp"]).then_inc(c_in, 16)
            sp.dma_start(blk[:], d["blk"]).then_inc(c_in, 16)
            sp.dma_start(gt[:], d["gate_s"].rearrange("(r c) o -> r (c o)", c=3)).then_inc(c_in, 16)
            for b in range(NS):
                sp.dma_start(b_far[b * 8:(b + 1) * 8, :],
                             bass.AP(dist, RMAX - P, [[RLEN, 8], [1, P + 1]])).then_inc(b_in, 16)
                sp.dma_start(b_cmp[b * 8:(b + 1) * 8, :],
                             bass.AP(dist, 16 * 40 - 633, [[RLEN, 8], [16, 23]]), allow_slow_non_contiguous=True).then_inc(b_in, 16)
                for j, u in enumerate((U_SELV, U_WINV)):
                    sp.dma_start(vnew[0:1, b, j, :], bass.AP(d["z"].tensor, u * P * T + NP_ + b, [[0, 1], [T, P]]),
                                 allow_slow_non_contiguous=True).then_inc(vn_in, 16)
            sp.wait_ge(pt_in, 16)
            for b in range(NS):
                if b >= 2:
                    sp.wait_ge(s_mm, b - 1)
                sp.dma_start(kw[:, b % 2], d["winkT"][b]).then_inc(k_in[b % 2], 16)
                with sp.Fori(0, PAGES) as i:
                    page = sp.value_load(pt[0:1, bass.ds(i + b * PAGES, 1)], min_val=0, max_val=d["sel_kT"].shape[0] - 1)
                    sp.dma_start(ks[:, b % 2, bass.ds(i, 1), :].rearrange("p a n -> p (a n)"),
                                 d["sel_kT"][bass.ds(page, 1)].rearrange("a p n -> p (a n)")).then_inc(k_in[b % 2], 16)
            for b in range(NS):
                if b >= 2:
                    sp.wait_ge(o_mm, b - 1)
                sp.dma_start(vw[:, b % 2], d["win_v"][b].rearrange("t p n -> p t n")).then_inc(v_in[b % 2], 16)
                sp.dma_start(vc[:, b % 2], d["vc"][:, b, :]).then_inc(v_in[b % 2], 16)
                with sp.Fori(0, PAGES) as i:
                    page = sp.value_load(pt[0:1, bass.ds(i + b * PAGES, 1)], min_val=0, max_val=d["sel_v"].shape[0] - 1)
                    sp.dma_start(vs[:, b % 2, bass.ds(i, 1), :].rearrange("p a n -> p (a n)"),
                                 d["sel_v"][bass.ds(page, 1)].rearrange("a p n -> p (a n)")).then_inc(v_in[b % 2], 16)
            sp.wait_ge(o_done, 2)
            sp.dma_start(d["o_nsa"][:, :, NP_:T].rearrange("r p b -> p r b"), oT[:]).then_inc(o_out, 16)
            sp.wait_ge(o_out, 16)

        @block.tensor
        def _(pe):
            pe.wait_ge(qb_done, 2)
            pe.wait_ge(c_in, 16 * 7)
            for b in range(NS):
                st, sp_ = b == 0, b == NS - 1
                lhs = qb[:, b, :]
                pe.wait_ge(k_in[b % 2], 16 * 9 * (b // 2 + 1))
                pe.matmul(S0[0:RW, :], lhs, ks[:, b % 2, 0:4].rearrange("p a n -> p (a n)"), start=st, stop=sp_)
                pe.matmul(S1[0:RW, :], lhs, ks[:, b % 2, 4:8].rearrange("p a n -> p (a n)"), start=st, stop=sp_)
                pe.matmul(S2[0:RW, :], lhs, kw[:, b % 2], start=st, stop=sp_)
                pe.matmul(S3[0:RW, 0:2], lhs, knew[:, b, :], start=st, stop=sp_)
                pe.matmul(S4[0:RW, 0:NCK], lhs, kc[:, b, :], start=st, stop=sp_).then_inc(s_mm, 1)
            pe.wait_ge(g_mm, 1)
            pe.matmul(S5[0:RW, 0:NCMP], grp[:], lc[:, 0:NCMP], start=True, stop=True).then_inc(tp_done, 1)
            pe.wait_ge(m_done, 1)
            idn = per["ident"][0:RW, 0:RW]
            for t in range(8):
                pe.transpose(S6[:, t * RW:(t + 1) * RW], ls[:, t * P:(t + 1) * P], idn)
            for t in range(4):
                pe.transpose(S7[:, t * RW:(t + 1) * RW], lw[:, t * P:(t + 1) * P], idn)
            pe.transpose(S7[0:NCMP, 4 * RW:5 * RW], lc[:, 0:NCMP], idn)
            pe.transpose(S5[0:1, 128:128 + RW], ls[:, NP_:LS], idn)
            pe.transpose(S5[0:1, 256:256 + RW], lw[:, WIN:LW], idn).then_inc(tp_done, 1)
            pe.wait_ge(te_done, 4)
            pe.wait_ge(vn_in, 16 * 2 * NS)
            for b in range(NS):
                s, c = b % 2, slice(b * 8, (b + 1) * 8)
                pe.wait_ge(v_in[s], 16 * 10 * (b // 2 + 1))
                for t in range(8):
                    pe.matmul(S0[:, c], vs[:, s, t], pT[:, t, c], start=(t == 0), stop=False)
                for t in range(4):
                    pe.matmul(S0[:, c], vw[:, s, t], pT[:, 8 + t, c], start=False, stop=False)
                pe.matmul(S0[:, c], vc[0:NCMP, s], pT[0:NCMP, 12, c], start=False, stop=False)
                pe.matmul(S0[:, c], vnew[0:1, b, 0, :], nT[0:1, 0, c], start=False, stop=False)
                pe.matmul(S0[:, c], vnew[0:1, b, 1, :], nT[0:1, 1, c], start=False, stop=True).then_inc(o_mm, 1)

        @block.scalar
        def _(act):
            act.wait_ge(a_done, 1)
            act.activation(lc[:, 0:NCMP], lc[:, 0:NCMP], ACT.Exp, bias=sc[:, 0:1], accum_out=sc[:, 1:2]).then_inc(e_done, 1)
            act.wait_ge(a_done, 2)
            act.activation(ls[:, 0:LS], ls[:, 0:LS], ACT.Exp, bias=sc[:, 2:3], accum_out=sc[:, 3:4]).then_inc(e_done, 1)
            act.wait_ge(a_done, 3)
            act.activation(lw[:, 0:LW], lw[:, 0:LW], ACT.Exp, bias=sc[:, 4:5], accum_out=sc[:, 5:6]).then_inc(e_done, 1)

        @block.vector
        def _(dve):
            n = [0]

            def chain(ins):
                n[0] += 1
                ins.then_inc(ch, 1)
                dve.wait_ge(ch, n[0])

            chain(dve.memset(qb[:], 0.0))
            dve.wait_ge(c_in, 16 * 7)
            for g in range(G):
                rows = slice(g * HD, (g + 1) * HD)
                q0 = qb[rows].rearrange("p b c -> p (b c)")
                for b in range(NS):
                    ins = dve.tensor_copy(q0[:, b * (RW + 8) + g * R:b * (RW + 8) + (g + 1) * R], qs[rows, :, b])
                ins.then_inc(qb_done, 1)
            dve.wait_ge(s_mm, NS)
            dve.wait_ge(b_in, 16 * 2 * NS)
            chain(dve.tensor_copy(lc[:, 0:40], S4[0:RW, 0:40]))
            chain(dve.tensor_tensor(lc[:, 40:NCMP], S4[0:RW, 40:NCMP], b_cmp[:], ALU.add))
            dve.tensor_reduce(sc[:, 0:1], lc[:, 0:NCMP], AX, ALU.max, negate=True).then_inc(a_done, 1)
            dve.wait_ge(e_done, 1)
            chain(dve.reciprocal(sc[:, 6:7], sc[:, 1:2]))
            dve.tensor_scalar(lc[:, 0:NCMP], lc[:, 0:NCMP], sc[:, 6:7], None, ALU.mult).then_inc(g_mm, 1)
            dve.wait_ge(tp_done, 1)
            ssum = keep[:]
            chain(dve.memset(ssum[:, NCMP:NCK], 0.0))
            chain(dve.tensor_copy(ssum[:, 0:NCMP], S5[0:RW, 0:NCMP]))
            chain(dve.tensor_reduce(sel[:, 0], ssum.rearrange("p (s c) -> p s c", c=4), AX, ALU.add))
            chain(dve.tensor_tensor(sel[:, 0, 1:NB], sel[:, 0, 1:NB], ssum.rearrange("p (s c) -> p s c", c=4)[:, 0:NB - 1, 3], ALU.add))
            chain(dve.tensor_reduce(sc[:, 7:8], sel[:, 0, 1:NB - 1], AX, ALU.min))
            chain(dve.memset(sel[:, 1], 0.0))
            chain(dve.tensor_scalar(sel[:, 1, 1:NB - 1], sel[:, 0, 1:NB - 1], sc[:, 7:8], None, ALU.is_le))
            chain(dve.tensor_tensor(sel[:, 1], sel[:, 1], blk[:], ALU.mult))
            chain(dve.tensor_reduce(sc[:, 8:9], sel[:, 1], AX, ALU.max))
            chain(dve.tensor_scalar(sel[:, 2], blk[:], sc[:, 8:9], NEGV, ALU.is_equal, ALU.mult))
            chain(dve.tensor_copy(ls[:, 0:512], S0[0:RW, :]))
            chain(dve.tensor_copy(ls[:, 512:NP_ - P], S1[0:RW, 0:512 - P]))
            chain(dve.tensor_tensor(ls[:, NP_ - P:NP_], S1[0:RW, 512 - P:512], b_far[:, 0:P], ALU.add))
            chain(dve.tensor_tensor(ls[:, NP_:LS], S3[0:RW, 0:1], b_far[:, P:P + 1], ALU.add))
            chain(dve.tensor_tensor(ls[:, 0:NP_].rearrange("p (s c) -> p s c", s=NB), ls[:, 0:NP_].rearrange("p (s c) -> p s c", s=NB),
                                    sel[:, 2].rearrange("p (s a) -> p s a", a=1).to_broadcast([RW, NB, NP_ // NB]), ALU.add))
            dve.tensor_reduce(sc[:, 2:3], ls[:, 0:LS], AX, ALU.max, negate=True).then_inc(a_done, 1)
            chain(dve.tensor_copy(lw[:, 0:WIN - P], S2[0:RW, 0:WIN - P]))
            chain(dve.tensor_tensor(lw[:, WIN - P:WIN], S2[0:RW, WIN - P:WIN], b_far[:, 0:P], ALU.add))
            chain(dve.tensor_tensor(lw[:, WIN:LW], S3[0:RW, 1:2], b_far[:, P:P + 1], ALU.add))
            chain(dve.memset(lw[:, 0:1], NEGV))
            dve.tensor_reduce(sc[:, 4:5], lw[:, 0:LW], AX, ALU.max, negate=True).then_inc(a_done, 1)
            chain(dve.tensor_scalar(lc[:, 0:NCMP], lc[:, 0:NCMP], gt[:, 0:1], None, ALU.mult))
            dve.wait_ge(e_done, 2)
            chain(dve.reciprocal(sc[:, 9:10], sc[:, 3:4]))
            chain(dve.tensor_scalar(ls[:, 0:LS], ls[:, 0:LS], sc[:, 9:10], gt[:, 1:2], ALU.mult, ALU.mult))
            dve.wait_ge(e_done, 3)
            chain(dve.reciprocal(sc[:, 10:11], sc[:, 5:6]))
            dve.tensor_scalar(lw[:, 0:LW], lw[:, 0:LW], sc[:, 10:11], gt[:, 2:3], ALU.mult, ALU.mult).then_inc(m_done, 1)
            dve.wait_ge(tp_done, 2)
            dve.tensor_copy(pT[:, 0:8].rearrange("p t r -> p (t r)"), S6[:, 0:8 * RW]).then_inc(te_done, 1)
            dve.tensor_copy(pT[:, 8:12].rearrange("p t r -> p (t r)"), S7[:, 0:4 * RW]).then_inc(te_done, 1)
            dve.tensor_copy(pT[0:NCMP, 12], S7[0:NCMP, 4 * RW:5 * RW]).then_inc(te_done, 1)
            dve.tensor_copy(nT[:], S5[0:1, 128:384].rearrange("p (j n) -> p j n", j=2)[:, :, 0:RW]).then_inc(te_done, 1)
            dve.wait_ge(o_mm, NS)
            for g in range(G):
                rows = slice(g * HD, (g + 1) * HD)
                dve.tensor_copy(oT[rows], S0[rows, 0:RW].rearrange("p (b h) -> p h b", h=8)[:, g * R:(g + 1) * R, :]).then_inc(o_done, 1)


def sample_memory(nc, d, per):
    RW = NS * MH
    RP = 64
    SC = P ** -0.5
    with ExitStack() as ctx:
        sb, ps, sem = sb_of(nc, ctx, "sme"), ps_of(nc, ctx, "sme"), sem_of(nc, ctx, "sme")
        qs = sb("qs", [P, MH, NS])
        qb = sb("qb", [P, RW, RP])
        km = sb("km", [P, 2, MH, NMEM])
        vm = sb("vm", [P, 2, 2, MH, P])
        pr = sb("pr", [RW, NMEM])
        pT = sb("pT", [P, 2, RW])
        sc = sb("sc", [RW, 4])
        oT = sb("oT", [P, MH, NS])
        O, tp, S = ps("O", [P, 512]), ps("tp", [P, 512]), ps("S", [P, 512])
        c_in, z_done, qb_done = sem("c_in"), sem("z_done"), sem("qb_done")
        k_in = [sem("k_in0"), sem("k_in1")]
        v_in = [sem("v_in0"), sem("v_in1")]
        s_mm, ch, a_done, e_done, p_done, tp_done, te_done, o_mm, o_done, o_out = (
            sem(x) for x in ("s_mm", "ch", "a_done", "e_done", "p_done", "tp_done", "te_done", "o_mm", "o_done", "o_out"))
        block = ctx.enter_context(nc.Block())

        @block.sync
        def _(sp):
            clear_last(sp)
            sp.dma_start(qs[:], d["zn"][6:10][:, :, NP_:T].rearrange("r p b -> p r b")).then_inc(c_in, 16)
            for b in range(NS):
                if b >= 2:
                    sp.wait_ge(s_mm, b - 1)
                sp.dma_start(km[:, b % 2], d["mem_kT"][b]).then_inc(k_in[b % 2], 16)
            for b in range(NS):
                if b >= 2:
                    sp.wait_ge(o_mm, b - 1)
                sp.dma_start(vm[:, b % 2], d["mem_v"][b].rearrange("t p h n -> p t h n")).then_inc(v_in[b % 2], 16)
            sp.wait_ge(o_done, 1)
            sp.dma_start(d["o_mem"][:, :, NP_:T].rearrange("r p b -> p r b"), oT[:]).then_inc(o_out, 16)
            sp.wait_ge(o_out, 16)

        @block.tensor
        def _(pe):
            pe.wait_ge(qb_done, 1)
            for b in range(NS):
                pe.wait_ge(k_in[b % 2], 16 * (b // 2 + 1))
                for h in range(MH):
                    n = b * MH + h
                    mm = pe.matmul(S[0:RP, 0:NMEM], qb[:, n, :], km[:, b % 2, h, :], start=(n == 0), stop=(n == RW - 1))
                mm.then_inc(s_mm, 1)
            pe.wait_ge(p_done, 1)
            for t in range(2):
                mm = pe.transpose(tp[:, t * RW:(t + 1) * RW], pr[:, t * P:(t + 1) * P], per["ident"][0:RW, 0:RW])
            mm.then_inc(tp_done, 1)
            pe.wait_ge(te_done, 1)
            for b in range(NS):
                pe.wait_ge(v_in[b % 2], 16 * (b // 2 + 1))
                for h in range(MH):
                    n = b * MH + h
                    for t in range(2):
                        mm = pe.matmul(O[:, n:n + 1], vm[:, b % 2, t, h, :], pT[:, t, n:n + 1], start=(t == 0), stop=(t == 1))
                mm.then_inc(o_mm, 1)

        @block.scalar
        def _(act):
            act.wait_ge(a_done, 1)
            act.activation(pr[:], S[0:RW, 0:NMEM], ACT.Exp, bias=sc[:, 1:2], scale=SC, accum_out=sc[:, 2:3]).then_inc(e_done, 1)

        @block.vector
        def _(dve):
            dve.memset(qb[:], 0.0).then_inc(z_done, 1)
            dve.wait_ge(z_done, 1)
            dve.wait_ge(c_in, 16)
            q0 = qb[:].rearrange("p n c -> p (n c)")
            for n in range(RW):
                ins = dve.tensor_copy(q0[:, n * (RP + 1):n * (RP + 1) + 1], qs[:, n % MH, n // MH:n // MH + 1])
            ins.then_inc(qb_done, 1)
            dve.wait_ge(s_mm, NS)
            dve.tensor_reduce(sc[:, 0:1], S[0:RW, 0:NMEM], AX, ALU.max).then_inc(ch, 1)
            dve.wait_ge(ch, 1)
            dve.tensor_scalar(sc[:, 1:2], sc[:, 0:1], -SC, None, ALU.mult).then_inc(a_done, 1)
            dve.wait_ge(e_done, 1)
            dve.reciprocal(sc[:, 3:4], sc[:, 2:3]).then_inc(ch, 1)
            dve.wait_ge(ch, 2)
            dve.tensor_scalar(pr[:], pr[:], sc[:, 3:4], None, ALU.mult).then_inc(p_done, 1)
            dve.wait_ge(tp_done, 1)
            dve.tensor_copy(pT[:].rearrange("p t n -> p (t n)"), tp[:, 0:2 * RW]).then_inc(te_done, 1)
            dve.wait_ge(o_mm, NS)
            dve.tensor_copy(oT[:], O[:, 0:RW].rearrange("p (b h) -> p h b", h=MH)).then_inc(o_done, 1)


def load_split(nc, tag, tiles, hi, lo, cols):
    with ExitStack() as ctx:
        sb, sem = sb_of(nc, ctx, tag), sem_of(nc, ctx, tag)
        raw = sb("raw", [P, 2, cols])
        t_in = [sem("t_in0"), sem("t_in1")]
        hi_done, lo_done = sem("hi_done"), sem("lo_done")
        block = ctx.enter_context(nc.Block())

        @block.sync
        def _(sp):
            clear_last(sp)
            for k, t in enumerate(tiles):
                if k >= 2:
                    sp.wait_ge(lo_done, k - 1)
                sp.dma_start(raw[:, k % 2], t).then_inc(t_in[k % 2], 16)

        @block.scalar
        def _(act):
            for k in range(len(tiles)):
                act.wait_ge(t_in[k % 2], 16 * (k // 2 + 1))
                act.activation(hi[:, k], raw[:, k % 2], ACT.Copy).then_inc(hi_done, 1)

        @block.vector
        def _(dve):
            for k in range(len(tiles)):
                dve.wait_ge(hi_done, k + 1)
                dve.tensor_tensor(lo[:, k], raw[:, k % 2], hi[:, k].bitcast(F32), ALU.subtract).then_inc(lo_done, 1)


def merge(nc, d, x_hi, x_lo):
    with ExitStack() as ctx:
        sb, ps, sem = sb_of(nc, ctx, "mrg"), ps_of(nc, ctx, "mrg"), sem_of(nc, ctx, "mrg")
        raw = sb("raw", [P, 2, KT, P])
        w_hi = sb("w_hi", [P, 2, KT, P], F32R)
        w_lo = sb("w_lo", [P, 2, KT, P], F32R)
        mg = sb("mg", [P, 2, 3, T])
        z = sb("z", [P, 2, T])
        acc = [ps(f"acc{s}", [P, NCH, 512]) for s in range(2)]
        raw_in = [sem("raw_in0"), sem("raw_in1")]
        mg_in = [sem("mg_in0"), sem("mg_in1")]
        z_out = [sem("z_out0"), sem("z_out1")]
        hi_done, lo_done, mm_done, ev_done, sg_done, z_done, ch = (
            sem(x) for x in ("hi_done", "lo_done", "mm_done", "ev_done", "sg_done", "z_done", "ch"))
        block = ctx.enter_context(nc.Block())
        GROUPS = [(0, 0, KT, 0), (1, 0, 4, 8), (1, 4, 4, 12), (2, 0, KT, 0), (3, 0, 4, 8), (3, 4, 4, 12)]
        UNIT_FREE = {0: 3 + 1, 1: 5 + 1, 2: 6 + 0 + 1, 3: 6 + 2 + 1}

        @block.sync
        def _(sp):
            clear_last(sp)
            sp.sem_inc(z_out[0], 16)
            sp.sem_inc(z_out[1], 16)
            sp.sem_inc(z_done, 2)
            for s in range(2):
                sp.dma_start(raw[:, s], d["w_up"][s]).then_inc(raw_in[s], 16)
            with sp.Fori(0, KT // 2) as i:
                for m in range(2):
                    row = [sp.snap(i * 2 + (U_MG + 8 * b + m)) for b in range(3)]
                    sp.wait_ge(z_done, i * 2 + (m + 1))
                    for b in range(3):
                        sp.dma_start(mg[:, m, b], d["z"][bass.ds(row[b], 1)].rearrange("a p n -> p (a n)")).then_inc(mg_in[m], 16)
                for u in range(4):
                    nxt = sp.snap(i * 4 + (u + 2))
                    sp.wait_ge(lo_done, i * 4 + (u + 1))
                    sp.dma_start(raw[:, u % 2], d["w_up"][bass.ds(nxt, 1)].rearrange("a p k n -> p (a k) n")).then_inc(raw_in[u % 2], 16)
                    if u % 2:
                        cur = sp.snap(i * 2 + u // 2)
                        sp.wait_ge(z_done, i * 2 + (u // 2 + 3))
                        sp.dma_start(d["zm"][bass.ds(cur, 1)].rearrange("a p n -> p (a n)"), z[:, u // 2]).then_inc(z_out[u // 2], 16)
            for s in range(2):
                sp.wait_ge(z_out[s], 16 * (KT // 2 + 1))
                sp.wait_ge(raw_in[s], 16 * (KT + 1))

        @block.scalar
        def _(act):
            with act.Fori(0, KT // 2) as i:
                for u in range(4):
                    if u % 2 == 0:
                        m = u // 2
                        act.wait_ge(mg_in[m], i * 48 + 48)
                        act.activation(mg[:, m], mg[:, m], ACT.Sigmoid).then_inc(sg_done, 1)
                    act.wait_ge(raw_in[u % 2], i * 32 + (16 * (u // 2) + 16))
                    act.wait_ge(mm_done, i * 6 + UNIT_FREE[u])
                    act.activation(w_hi[:, u % 2], raw[:, u % 2], ACT.Copy).then_inc(hi_done, 1)

        @block.gpsimd
        def _(pool):
            with pool.Fori(0, KT // 2) as i:
                for u in range(4):
                    pool.wait_ge(hi_done, i * 4 + (u + 1))
                    pool.tensor_tensor(w_lo[:, u % 2], raw[:, u % 2], w_hi[:, u % 2].bitcast(F32), ALU.subtract).then_inc(lo_done, 1)

        @block.tensor
        def _(pe):
            pe.sem_inc(mm_done, 6)
            with pe.Fori(0, KT // 2) as i:
                for g, (u, k0, nk, x0) in enumerate(GROUPS):
                    pe.wait_ge(lo_done, i * 4 + (u + 1))
                    pe.wait_ge(ev_done, i * 6 + (g + 1))
                    for k in range(nk):
                        for n, (w, x) in enumerate(((w_hi, x_hi), (w_hi, x_lo), (w_lo, x_hi))):
                            for c in range(NCH):
                                mm = pe.matmul(acc[g % 2][:, c, 0:CW], w[:, u % 2, k0 + k, :], x[:, x0 + k, c * CW:(c + 1) * CW],
                                               start=(k + n == 0), stop=(k == nk - 1 and n == 2))
                    mm.then_inc(mm_done, 1)

        @block.vector
        def _(dve):
            dve.sem_inc(ev_done, 2)
            with dve.Fori(0, KT // 2) as i:
                for g in range(6):
                    m, b = g // 3, g % 3
                    a = acc[g % 2][:, :, 0:CW]
                    gate = mg[:, m, b].rearrange("p (c n) -> p c n", c=NCH)
                    zz = z[:, m].rearrange("p (c n) -> p c n", c=NCH)
                    if b == 0:
                        dve.wait_ge(sg_done, i * 2 + (m + 1))
                        dve.wait_ge(z_out[m], i * 16 + 16)
                        dve.wait_ge(mm_done, i * 6 + (g + 7))
                        dve.tensor_tensor(zz, a, gate, ALU.mult).then_inc(ev_done, 1)
                    else:
                        dve.wait_ge(mm_done, i * 6 + (g + 7))
                        dve.tensor_tensor(gate, a, gate, ALU.mult).then_inc(ev_done, 1)
                        dve.wait_ge(ev_done, i * 6 + (g + 3))
                        if b == 2:
                            dve.wait_ge(ch, i * 2 + (m + 1))
                        ins = dve.tensor_tensor(zz, zz, gate, ALU.add)
                        ins.then_inc(ch if b == 1 else z_done, 1)


def residual_norm(nc, d, per, h, f_hi, f_lo):
    with ExitStack() as ctx:
        sb, ps, sem = sb_of(nc, ctx, "res"), ps_of(nc, ctx, "res"), sem_of(nc, ctx, "res")
        zo = sb("zo", [P, 2, T])
        sq = sb("sq", [P, 2, T])
        rstd = sb("rstd", [P, T])
        ss = ps("ss", [P, NCH, 512])
        x_in = sem("x_in")
        z_in = [sem("z_in0"), sem("z_in1")]
        h_done, sq_done, ss_done, rt_done, rs_done, n_done, hi_done, lo_done = (
            sem(x) for x in ("h_done", "sq_done", "ss_done", "rt_done", "rs_done", "n_done", "hi_done", "lo_done"))
        block = ctx.enter_context(nc.Block())

        @block.sync
        def _(sp):
            clear_last(sp)
            for k in range(KT):
                sp.dma_start(h[:, k], d["xT"][:, k, 0:T]).then_inc(x_in, 16)
            for k in range(KT):
                if k >= 2:
                    sp.wait_ge(h_done, k - 1)
                sp.dma_start(zo[:, k % 2], d["zo"][k]).then_inc(z_in[k % 2], 16)

        @block.scalar
        def _(act):
            for k in range(KT):
                act.wait_ge(h_done, k + 1)
                if k >= 2:
                    act.wait_ge(ss_done, k - 1)
                act.activation(sq[:, k % 2], h[:, k], ACT.Square).then_inc(sq_done, 1)
            act.wait_ge(ss_done, KT)
            act.activation(rstd[:].rearrange("p (c n) -> p c n", c=NCH), ss[:, :, 0:CW], ACT.Sqrt,
                           bias=per["eps"][:, 0:1], scale=1.0 / D).then_inc(rt_done, 1)
            for k in range(KT):
                act.wait_ge(n_done, k + 1)
                act.activation(f_hi[:, k], sq[:, k % 2], ACT.Copy).then_inc(hi_done, 1)

        @block.tensor
        def _(pe):
            for k in range(KT):
                pe.wait_ge(sq_done, k + 1)
                for c in range(NCH):
                    mm = pe.matmul(ss[:, c, 0:CW], per["ones"][:], sq[:, k % 2, c * CW:(c + 1) * CW],
                                   start=(k == 0), stop=(k == KT - 1))
                mm.then_inc(ss_done, 1)

        @block.vector
        def _(dve):
            dve.wait_ge(x_in, 16 * KT)
            for k in range(KT):
                dve.wait_ge(z_in[k % 2], 16 * (k // 2 + 1))
                dve.tensor_tensor(h[:, k], h[:, k], zo[:, k % 2], ALU.add).then_inc(h_done, 1)
            dve.wait_ge(rt_done, 1)
            dve.reciprocal(rstd[:], rstd[:]).then_inc(rs_done, 1)
            dve.wait_ge(rs_done, 1)
            for k in range(KT):
                if k >= 2:
                    dve.wait_ge(lo_done, k - 1)
                dve.scalar_tensor_tensor(sq[:, k % 2], h[:, k], per["vec"][:, V_FFN + k:V_FFN + k + 1], rstd[:],
                                         ALU.mult, ALU.mult).then_inc(n_done, 1)

        @block.gpsimd
        def _(pool):
            for k in range(KT):
                pool.wait_ge(hi_done, k + 1)
                pool.tensor_tensor(f_lo[:, k], sq[:, k % 2], f_hi[:, k].bitcast(F32), ALU.subtract).then_inc(lo_done, 1)


def ffn(nc, d, h, f_hi, f_lo):
    NG = 20
    with ExitStack() as ctx:
        sb, ps, sem = sb_of(nc, ctx, "ffn"), ps_of(nc, ctx, "ffn"), sem_of(nc, ctx, "ffn")
        raw = sb("raw", [P, 2, KT, P])
        w_hi = sb("w_hi", [P, 2, KT, P], F32R)
        w_lo = sb("w_lo", [P, 2, KT, P], F32R)
        sg = sb("sg", [P, 2, T])
        a = sb("a", [P, 2, T])
        a_hi = sb("a_hi", [P, 2, T], F32R)
        a_lo = sb("a_lo", [P, 2, T], F32R)
        acc = [ps(f"acc{s}", [P, NCH, 512]) for s in range(2)]
        raw_in = [sem("raw_in0"), sem("raw_in1")]
        hi_done, lo_done, mm_done, ev_done, sg_done, ahi_done, alo_done, y_out = (
            sem(x) for x in ("hi_done", "lo_done", "mm_done", "ev_done", "sg_done", "ahi_done", "alo_done", "y_out"))
        block = ctx.enter_context(nc.Block())
        UNIT_FREE = (12, 20, NG + 1, NG + 2, NG + 3, NG + 4)

        @block.sync
        def _(sp):
            clear_last(sp)
            for s in range(2):
                sp.dma_start(raw[:, s], d["w_ff"][s]).then_inc(raw_in[s], 16)
            with sp.Fori(0, FFG) as i:
                for u in range(6):
                    nxt = sp.snap(i * 6 + (u + 2))
                    sp.wait_ge(lo_done, i * 6 + (u + 1))
                    sp.dma_start(raw[:, u % 2], d["w_ff"][bass.ds(nxt, 1)].rearrange("a p k n -> p (a k) n")).then_inc(raw_in[u % 2], 16)
            sp.wait_ge(ev_done, FFG * NG + 2)
            for k in range(KT):
                sp.dma_start(d["yT"][k], h[:, k]).then_inc(y_out, 16)
            sp.wait_ge(y_out, 16 * KT)
            for s in range(2):
                sp.wait_ge(raw_in[s], 16 * (3 * FFG + 1))

        @block.scalar
        def _(act):
            with act.Fori(0, FFG) as i:

                def w_part(u):
                    act.wait_ge(raw_in[u % 2], i * 48 + (16 * (u // 2) + 16))
                    act.wait_ge(mm_done, i * NG + UNIT_FREE[u])
                    act.activation(w_hi[:, u % 2], raw[:, u % 2], ACT.Copy).then_inc(hi_done, 1)

                def sigma(j):
                    act.wait_ge(mm_done, i * NG + (NG + 2 * j + 1))
                    act.activation(sg[:, j].rearrange("p (c n) -> p c n", c=NCH), acc[0][:, :, 0:CW], ACT.Sigmoid).then_inc(sg_done, 1)

                def a_part(j):
                    act.wait_ge(ev_done, i * NG + (2 * j + 4))
                    act.wait_ge(mm_done, i * NG + (12 + 8 * j))
                    act.activation(a_hi[:, j], a[:, j], ACT.Copy).then_inc(ahi_done, 1)

                w_part(0)
                w_part(1)
                sigma(0)
                w_part(2)
                a_part(0)
                w_part(3)
                sigma(1)
                w_part(4)
                a_part(1)
                w_part(5)

        @block.gpsimd
        def _(pool):
            with pool.Fori(0, FFG) as i:

                def w_part(u):
                    pool.wait_ge(hi_done, i * 6 + (u + 1))
                    pool.tensor_tensor(w_lo[:, u % 2], raw[:, u % 2], w_hi[:, u % 2].bitcast(F32), ALU.subtract).then_inc(lo_done, 1)

                def a_part(j):
                    pool.wait_ge(ahi_done, i * 2 + (j + 1))
                    pool.tensor_tensor(a_lo[:, j], a[:, j], a_hi[:, j].bitcast(F32), ALU.subtract).then_inc(alo_done, 1)

                w_part(0)
                w_part(1)
                w_part(2)
                a_part(0)
                w_part(3)
                w_part(4)
                a_part(1)
                w_part(5)

        @block.tensor
        def _(pe):
            pe.sem_inc(mm_done, NG)
            with pe.Fori(0, FFG) as i:
                for u in range(4):
                    pe.wait_ge(lo_done, i * 6 + (u + 1))
                    pe.wait_ge(ev_done, i * NG + (u + 1))
                    for k in range(KT):
                        for n, (w, x) in enumerate(((w_hi, f_hi), (w_hi, f_lo), (w_lo, f_hi))):
                            for c in range(NCH):
                                mm = pe.matmul(acc[u % 2][:, c, 0:CW], w[:, u % 2, k, :], x[:, k, c * CW:(c + 1) * CW],
                                               start=(k + n == 0), stop=(k == KT - 1 and n == 2))
                    mm.then_inc(mm_done, 1)
                for j in range(2):
                    pe.wait_ge(lo_done, i * 6 + (5 + j))
                    pe.wait_ge(alo_done, i * 2 + (j + 1))
                    for m in range(KT):
                        pe.wait_ge(ev_done, i * NG + (4 + 8 * j + m + 1))
                        for n, (w, x) in enumerate(((w_hi, a_hi), (w_hi, a_lo), (w_lo, a_hi))):
                            for c in range(NCH):
                                mm = pe.matmul(acc[m % 2][:, c, 0:CW], w[:, j, m, :], x[:, j, c * CW:(c + 1) * CW],
                                               start=(n == 0), stop=(n == 2))
                        mm.then_inc(mm_done, 1)

        @block.vector
        def _(dve):
            dve.sem_inc(ev_done, 2)
            with dve.Fori(0, FFG) as i:
                for j in range(2):
                    aj = a[:, j].rearrange("p (c n) -> p c n", c=NCH)
                    dve.wait_ge(sg_done, i * 2 + (j + 1))
                    dve.wait_ge(mm_done, i * NG + (12 + 8 * j))
                    dve.tensor_tensor(aj, acc[0][:, :, 0:CW], sg[:, j].rearrange("p (c n) -> p c n", c=NCH), ALU.mult).then_inc(ev_done, 1)
                    dve.wait_ge(ev_done, i * NG + (2 * j + 3))
                    dve.wait_ge(mm_done, i * NG + (NG + 2 * j + 2))
                    dve.tensor_tensor(aj, acc[1][:, :, 0:CW], aj, ALU.mult).then_inc(ev_done, 1)
                for g in range(16):
                    m = g % 8
                    dve.wait_ge(mm_done, i * NG + (NG + 5 + g))
                    hm = h[:, m].rearrange("p (c n) -> p c n", c=NCH)
                    dve.tensor_tensor(hm, acc[m % 2][:, :, 0:CW], hm, ALU.add).then_inc(ev_done, 1)


def outputs(nc, d):
    with ExitStack() as ctx:
        sem = sem_of(nc, ctx, "out")
        o = sem("o")
        block = ctx.enter_context(nc.Block())

        @block.sync
        def _(sp):
            clear_last(sp)
            for n, src in enumerate((d["z"][U_CMPK], d["z"][U_CMPV], d["zn"][0], d["z"][U_SELV], d["zn"][1], d["z"][U_WINV])):
                sp.dma_start(d["kvT"][n], src).then_inc(o, 16)
            for h in range(MH):
                sp.dma_start(d["memT"][h], d["memn"][h]).then_inc(o, 16)
                sp.dma_start(d["memT"][MH + h], d["memz"][MH + h]).then_inc(o, 16)
            for b in range(NS):
                sp.dma_start(d["win_out"][b, 0:WIN - 1], d["win_in"][b, 1:WIN]).then_inc(o, 16)
            for j, src in enumerate((d["zn"][1], d["z"][U_WINV])):
                sp.dma_start(d["win_out"][:, WIN - 1, j * P:(j + 1) * P].rearrange("b p -> p b"), src[:, NP_:T],
                             allow_slow_non_contiguous=True).then_inc(o, 16)
            sp.wait_ge(o, 16 * 24)


def program(nc, d):
    PHASE_SEMS["last"], PHASE_SEMS["now"] = [], []
    scratch = lambda name, shape: nc.dram_tensor(name, shape, F32, kind="Internal").ap()
    d["z"] = scratch("z", [NU_IN, P, T])
    d["zn"] = scratch("zn", [NHN, P, T])
    d["memz"] = scratch("memz", [2 * MH, P, NMEM])
    d["memn"] = scratch("memn", [MH, P, NMEM])
    d["gate_s"] = scratch("gate_s", [NS * 24, 1])
    d["vtok"] = scratch("vtok", [2, QT, P, P])
    d["memv"] = scratch("memv", [MH, 2, P, P])
    d["o_lru"] = scratch("o_lru", [KT, P, T])
    d["o_nsa"] = scratch("o_nsa", [R, P, T])
    d["o_mem"] = scratch("o_mem", [MH, P, T])
    d["zm"] = scratch("zm", [KT, P, T])
    d["zo"] = scratch("zo", [KT, P, T])
    d["dist"] = scratch("dist", [P, 8, RLEN])
    d["kcT"] = scratch("kcT", [P, (NS + 1) * NCK])
    d["vc"] = scratch("vc", [NCK, NS + 1, P])
    with ExitStack() as ctx:
        sb = sb_of(nc, ctx, "per")
        per = {"ident": sb("ident", [P, P]), "ones": sb("ones", [P, P]), "vec": sb("vec", [P, NV]), "eps": sb("eps", [P, 1]),
               "gate": sb("gate", [P, QT, 24])}
        with ExitStack() as part:
            sbh = sb_of(nc, part, "h")
            h_hi, h_lo = sbh("hi", [P, KT, XC], F32R), sbh("lo", [P, KT, XC], F32R)
            normalise(nc, d, per, h_hi, h_lo)
            project(nc, "pin", d["w_in"], U_LX, h_hi, h_lo, 0, NCH, CW, d["z"])
            project(nc, "pmem", d["w_mem"], 2 * MH, h_hi, h_lo, T, 1, NMEM, d["memz"])
            gates(nc, d, per, h_hi, h_lo)
            head_norm(nc, "hn", d, d["z"], U_SELK, NHN, T, NCH, d["mats"], d["gains"], d["zn"])
            head_norm(nc, "hm", d, d["memz"], 0, MH, NMEM, 1, d["mats_m"], d["gains_m"], d["memn"])
            to_tokens(nc, "tv", per, d["z"], U_SELV, 2, NP_, d["vtok"])
            to_tokens(nc, "tm", per, d["memz"], MH, MH, NMEM, d["memv"])
            outputs(nc, d)
            distance_bias(nc, d)
            compress(nc, d, per)
            prompt_attention(nc, d, per, h_hi, h_lo)
            project(nc, "pmg", d["w_in"][U_MG:NU_IN], NU_IN - U_MG, h_hi, h_lo, 0, NCH, CW, d["z"][U_MG:NU_IN])
        recurrence(nc, d, per)
        memory_attention(nc, d, per)
        sample_attention(nc, d, per)
        sample_memory(nc, d, per)
        with ExitStack() as part:
            sbx = sb_of(nc, part, "x")
            x_hi, x_lo = sbx("hi", [P, 16, T], F32R), sbx("lo", [P, 16, T], F32R)
            load_split(nc, "lsx", [d["o_lru"][k] for k in range(8)] + [d["o_nsa"][k] for k in range(4)]
                       + [d["o_mem"][k] for k in range(4)], x_hi, x_lo, T)
            merge(nc, d, x_hi, x_lo)
        with ExitStack() as part:
            sbx = sb_of(nc, part, "m")
            x_hi, x_lo = sbx("hi", [P, KT, T], F32R), sbx("lo", [P, KT, T], F32R)
            load_split(nc, "lsm", [d["zm"][k] for k in range(8)], x_hi, x_lo, T)
            project(nc, "pwo", d["w_o"], KT, x_hi, x_lo, 0, NCH, CW, d["zo"])
        with ExitStack() as part:
            sbx = sb_of(nc, part, "f")
            h = sbx("h", [P, KT, T])
            f_hi, f_lo = sbx("hi", [P, KT, T], F32R), sbx("lo", [P, KT, T], F32R)
            residual_norm(nc, d, per, h, f_hi, f_lo)
            ffn(nc, d, h, f_hi, f_lo)



def _bucket(n):
    if n < 16:
        return n
    return min(31, 16 + int(math.log(n / 16) / math.log(8) * 16 + 1e-9))


def _constants():
    f = np.float32
    hot = np.zeros((33, RLEN), f)
    for i in range(RLEN):
        dist = RMAX - i
        if dist < 0:
            hot[32, i] = NEGV
        else:
            hot[_bucket(dist), i] += 1
            hot[31, i] -= 1
    blk64 = np.kron(np.eye(2, dtype=f), np.ones((HD, HD), f))
    one = np.ones((P, P), f)

    def mat(m, eps):
        return np.concatenate([m, np.full((P, 1), eps, f)], 1)

    qi, xi, ui = np.arange(P)[:, None], np.arange(P)[None, :], np.arange(CU)[None, :]
    return {
        "ident": np.eye(P, dtype=f), "ones": one, "hot": hot,
        "mats": np.stack([mat(blk64 / 64, EPS)] * 2 + [mat(blk64, 64 * EPS)] * 4 + [mat(one / 128, EPS)] * 4),
        "mats_m": np.stack([mat(one / 128, EPS)] * 4),
        "avg": mat(blk64 / 64, EPS),
        "wmask": np.where(xi > qi, 0, NEGV).astype(f),
        "cmask": (qi >= 16 * (ui - 56) + 31).astype(f),
        "grp": np.kron(np.eye(16, dtype=f), np.ones((4, 4), f)),
        "blk": np.tile(np.arange(1, 17, dtype=f), (64, 1)),
    }


def _layout(x):
    x = {k: np.asarray(v) for k, v in x.items()}
    c = _constants()

    def fm(a):
        return a.T.reshape(-1, P, a.shape[0]).transpose(1, 0, 2)

    def units(w, cols=None):
        w = w if cols is None else w[:, cols]
        return w.reshape(-1, P, w.shape[1] // P, P).transpose(2, 1, 0, 3)

    def cols8(v):
        return v.reshape(-1, P).T

    w_in = x["w_in"][0]
    starts = [2560, 2688, 2944, 3200, 2816, 3072]
    cols = [np.arange(s, s + P) for s in starts]
    cols += [np.concatenate([2048 + r * HD + np.arange(HD), 2048 + (R + r) * HD + np.arange(HD)]) for r in range(R)]
    cols += [np.arange(3352 + P * h, 3352 + P * (h + 1)) for h in range(MH)]
    cols += [np.arange(P * m, P * (m + 1)) for m in range(16)]
    cols += [np.arange(3864 + P * m, 3864 + P * (m + 1)) for m in range(24)]
    order = np.concatenate([np.concatenate([r * HD + np.arange(HD), (R + r) * HD + np.arange(HD)]) for r in range(R)])
    ua, ub, um = units(x["w_up_a"][0]), units(x["w_up_b"][0][order]), units(x["w_up_m"][0])
    ubm = np.concatenate([ub, um], 2)
    zero = np.zeros((2, P, KT, P), np.float32)
    w_up = np.concatenate([np.stack([ua, ubm], 1).reshape(16, P, KT, P), zero])
    gu = np.stack([units(x["w_ffn_gate"][0]), units(x["w_ffn_up"][0])], 1).reshape(FFG, 4, P, KT, P)
    dn = x["w_ffn_down"][0].reshape(FFG, 2, P, KT, P)
    w_ff = np.concatenate([np.concatenate([gu, dn], 1).reshape(6 * FFG, P, KT, P), zero])
    dup = lambda g: np.concatenate([g, g])[:, None]
    gk = x["g_nsa_k"][0]
    gq, gm = dup(x["g_nsa_q"][0]), x["g_mem_q"][0][:, None]
    pool = x["cache_cmp_kv"][0]
    npool = pool.shape[0]
    sel = x["cache_sel_kv"][0].reshape(npool, P, 2, P)
    win = x["cache_win_kv"][0]
    wk = win.reshape(NS, WIN, 2, P)
    mem = x["cache_mem_kv"][0]
    out = {
        "xT": np.concatenate([fm(x["x_prompt"][0]), fm(x["x_sample"][:, 0]), fm(x["mem_prompt"][0])], 2),
        "vec": np.concatenate([cols8(x["norm_mix"][0]), cols8(x["norm_mem"][0]), cols8(x["norm_ffn"][0]),
                               x["g_mem_k"][0][:, None], cols8(x["pe_cmp_k"][0]), cols8(x["pe_cmp_v"][0])], 1),
        "w_in": units(w_in, np.concatenate(cols)), "w_mem": units(x["w_mem_kv"][0]),
        "w_ng": w_in[:, 3328:3352].reshape(KT, P, 24).transpose(1, 0, 2),
        "gains": np.stack([dup(gk[1]), dup(gk[2])] + [gq] * 4 + [gm] * 4),
        "gains_m": np.stack([x["g_mem_k"][0][:, None]] * 4),
        "nm_kc": np.concatenate([c.pop("avg"), dup(gk[0])], 1),
        "rel": np.concatenate([np.repeat(x["rel_bias"][:, :, None], P, 2), np.ones((1, 8, P), np.float32)]),
        "st": np.concatenate([x["state_conv"][0].transpose(2, 1, 0).reshape(KT, P, 3 * NS).transpose(1, 0, 2),
                              fm(x["state_lru_h"][0])], 2),
        "par": np.stack([cols8(v) for v in (*x["conv_w"][0], x["conv_b"][0], x["b_lru_a"][0], x["b_lru_i"][0],
                                            x["lru_lambda"][0])], 2),
        "w_a": x["w_lru_a"][0].reshape(4, 2, P, 256).transpose(0, 2, 1, 3),
        "w_i": x["w_lru_i"][0].reshape(4, 2, P, 256).transpose(0, 2, 1, 3),
        "w_c1": np.stack([x["w_cmp_k1"][0], x["w_cmp_v1"][0]]).reshape(2, 16, P, P).transpose(0, 2, 1, 3),
        "w_c2": np.stack([x["w_cmp_k2"][0], x["w_cmp_v2"][0]]),
        "cmp_pool": pool.reshape(npool, 8, 8, 2, 2, 2, HD).transpose(0, 3, 6, 4, 5, 2, 1).reshape(npool, P, 256),
        "sel_kT": sel[:, :, 0].transpose(0, 2, 1), "sel_v": sel[:, :, 1],
        "winkT": wk[:, :, 0].transpose(0, 2, 1), "win_v": wk[:, :, 1].reshape(NS, WIN // P, P, P),
        "win_in": win.reshape(NS, WIN, 256),
        "mem_kT": mem[:, :, 0].transpose(0, 3, 2, 1), "mem_v": mem[:, :, 1].reshape(NS, 2, P, MH, P),
        "page_table": x["page_table"].reshape(1, NS * PAGES),
        "w_up": w_up, "w_o": units(x["w_o"][0]), "w_ff": w_ff,
    }
    out.update(c)
    return {k: np.ascontiguousarray(v) for k, v in out.items()}


_OUTS = {"yT": (KT, P, T), "kvT": (6, P, T), "memT": (2 * MH, P, NMEM), "win_out": (NS, WIN, 256),
         "hT": (KT, P, 1 + NS), "cvT": (KT, P, 3), "cvsT": (KT, P, 3 * NS)}


def kernel(**inputs):
    import concourse.bacc as _bacc
    from concourse.bass_utils import run_bass_kernel_spmd as _run

    nc = _bacc.Bacc("TRN2", target_bir_lowering=False, num_devices=1)
    arrays, d = {}, {}
    for name, a in _layout(inputs).items():
        arrays[f"in_{name}"] = a
        d[name] = nc.dram_tensor(f"in_{name}", a.shape, mybir.dt.from_np(a.dtype), kind="ExternalInput").ap()
    for name, shape in _OUTS.items():
        d[name] = nc.dram_tensor(f"out_{name}", shape, F32, kind="ExternalOutput").ap()
    program(nc, d)
    r = _run(nc, [arrays], core_ids=[0]).results[0]
    got = {name: np.asarray(r[f"out_{name}"]) for name in _OUTS}

    y = got["yT"].reshape(D, T).T
    kv = got["kvT"].reshape(3, 2, P, T).transpose(0, 3, 1, 2).reshape(3, T, 2, G, HD)
    mem = got["memT"].reshape(2, MH, P, NMEM).transpose(3, 0, 1, 2)
    h = got["hT"].reshape(D, 1 + NS).T
    cv = got["cvT"].reshape(D, 3).T
    cvs = got["cvsT"].reshape(D, 3, NS).transpose(2, 1, 0)
    res = (y[None, :NP_], y[NP_:, None], kv[0][None, None, :NP_], kv[0][None, NP_:, None],
           kv[1][None, None, :NP_], kv[1][None, NP_:, None], kv[2][None, None, NP_ - WIN:NP_],
           got["win_out"].reshape(1, NS, WIN, 2, G, HD), mem[None, None], h[None, 0:1], h[None, 1:], cv[None, None], cvs[None])
    return tuple(np.ascontiguousarray(a) for a in res)
```

```python
from contextlib import ExitStack
import math

import numpy as np
import concourse.bass as bass
from concourse import mybir

F32 = mybir.dt.float32
F32R = mybir.dt.float32r
I32 = mybir.dt.int32
ACT = mybir.ActivationFunctionType
ALU = mybir.AluOpType
AX = mybir.AxisListType.X

P = 128
D = 1024
KT = D // P
NP_ = 1024
NS = 8
T = NP_ + NS
NCH, CW = 3, T // 3
NMEM = 256
XC = T + NMEM
G, R, HD = 2, 4, 64
MH = 4
QT = NP_ // P
PAGES = 8
NCMP = 63
NCK = 64
WIN = 512
FFG = 11
EPS = 1e-6
NEGV = -1e30
RLEN, RMAX = 512, 360
CU = 120

U_CMPK, U_CMPV, U_SELV, U_WINV, U_SELK, U_WINK, U_Q, U_MQ, U_LX, U_LG, U_MG = 0, 1, 2, 3, 4, 5, 6, 10, 14, 22, 30
NU_IN = 54
NHN = 10
V_MIX, V_MEM, V_FFN, V_GMK, V_PEK, V_PEV, NV = 0, 8, 16, 24, 25, 41, 57
L_CW, L_CB, L_BA, L_BI, L_LAM, NL = 0, 4, 5, 6, 7, 8


def sb_of(nc, ctx, tag):
    return lambda name, shape, dt=F32: ctx.enter_context(nc.sbuf_tensor(f"{tag}_{name}", shape, dt))


def ps_of(nc, ctx, tag):
    return lambda name, shape: ctx.enter_context(nc.psum_tensor(f"{tag}_{name}", shape, F32))


PHASE_SEMS = {"last": [], "now": []}


def sem_of(nc, ctx, tag):
    PHASE_SEMS["last"], PHASE_SEMS["now"] = PHASE_SEMS["now"], []

    def sem(name):
        s = ctx.enter_context(nc.semaphore(f"{tag}_{name}"))
        PHASE_SEMS["now"].append(s)
        return s

    return sem


def clear_last(sp):
    for s in PHASE_SEMS["last"]:
        sp.sem_clear(s)


def normalise(nc, d, per, h_hi, h_lo):
    with ExitStack() as ctx:
        sb, ps, sem = sb_of(nc, ctx, "nrm"), ps_of(nc, ctx, "nrm"), sem_of(nc, ctx, "nrm")
        x = sb("x", [P, KT, XC])
        sq = sb("sq", [P, 2, XC])
        rstd = sb("rstd", [P, XC])
        nrm = sb("nrm", [P, 2, XC])
        ss = ps("ss", [P, 4, 512])
        w = XC // 4
        x_in, c_in, sq_done, ss_done = sem("x_in"), sem("c_in"), sem("sq_done"), sem("ss_done")
        sum_done, rt_done, rs_done, n_done, hi_done, lo_done = (sem("sum_done"), sem("rt_done"), sem("rs_done"), sem("n_done"),
                                                      sem("hi_done"), sem("lo_done"))
        eps_done = sem("eps_done")
        block = ctx.enter_context(nc.Block())

        @block.sync
        def _(sp):
            clear_last(sp)
            sp.dma_start(per["ones"][:], d["ones"]).then_inc(c_in, 16)
            sp.dma_start(per["vec"][:], d["vec"]).then_inc(c_in, 16)
            for k in range(KT):
                sp.dma_start(x[:, k, :], d["xT"][:, k, :]).then_inc(x_in, 16)
            sp.dma_start(per["ident"][:], d["ident"]).then_inc(c_in, 16)
            sp.wait_ge(c_in, 48)

        @block.scalar
        def _(act):
            act.wait_ge(x_in, 16 * KT)
            for k in range(KT):
                if k >= 2:
                    act.wait_ge(ss_done, k - 1)
                act.activation(sq[:, k % 2, :], x[:, k, :], ACT.Square).then_inc(sq_done, 1)
            act.wait_ge(ss_done, KT)
            act.wait_ge(eps_done, 1)
            act.activation(rstd[:].rearrange("p (c n) -> p c n", c=4), ss[:, :, 0:w], ACT.Sqrt,
                           bias=per["eps"][:, 0:1], scale=1.0 / D).then_inc(rt_done, 1)
            for k in range(KT):
                act.wait_ge(n_done, 2 * k + 2)
                act.activation(h_hi[:, k, :], nrm[:, k % 2, :], ACT.Copy).then_inc(hi_done, 1)

        @block.tensor
        def _(pe):
            pe.wait_ge(c_in, 32)
            for k in range(KT):
                pe.wait_ge(sq_done, k + 1)
                for c in range(4):
                    mm = pe.matmul(ss[:, c, 0:w], per["ones"][:], sq[:, k % 2, c * w:c * w + w],
                                   start=(k == 0), stop=(k == KT - 1))
                mm.then_inc(ss_done, 1)

        @block.vector
        def _(dve):
            dve.memset(per["eps"][:], EPS).then_inc(eps_done, 1)
            dve.wait_ge(rt_done, 1)
            dve.reciprocal(rstd[:], rstd[:]).then_inc(rs_done, 1)
            dve.wait_ge(rs_done, 1)
            dve.wait_ge(c_in, 32)
            dve.wait_ge(x_in, 16 * KT)
            for k in range(KT):
                if k >= 2:
                    dve.wait_ge(lo_done, k - 1)
                dve.scalar_tensor_tensor(nrm[:, k % 2, 0:T], x[:, k, 0:T], per["vec"][:, V_MIX + k:V_MIX + k + 1],
                                         rstd[:, 0:T], ALU.mult, ALU.mult).then_inc(n_done, 1)
                dve.scalar_tensor_tensor(nrm[:, k % 2, T:XC], x[:, k, T:XC], per["vec"][:, V_MEM + k:V_MEM + k + 1],
                                         rstd[:, T:XC], ALU.mult, ALU.mult).then_inc(n_done, 1)

        @block.gpsimd
        def _(pool):
            for k in range(KT):
                pool.wait_ge(hi_done, k + 1)
                pool.tensor_tensor(h_lo[:, k, :], nrm[:, k % 2, :], h_hi[:, k, :].bitcast(F32),
                                   ALU.subtract).then_inc(lo_done, 1)


def project(nc, tag, units, n_units, h_hi, h_lo, col, chunks, cw, out):
    cols = chunks * cw
    with ExitStack() as ctx:
        sb, ps, sem = sb_of(nc, ctx, tag), ps_of(nc, ctx, tag), sem_of(nc, ctx, tag)
        raw = sb("raw", [P, 2, KT, P])
        w_hi = sb("w_hi", [P, 2, KT, P], F32R)
        w_lo = sb("w_lo", [P, 2, KT, P], F32R)
        z = sb("z", [P, 2, cols])
        acc = [ps(f"acc{s}", [P, chunks, 512]) for s in range(2)]
        raw_in = [sem("raw_in0"), sem("raw_in1")]
        z_out = [sem("z_out0"), sem("z_out1")]
        hi_done, lo_done, mm_done, ev_done = sem("hi_done"), sem("lo_done"), sem("mm_done"), sem("ev_done")
        block = ctx.enter_context(nc.Block())
        pairs = n_units // 2

        @block.sync
        def _(sp):
            clear_last(sp)
            sp.sem_inc(z_out[0], 16)
            sp.sem_inc(z_out[1], 16)
            for s in range(2):
                sp.dma_start(raw[:, s], units[s]).then_inc(raw_in[s], 16)

            def store(s, row, n):
                sp.wait_ge(ev_done, n + 2)
                sp.dma_start(out[row], z[:, s]).then_inc(z_out[s], 16)

            with sp.Fori(0, pairs - 1) as i:
                for s in range(2):
                    nxt = sp.snap(i * 2 + (s + 2))
                    cur = sp.snap(i * 2 + s)
                    sp.wait_ge(lo_done, i * 2 + (s + 1))
                    sp.dma_start(raw[:, s], units[bass.ds(nxt, 1)].rearrange("a p k m -> p (a k) m")).then_inc(raw_in[s], 16)
                    sp.wait_ge(ev_done, i * 2 + (s + 3))
                    sp.dma_start(out[bass.ds(cur, 1)].rearrange("a p n -> p (a n)"), z[:, s]).then_inc(z_out[s], 16)
            for s in range(2):
                store(s, n_units - 2 + s, n_units - 1 + s)
            for s in range(2):
                sp.wait_ge(z_out[s], 16 * (pairs + 1))

        @block.scalar
        def _(act):
            with act.Fori(0, pairs) as i:
                for s in range(2):
                    act.wait_ge(raw_in[s], i * 16 + 16)
                    act.wait_ge(mm_done, i * 2 + (s + 1))
                    act.activation(w_hi[:, s], raw[:, s], ACT.Copy).then_inc(hi_done, 1)

        @block.gpsimd
        def _(pool):
            with pool.Fori(0, pairs) as i:
                for s in range(2):
                    pool.wait_ge(hi_done, i * 2 + (s + 1))
                    pool.tensor_tensor(w_lo[:, s], raw[:, s], w_hi[:, s].bitcast(F32), ALU.subtract).then_inc(lo_done, 1)

        @block.tensor
        def _(pe):
            pe.sem_inc(mm_done, 2)
            with pe.Fori(0, pairs) as i:
                for s in range(2):
                    pe.wait_ge(lo_done, i * 2 + (s + 1))
                    pe.wait_ge(ev_done, i * 2 + (s + 1))
                    for k in range(KT):
                        for n, (w, h) in enumerate(((w_hi, h_hi), (w_hi, h_lo), (w_lo, h_hi))):
                            for c in range(chunks):
                                mm = pe.matmul(acc[s][:, c, 0:cw], w[:, s, k, :],
                                               h[:, k, col + c * cw:col + (c + 1) * cw],
                                               start=(k + n == 0), stop=(k == KT - 1 and n == 2))
                    mm.then_inc(mm_done, 1)

        @block.vector
        def _(dve):
            dve.sem_inc(ev_done, 2)
            with dve.Fori(0, pairs) as i:
                for s in range(2):
                    dve.wait_ge(z_out[s], i * 16 + 16)
                    dve.wait_ge(mm_done, i * 2 + (s + 3))
                    dve.tensor_copy(z[:, s].rearrange("p (c n) -> p c n", c=chunks), acc[s][:, :, 0:cw]).then_inc(ev_done, 1)


def gates(nc, d, per, h_hi, h_lo):
    with ExitStack() as ctx:
        sb, ps, sem = sb_of(nc, ctx, "gat"), ps_of(nc, ctx, "gat"), sem_of(nc, ctx, "gat")
        raw = sb("raw", [P, KT, 24])
        hi = sb("hi", [P, KT, 24], F32R)
        lo = sb("lo", [P, KT, 24], F32R)
        gs = sb("gs", [NS, 24])
        acc = ps("acc", [P, QT + 1, 32])
        w_in, hi_done, lo_done, mm_done, sig_done, g_out = (sem("w_in"), sem("hi_done"), sem("lo_done"), sem("mm_done"),
                                                      sem("sig_done"), sem("g_out"))
        block = ctx.enter_context(nc.Block())

        @block.sync
        def _(sp):
            clear_last(sp)
            sp.dma_start(raw[:], d["w_ng"]).then_inc(w_in, 16)
            sp.wait_ge(sig_done, 2)
            sp.dma_start(d["gate_s"].rearrange("(b n) c -> b (n c)", b=NS), gs[:]).then_inc(g_out, 16)
            sp.wait_ge(g_out, 16)

        @block.vector
        def _(dve):
            dve.wait_ge(w_in, 16)
            dve.tensor_copy(hi[:], raw[:]).then_inc(hi_done, 1)
            dve.wait_ge(hi_done, 1)
            dve.tensor_tensor(lo[:], raw[:], hi[:].bitcast(F32), ALU.subtract).then_inc(lo_done, 1)

        @block.tensor
        def _(pe):
            pe.wait_ge(lo_done, 1)
            for t in range(QT + 1):
                m = P if t < QT else NS
                for k in range(KT):
                    for n, (h, w) in enumerate(((h_hi, hi), (h_lo, hi), (h_hi, lo))):
                        mm = pe.matmul(acc[0:m, t, 0:24], h[:, k, t * P:t * P + m], w[:, k, :],
                                       start=(k + n == 0), stop=(k == KT - 1 and n == 2))
            mm.then_inc(mm_done, 1)

        @block.scalar
        def _(act):
            act.wait_ge(mm_done, 1)
            act.activation(per["gate"][:], acc[:, 0:QT, 0:24], ACT.Sigmoid).then_inc(sig_done, 1)
            act.activation(gs[:], acc[0:NS, QT, 0:24], ACT.Sigmoid).then_inc(sig_done, 1)


def head_norm(nc, tag, d, src, row0, n, cols, chunks, mats, gains, dst):
    cw = cols // chunks
    with ExitStack() as ctx:
        sb, ps, sem = sb_of(nc, ctx, tag), ps_of(nc, ctx, tag), sem_of(nc, ctx, tag)
        z = sb("z", [P, 2, cols])
        m = sb("m", [P, 2, P + 1])
        g = sb("g", [P, 2, 1])
        sq = sb("sq", [P, 2, cols])
        o = sb("o", [P, 2, cols])
        ms = [ps(f"ms{s}", [P, chunks, 512]) for s in range(2)]
        t_in = [sem("t_in0"), sem("t_in1")]
        t_out = [sem("t_out0"), sem("t_out1")]
        sq_done, mm_done, rt_done, rc_done, n_done = sem("sq_done"), sem("mm_done"), sem("rt_done"), sem("rc_done"), sem("n_done")
        block = ctx.enter_context(nc.Block())

        @block.sync
        def _(sp):
            clear_last(sp)
            sp.sem_inc(t_out[0], 16)
            sp.sem_inc(t_out[1], 16)
            def load(j, jr, s):
                sp.dma_start(z[:, s], src[bass.ds(jr, 1)].rearrange("a p n -> p (a n)")).then_inc(t_in[s], 16)
                sp.dma_start(m[:, s], mats[bass.ds(j, 1)].rearrange("a p n -> p (a n)")).then_inc(t_in[s], 16)
                sp.dma_start(g[:, s], gains[bass.ds(j, 1)].rearrange("a p n -> p (a n)")).then_inc(t_in[s], 16)

            for s in range(2):
                load(s, row0 + s, s)
            with sp.Fori(0, n // 2 - 1) as i:
                for s in range(2):
                    last, nxt, row = sp.snap(i * 2 + s), sp.snap(i * 2 + (s + 2)), sp.snap(i * 2 + (s + 2 + row0))
                    sp.wait_ge(n_done, i * 2 + (s + 1))
                    sp.dma_start(dst[bass.ds(last, 1)].rearrange("a p n -> p (a n)"), o[:, s]).then_inc(t_out[s], 16)
                    load(nxt, row, s)
            for s in range(2):
                sp.wait_ge(n_done, n - 1 + s)
                sp.dma_start(dst[n - 2 + s], o[:, s]).then_inc(t_out[s], 16)
            for s in range(2):
                sp.wait_ge(t_out[s], 16 * (n // 2 + 1))

        @block.scalar
        def _(act):
            with act.Fori(0, n // 2) as i:
                for s in range(2):
                    act.wait_ge(t_in[s], i * 48 + 48)
                    act.activation(sq[:, s], z[:, s], ACT.Square).then_inc(sq_done, 1)
                    act.wait_ge(mm_done, i * 2 + (s + 1))
                    act.activation(sq[:, s].rearrange("p (c n) -> p c n", c=chunks), ms[s][:, :, 0:cw], ACT.Sqrt,
                                   bias=m[:, s, P:P + 1]).then_inc(rt_done, 1)

        @block.tensor
        def _(pe):
            with pe.Fori(0, n // 2) as i:
                for s in range(2):
                    pe.wait_ge(sq_done, i * 2 + (s + 1))
                    for c in range(chunks):
                        mm = pe.matmul(ms[s][:, c, 0:cw], m[:, s, 0:P], sq[:, s, c * cw:(c + 1) * cw], start=True, stop=True)
                    mm.then_inc(mm_done, 1)

        @block.vector
        def _(dve):
            with dve.Fori(0, n // 2) as i:
                for s in range(2):
                    dve.wait_ge(rt_done, i * 2 + (s + 1))
                    dve.reciprocal(sq[:, s], sq[:, s]).then_inc(rc_done, 1)
                    dve.wait_ge(t_out[s], i * 16 + 16)
                    dve.wait_ge(rc_done, i * 2 + (s + 1))
                    dve.scalar_tensor_tensor(o[:, s], z[:, s], g[:, s], sq[:, s], ALU.mult, ALU.mult).then_inc(n_done, 1)


def to_tokens(nc, tag, per, src, row0, n, cols, dst):
    nt = cols // P
    with ExitStack() as ctx:
        sb, ps, sem = sb_of(nc, ctx, tag), ps_of(nc, ctx, tag), sem_of(nc, ctx, tag)
        z = sb("z", [P, 2, cols])
        o = sb("o", [P, 2, cols])
        tp = [ps(f"tp{s}", [P, nt, P]) for s in range(2)]
        t_in = [sem("t_in0"), sem("t_in1")]
        t_out = [sem("t_out0"), sem("t_out1")]
        tp_done, ev_done = sem("tp_done"), sem("ev_done")
        block = ctx.enter_context(nc.Block())

        def store(sp, j):
            sp.wait_ge(ev_done, j + 1)
            sp.dma_start(dst[j].rearrange("t p n -> p t n"), o[:, j % 2].rearrange("p (t n) -> p t n", n=P)).then_inc(t_out[j % 2], 16)

        @block.sync
        def _(sp):
            clear_last(sp)
            for j in range(n):
                s = j % 2
                if j >= 2:
                    sp.wait_ge(tp_done, j - 1)
                sp.dma_start(z[:, s], src[row0 + j][:, 0:cols]).then_inc(t_in[s], 16)
                if j >= 1:
                    store(sp, j - 1)
            store(sp, n - 1)
            for s in range(2):
                sp.wait_ge(t_out[s], 16 * ((n - s + 1) // 2))

        @block.tensor
        def _(pe):
            for j in range(n):
                s = j % 2
                pe.wait_ge(t_in[s], 16 * (j // 2 + 1))
                if j >= 2:
                    pe.wait_ge(ev_done, j - 1)
                for t in range(nt):
                    mm = pe.transpose(tp[s][:, t, :], z[:, s, t * P:(t + 1) * P], per["ident"][:])
                mm.then_inc(tp_done, 1)

        @block.vector
        def _(dve):
            for j in range(n):
                s = j % 2
                dve.wait_ge(tp_done, j + 1)
                if j >= 2:
                    dve.wait_ge(t_out[s], 16 * (j // 2))
                dve.tensor_copy(o[:, s].rearrange("p (t n) -> p t n", n=P), tp[s][:]).then_inc(ev_done, 1)


def merge_gates_and_recurrence(nc, d, h_hi, h_lo):
    CWD = 4
    NBLK = 4
    NU = (NU_IN - U_MG) // NBLK
    with ExitStack() as ctx:
        sb, ps, sem = sb_of(nc, ctx, "lru"), ps_of(nc, ctx, "lru"), sem_of(nc, ctx, "lru")
        raw = sb("raw", [P, 2, KT, P])
        w_hi = sb("w_hi", [P, 2, KT, P], F32R)
        w_lo = sb("w_lo", [P, 2, KT, P], F32R)
        z = sb("z", [P, 2, T])
        acc = [ps(f"acc{s}", [P, NCH, 512]) for s in range(2)]
        raw_in = [sem("raw_in0"), sem("raw_in1")]
        z_out = [sem("z_out0"), sem("z_out1")]
        hi_done, lo_done, mm_done, ev_done = sem("hi_done"), sem("lo_done"), sem("mm_done"), sem("ev_done")

        xp = sb("xp", [P, 2, CWD - 1 + T])
        st = sb("st", [P, 2, 4 * NS])
        par = sb("par", [P, 2, NL])
        wa = sb("wa", [P, 2, 256])
        wi = sb("wi", [P, 2, 256])
        gate = sb("gate", [P, 2, T])
        xc = sb("xc", [P, 2, T])
        r = sb("r", [P, 2, T])
        ig = sb("ig", [P, 2, T])
        a = sb("a", [P, 2, T])
        th = sb("th", [P, 2, T])
        h = sb("h", [P, 2, T])
        lam = sb("lam", [P, 8, 2])
        ps_r = ps("ps_r", [P, 512])
        ps_i = ps("ps_i", [P, 512])
        b_in, b_out, pad_done, ch, xc_done, gm_done, sig_done, lam_done, ex_done, act_done, sq_in, rt_done, o_done = (
            sem(x) for x in ("b_in", "b_out", "pad_done", "ch", "xc_done", "gm_done", "sig_done", "lam_done", "ex_done",
                             "act_done", "sq_in", "rt_done", "o_done"))
        block = ctx.enter_context(nc.Block())

        @block.sync
        def _(sp):
            clear_last(sp)
            sp.sem_inc(b_out, 80)
            sp.sem_inc(z_out[0], 16)
            sp.sem_inc(z_out[1], 16)
            for s in range(2):
                sp.dma_start(raw[:, s], d["w_in"][U_MG + s]).then_inc(raw_in[s], 16)
            with sp.Fori(0, NBLK) as n:
                t2 = sp.snap(n * 2)
                for u in range(NU):
                    nxt, cur = sp.snap(n * NU + (U_MG + u + 2)), sp.snap(n * NU + (U_MG + u))
                    sp.wait_ge(lo_done, n * NU + (u + 1))
                    sp.dma_start(raw[:, u % 2], d["w_in"][bass.ds(nxt, 1)].rearrange("a p k m -> p (a k) m")).then_inc(raw_in[u % 2], 16)
                    if u == 4:
                        sp.wait_ge(o_done, n * 2 + 2)
                        sp.dma_start(d["o_lru"][bass.ds(t2, 2)].rearrange("a p n -> p a n"), r[:]).then_inc(b_out, 16)
                        sp.dma_start(d["hT"][bass.ds(t2, 2)].rearrange("a p n -> p a n"), h[:, :, NP_ - 1:T]).then_inc(b_out, 16)
                        sp.dma_start(d["cvT"][bass.ds(t2, 2)].rearrange("a p n -> p a n"), xp[:, :, NP_:NP_ + 3]).then_inc(b_out, 16)
                        sp.dma_start(d["cvsT"][bass.ds(t2, 2), :, 0:2 * NS].rearrange("a p n -> p a n"),
                                     st[:, :, NS:3 * NS]).then_inc(b_out, 16)
                        sp.dma_start(d["cvsT"][bass.ds(t2, 2), :, 2 * NS:].rearrange("a p n -> p a n"),
                                     xp[:, :, CWD - 1 + NP_:]).then_inc(b_out, 16)
                    sp.wait_ge(ev_done, n * NU + (u + 3))
                    sp.dma_start(d["z"][bass.ds(cur, 1)].rearrange("a p n -> p (a n)"), z[:, u % 2]).then_inc(z_out[u % 2], 16)
            sp.wait_ge(b_out, 80 * (NBLK + 1))
            for s in range(2):
                sp.wait_ge(z_out[s], 16 * (NBLK * NU // 2 + 1))
                sp.wait_ge(raw_in[s], 16 * (NBLK * NU // 2 + 1))

        @block.gpsimd
        def _(pool):
            with pool.Fori(0, NBLK * NU // 2) as i:
                for s in range(2):
                    pool.wait_ge(hi_done, i * 2 + (s + 1))
                    pool.tensor_tensor(w_lo[:, s], raw[:, s], w_hi[:, s].bitcast(F32), ALU.subtract).then_inc(lo_done, 1)

        @block.tensor
        def _(pe):
            pe.sem_inc(mm_done, 2)
            with pe.Fori(0, NBLK) as n:

                def gate_products(t, c):
                    if t == 0 and c == 0:
                        pe.wait_ge(xc_done, n * 4 + 4)
                    pe.wait_ge(sig_done, n * 12 + (2 * (NCH * t + c) + 2))
                    for w, o in ((wa, ps_r), (wi, ps_i)):
                        for k in range(2):
                            mm = pe.matmul(o[:, 0:CW], w[:, k, t * P:(t + 1) * P], xc[:, k, c * CW:(c + 1) * CW],
                                           start=(k == 0), stop=(k == 1))
                    mm.then_inc(gm_done, 1)

                for u in range(NU):
                    s = u % 2
                    pe.wait_ge(lo_done, n * NU + (u + 1))
                    pe.wait_ge(ev_done, n * NU + (u + 1))
                    for k in range(KT):
                        for p, (w, x) in enumerate(((w_hi, h_hi), (w_hi, h_lo), (w_lo, h_hi))):
                            for c in range(NCH):
                                mm = pe.matmul(acc[s][:, c, 0:CW], w[:, s, k, :], x[:, k, c * CW:(c + 1) * CW],
                                               start=(k + p == 0), stop=(k == KT - 1 and p == 2))
                        if u in (2, 3) and k in (1, 3, 5):
                            gate_products(u - 2, k // 2)
                    mm.then_inc(mm_done, 1)

        @block.scalar
        def _(act):
            with act.Fori(0, NBLK) as n:
                lx, lg = act.snap(n * 2 + U_LX), act.snap(n * 2 + U_LG)
                t2, blk = act.snap(n * 2), act.snap(n * 1)

                def w_part(u):
                    act.wait_ge(raw_in[u % 2], n * (8 * NU) + (16 * (u // 2) + 16))
                    act.wait_ge(mm_done, n * NU + (u + 1))
                    act.activation(w_hi[:, u % 2], raw[:, u % 2], ACT.Copy).then_inc(hi_done, 1)

                def sigmoids(t, c):
                    act.wait_ge(gm_done, n * 6 + (NCH * t + c + 1))
                    for o, v, b in ((ps_r, r, L_BA), (ps_i, ig, L_BI)):
                        act.activation(v[:, t, c * CW:(c + 1) * CW], o[:, 0:CW], ACT.Sigmoid,
                                       bias=par[:, t, b:b + 1]).then_inc(sig_done, 1)

                def decay(t):
                    act.wait_ge(sig_done, n * 12 + (6 * t + 8))
                    act.activation(th[:, t], r[:, t], ACT.Tanh, scale=lam[:, 7, t:t + 1])
                    act.activation(a[:, t], r[:, t], ACT.Exp, scale=lam[:, 6, t:t + 1]).then_inc(act_done, 1)

                def root(t):
                    act.wait_ge(sq_in, n * 2 + (t + 1))
                    act.activation(th[:, t], th[:, t], ACT.Sqrt).then_inc(rt_done, 1)

                w_part(0)
                act.wait_ge(b_out, n * 80 + 80)
                act.dma_start(par[:], d["par"][:, bass.ds(t2, 2), :]).then_inc(b_in, 16)
                act.dma_start(xp[:, :, CWD - 1:], d["z"][bass.ds(lx, 2)].rearrange("a p n -> p a n")).then_inc(b_in, 16)
                act.dma_start(st[:], d["st"][:, bass.ds(t2, 2), :]).then_inc(b_in, 16)
                act.dma_start(gate[:], d["z"][bass.ds(lg, 2)].rearrange("a p n -> p a n")).then_inc(b_in, 16)
                act.dma_start(wa[:], d["w_a"][bass.ds(blk, 1)].rearrange("a p k n -> p (a k) n")).then_inc(b_in, 16)
                act.dma_start(wi[:], d["w_i"][bass.ds(blk, 1)].rearrange("a p k n -> p (a k) n")).then_inc(b_in, 16)
                w_part(1)
                act.wait_ge(lam_done, n * 2 + 1)
                act.activation(lam[:, 3], lam[:, 1], ACT.Exp, scale=-1.0).then_inc(ex_done, 1)
                act.activation(gate[:], gate[:], ACT.Gelu_apprx_tanh)
                w_part(2)
                w_part(3)
                act.wait_ge(lam_done, n * 2 + 2)
                for c in range(NCH):
                    sigmoids(0, c)
                decay(0)
                w_part(4)
                sigmoids(1, 0)
                root(0)
                sigmoids(1, 1)
                sigmoids(1, 2)
                decay(1)
                w_part(5)
                root(1)

        @block.vector
        def _(dve):
            per_block = [0]

            def chain(ins, n):
                per_block[0] += 1
                ins.then_inc(ch, 1)
                dve.wait_ge(ch, n * CH + per_block[0])

            dve.sem_inc(ev_done, 2)
            dve.sem_inc(sig_done, 2)
            dve.memset(xp[:, :, 0:CWD - 1], 0.0).then_inc(pad_done, 1)
            dve.wait_ge(pad_done, 1)
            CH = 52
            with dve.Fori(0, NBLK) as n:

                def store(u):
                    s = u % 2
                    dve.wait_ge(z_out[s], n * (8 * NU) + (16 * (u // 2) + 16))
                    dve.wait_ge(mm_done, n * NU + (u + 3))
                    dve.tensor_copy(z[:, s].rearrange("p (c n) -> p c n", c=NCH), acc[s][:, :, 0:CW]).then_inc(ev_done, 1)

                def scan(t):
                    dve.wait_ge(xc_done, n * 4 + (2 * t + 2))
                    dve.wait_ge(act_done, n * 2 + (t + 1))
                    chain(dve.tensor_tensor(r[:, t], a[:, t], a[:, t], ALU.mult), n)
                    dve.scalar_tensor_tensor(th[:, t], r[:, t], 1.0, th[:, t], ALU.add, ALU.mult).then_inc(sq_in, 1)
                    chain(dve.tensor_tensor(ig[:, t], ig[:, t], xc[:, t], ALU.mult), n)
                    dve.wait_ge(rt_done, n * 2 + (t + 1))
                    chain(dve.tensor_tensor(ig[:, t], ig[:, t], th[:, t], ALU.mult), n)
                    chain(dve.tensor_tensor(h[:, t, NP_:T], a[:, t, NP_:T], st[:, t, 3 * NS:4 * NS], ALU.mult), n)
                    chain(dve.tensor_tensor(h[:, t, NP_:T], h[:, t, NP_:T], ig[:, t, NP_:T], ALU.add), n)
                    chain(dve.tensor_tensor_scan(h[:, t, 0:NP_], a[:, t, 0:NP_], ig[:, t, 0:NP_], 0.0, ALU.mult, ALU.add), n)
                    dve.tensor_tensor(r[:, t], h[:, t], gate[:, t], ALU.mult).then_inc(o_done, 1)

                dve.wait_ge(b_in, n * 96 + 96)
                L = par[:, :, L_LAM]
                chain(dve.tensor_scalar(lam[:, 0], L, -1.0, None, ALU.mult), n)
                chain(dve.tensor_tensor(lam[:, 1], L, lam[:, 0], ALU.max), n)
                dve.tensor_scalar(lam[:, 2], lam[:, 0], 0.0, None, ALU.max).then_inc(lam_done, 1)
                dve.wait_ge(ex_done, n + 1)
                chain(dve.tensor_scalar(lam[:, 4], lam[:, 3], 2.0, None, ALU.add), n)
                chain(dve.reciprocal(lam[:, 4], lam[:, 4]), n)
                chain(dve.tensor_tensor(lam[:, 4], lam[:, 3], lam[:, 4], ALU.mult), n)
                chain(dve.tensor_tensor(lam[:, 5], lam[:, 4], lam[:, 4], ALU.mult), n)
                chain(dve.memset(lam[:, 6], 1.0 / 19), n)
                for q in range(17, 0, -2):
                    chain(dve.tensor_tensor(lam[:, 6], lam[:, 6], lam[:, 5], ALU.mult), n)
                    chain(dve.tensor_scalar(lam[:, 6], lam[:, 6], 1.0 / q, None, ALU.add), n)
                chain(dve.tensor_tensor(lam[:, 6], lam[:, 6], lam[:, 4], ALU.mult), n)
                chain(dve.scalar_tensor_tensor(lam[:, 6], lam[:, 6], 2.0, lam[:, 2], ALU.mult, ALU.add), n)
                chain(dve.tensor_scalar(lam[:, 6], lam[:, 6], -8.0, None, ALU.mult), n)
                dve.tensor_scalar(lam[:, 7], lam[:, 6], -1.0, None, ALU.mult).then_inc(lam_done, 1)
                for t in range(2):
                    w = [par[:, t, L_CW + j:L_CW + j + 1] for j in range(CWD)]
                    chain(dve.tensor_scalar(xc[:, t, 0:NP_], xp[:, t, 0:NP_], w[0], par[:, t, L_CB:L_CB + 1],
                                            ALU.mult, ALU.add), n)
                    chain(dve.tensor_scalar(xc[:, t, NP_:T], st[:, t, 0:NS], w[0], par[:, t, L_CB:L_CB + 1],
                                            ALU.mult, ALU.add), n)
                    for j in range(1, CWD):
                        x_s = st[:, t, j * NS:(j + 1) * NS] if j < CWD - 1 else xp[:, t, CWD - 1 + NP_:]
                        p = dve.scalar_tensor_tensor(xc[:, t, 0:NP_], xp[:, t, j:j + NP_], w[j], xc[:, t, 0:NP_],
                                                     ALU.mult, ALU.add)
                        if j < CWD - 1:
                            chain(p, n)
                        else:
                            p.then_inc(xc_done, 1)
                        p = dve.scalar_tensor_tensor(xc[:, t, NP_:T], x_s, w[j], xc[:, t, NP_:T], ALU.mult, ALU.add)
                        if j < CWD - 1:
                            chain(p, n)
                        else:
                            p.then_inc(xc_done, 1)
                store(0)
                store(1)
                store(2)
                scan(0)
                store(3)
                scan(1)
                store(4)
                store(5)
                assert per_block[0] == CH, per_block[0]


def distance_bias(nc, d):
    with ExitStack() as ctx:
        sb, ps, sem = sb_of(nc, ctx, "dst"), ps_of(nc, ctx, "dst"), sem_of(nc, ctx, "dst")
        rel = sb("rel", [33, 8, P])
        hot = sb("hot", [33, RLEN])
        f = sb("f", [P, 8, RLEN])
        acc = ps("acc", [P, 8, RLEN])
        r_in, mm_done, ev_done, f_out = sem("r_in"), sem("mm_done"), sem("ev_done"), sem("f_out")
        block = ctx.enter_context(nc.Block())

        @block.sync
        def _(sp):
            clear_last(sp)
            sp.dma_start(rel[:], d["rel"]).then_inc(r_in, 16)
            sp.dma_start(hot[:], d["hot"]).then_inc(r_in, 16)
            sp.wait_ge(ev_done, 8)
            sp.dma_start(d["dist"].rearrange("p h n -> p (h n)"), f[:].rearrange("p h n -> p (h n)")).then_inc(f_out, 16)
            sp.wait_ge(f_out, 16)

        @block.tensor
        def _(pe):
            pe.wait_ge(r_in, 32)
            for h in range(8):
                pe.matmul(acc[:, h, :], rel[:, h, :], hot[:], start=True, stop=True).then_inc(mm_done, 1)

        @block.vector
        def _(dve):
            for h in range(8):
                dve.wait_ge(mm_done, h + 1)
                dve.tensor_copy(f[:, h, :], acc[:, h, :]).then_inc(ev_done, 1)


def compress(nc, d, per):
    SEQ = NS + 1
    with ExitStack() as ctx:
        sb, ps, sem = sb_of(nc, ctx, "cmp"), ps_of(nc, ctx, "cmp"), sem_of(nc, ctx, "cmp")
        pt = sb("pt", [1, NS * PAGES], I32)
        pool_x = sb("pool_x", [P, NS * PAGES, 256])
        zc = sb("zc", [P, 2, NP_])
        zr = sb("zr", [P, 2, 2, 8 * NCK])
        cp = sb("cp", [P, 2, 2, 8, NCK])
        w1 = sb("w1", [P, 2, 16, P])
        w2 = sb("w2", [P, 2, HD])
        pos = sb("pos", [P, 2])
        lo = sb("lo", [P, 2, SEQ, NCK])
        hd = sb("hd", [P, 2, SEQ, NCK])
        kc = sb("kc", [P, SEQ * NCK])
        sq = sb("sq", [P, SEQ * NCK])
        vc = sb("vc", [NCK, SEQ, P])
        nm = sb("nm", [P, P + 2])
        ps_lo = [ps(f"lo{s}", [P, NS, NCK]) for s in range(2)]
        ps_hi = [ps(f"hi{s}", [P, NS, NCK]) for s in range(2)]
        ps_pr = [ps(f"pr{s}", [P, 8, NCK]) for s in range(2)]
        ps_o = ps("o", [P, NS * NCK])
        ps_p = ps("p", [P, 8, NCK])
        pt_in, pg_in, zc_in, zr_done, cp_in, w_in, pos_mm, pos_done = (sem("pt_in"), [sem("pg_in0"), sem("pg_in1")], sem("zc_in"), sem("zr_done"),
                                                              sem("cp_in"), sem("w_in"), sem("pos_mm"), sem("pos_done"))
        mm_done, lo_ev, sum_done, act_done, o_mm, o_ev, z_done, c_out = (sem("mm_done"), sem("lo_ev"), sem("sum_done"),
                                                                 sem("act_done"), sem("o_mm"), sem("o_ev"), sem("z_done"),
                                                                 sem("c_out"))
        sq_done, ms_mm, rt_done, rc_done, kc_done = sem("sq_done"), sem("ms_mm"), sem("rt_done"), sem("rc_done"), sem("kc_done")
        block = ctx.enter_context(nc.Block())
        COMBOS = [(kv, g) for kv in range(2) for g in range(2)]

        def pages(eng, half):
            n = NS * PAGES // 2
            eng.wait_ge(pt_in, 16)
            with eng.Fori(half * n, (half + 1) * n) as i:
                page = eng.value_load(pt[0:1, bass.ds(i, 1)], min_val=0, max_val=d["cmp_pool"].shape[0] - 1)
                eng.dma_start(pool_x[:, bass.ds(i, 1), :].rearrange("p a n -> p (a n)"),
                              d["cmp_pool"][bass.ds(page, 1)].rearrange("a p n -> p (a n)")).then_inc(pg_in[half], 16)

        @block.gpsimd
        def _(pool):
            pages(pool, 1)

        @block.sync
        def _(sp):
            clear_last(sp)
            sp.dma_start(pt[:], d["page_table"]).then_inc(pt_in, 16)
            sp.dma_start(zc[:, 0, :], d["z"][U_CMPK][:, 0:NP_]).then_inc(zc_in, 16)
            sp.dma_start(zc[:, 1, :], d["z"][U_CMPV][:, 0:NP_]).then_inc(zc_in, 16)
            for kv in range(2):
                sp.dma_start(w1[:, kv], d["w_c1"][kv]).then_inc(w_in, 16)
                sp.dma_start(w2[:, kv], d["w_c2"][kv]).then_inc(w_in, 16)
            sp.dma_start(nm[:], d["nm_kc"]).then_inc(w_in, 16)
            pages(sp, 0)
            sp.wait_ge(zr_done, 2)
            for g in range(2):
                for s in range(2):
                    sp.dma_start(cp[s * HD:(s + 1) * HD, :, g].rearrange("p k a c -> p k (a c)"),
                                 zr[g * HD:(g + 1) * HD, :, s]).then_inc(cp_in, 16)
            sp.wait_ge(kc_done, 1)
            sp.dma_start(d["kcT"], kc[:]).then_inc(c_out, 16)
            sp.wait_ge(o_ev, 6)
            sp.dma_start(d["vc"], vc[:]).then_inc(c_out, 16)
            sp.wait_ge(c_out, 32)

        @block.vector
        def _(dve):
            dve.memset(hd[:], 0.0).then_inc(z_done, 1)
            dve.wait_ge(zc_in, 32)
            for kv in range(2):
                dve.tensor_copy(zr[:, kv].rearrange("p s (a c) -> p s a c", a=8),
                                zc[:, kv].rearrange("p (c a s) -> p s a c", a=8, s=2)).then_inc(zr_done, 1)
            dve.wait_ge(pos_mm, 1)
            dve.tensor_copy(pos[:], ps_p[:, 0, 0:2]).then_inc(pos_done, 1)
            dve.wait_ge(z_done, 1)
            for n, (kv, g) in enumerate(COMBOS):
                s = n % 2
                dve.wait_ge(lo_ev, 2 * n + 2)
                dve.tensor_tensor(hd[:, s, 0:NS, 0:NCMP], lo[:, s, 0:NS, 0:NCMP], ps_hi[s][:, :, 1:NCK], ALU.add).then_inc(sum_done, 1)
                dve.tensor_tensor(hd[:, s, NS, 0:NCMP], lo[:, s, NS, 0:NCMP], ps_pr[s][:, 1, 1:NCK], ALU.add).then_inc(sum_done, 1)
                if kv == 0:
                    if g == 1:
                        dve.wait_ge(o_mm, 2)
                        dve.tensor_copy(kc[:, 0:NS * NCK], ps_o[:]).then_inc(o_ev, 1)
                        dve.tensor_copy(kc[:, NS * NCK:], ps_p[:, 0, :]).then_inc(o_ev, 1)
                        dve.wait_ge(rt_done, 1)
                        dve.reciprocal(sq[:], sq[:]).then_inc(rc_done, 1)
                        dve.wait_ge(rc_done, 1)
                        dve.scalar_tensor_tensor(kc[:], kc[:], nm[:, P + 1:P + 2], sq[:], ALU.mult, ALU.mult).then_inc(kc_done, 1)
                else:
                    dve.wait_ge(o_mm, n + 1)
                    dve.tensor_copy(vc[:, 0:NS, g * HD:(g + 1) * HD], ps_o[0:NCK, :].rearrange("p (b n) -> p b n", b=NS)).then_inc(o_ev, 1)
                    dve.tensor_copy(vc[:, NS, g * HD:(g + 1) * HD], ps_p[0:NCK, 0, :]).then_inc(o_ev, 1)
                    if n == 3:
                        dve.wait_ge(o_ev, 6)

        @block.scalar
        def _(act):
            act.wait_ge(pos_done, 1)
            for n, (kv, g) in enumerate(COMBOS):
                s = n % 2
                act.wait_ge(mm_done, n + 1)
                if n >= 2:
                    act.wait_ge(sum_done, 2 * (n - 1))
                act.activation(lo[:, s, 0:NS], ps_lo[s][:], ACT.Identity, bias=pos[:, kv:kv + 1]).then_inc(lo_ev, 1)
                act.activation(lo[:, s, NS], ps_pr[s][:, 0], ACT.Identity, bias=pos[:, kv:kv + 1]).then_inc(lo_ev, 1)
                act.wait_ge(sum_done, 2 * n + 2)
                act.activation(hd[:, s, :, 0:NCMP], hd[:, s, :, 0:NCMP], ACT.Gelu_apprx_tanh).then_inc(act_done, 1)
                if n == 1:
                    act.wait_ge(o_ev, 2)
                    act.activation(sq[:], kc[:], ACT.Square).then_inc(sq_done, 1)
                    act.wait_ge(ms_mm, 1)
                    act.activation(sq[:, 0:NS * NCK], ps_o[:], ACT.Sqrt, bias=nm[:, P:P + 1])
                    act.activation(sq[:, NS * NCK:], ps_p[:, 0, :], ACT.Sqrt, bias=nm[:, P:P + 1]).then_inc(rt_done, 1)

        @block.tensor
        def _(pe):
            pe.wait_ge(w_in, 80)
            for kv, v0 in enumerate((V_PEK, V_PEV)):
                for i in range(16):
                    mm = pe.matmul(ps_p[:, 0, kv:kv + 1], w1[:, kv, i, :], per["vec"][:, v0 + i:v0 + i + 1],
                                   start=(i == 0), stop=(i == 15))
            mm.then_inc(pos_mm, 1)
            pe.wait_ge(pg_in[0], 16 * NS * PAGES // 2)
            pe.wait_ge(pg_in[1], 16 * NS * PAGES // 2)
            pe.wait_ge(cp_in, 64)

            def hidden(n):
                kv, g = COMBOS[n]
                s = n % 2
                if n >= 2:
                    pe.wait_ge(sum_done, 2 * (n - 1))
                for half, o in ((0, ps_lo[s]), (1, ps_hi[s])):
                    for a in range(8):
                        c0 = ((kv * 2 + g) * 8 + a) * 8
                        pe.matmul(o[:].rearrange("p b c -> p (b c)").rearrange("p (i c) -> p i c", c=8),
                                  w1[:, kv, half * 8 + a, :], pool_x[:, :, c0:c0 + 8], start=(a == 0), stop=(a == 7))
                for half in range(2):
                    for a in range(8):
                        mm = pe.matmul(ps_pr[s][:, half, :], w1[:, kv, half * 8 + a, :], cp[:, kv, g, a, :],
                                       start=(a == 0), stop=(a == 7))
                mm.then_inc(mm_done, 1)

            def output(n):
                kv, g = COMBOS[n]
                s = n % 2
                pe.wait_ge(act_done, n + 1)
                if kv == 0:
                    pe.wait_ge(pos_done, 1)
                    pe.matmul(ps_o[g * HD:(g + 1) * HD, :], w2[:, 0, :], hd[:, s, 0:NS].rearrange("p b c -> p (b c)"),
                              start=True, stop=True)
                    mm = pe.matmul(ps_p[g * HD:(g + 1) * HD, 0, :], w2[:, 0, :], hd[:, s, NS], start=True, stop=True)
                else:
                    if n == 2:
                        pe.wait_ge(rt_done, 1)
                    else:
                        pe.wait_ge(o_ev, 4)
                    for b in range(NS):
                        pe.matmul(ps_o[0:NCK, b * HD:(b + 1) * HD], hd[:, s, b], w2[:, 1, :], start=True, stop=True)
                    mm = pe.matmul(ps_p[0:NCK, 0, :], hd[:, s, NS], w2[:, 1, :], start=True, stop=True)
                mm.then_inc(o_mm, 1)

            hidden(0)
            hidden(1)
            output(0)
            output(1)
            hidden(2)
            pe.wait_ge(sq_done, 1)
            pe.wait_ge(o_ev, 2)
            pe.matmul(ps_o[:], nm[:, 0:P], sq[:, 0:NS * NCK], start=True, stop=True)
            pe.matmul(ps_p[:, 0, :], nm[:, 0:P], sq[:, NS * NCK:], start=True, stop=True).then_inc(ms_mm, 1)
            hidden(3)
            output(2)
            output(3)


def prompt_attention(nc, d, per, h_hi, h_lo):
    with ExitStack() as ctx:
        sb, ps, sem = sb_of(nc, ctx, "att"), ps_of(nc, ctx, "att"), sem_of(nc, ctx, "att")
        k_sel = sb("k_sel", [P, NP_])
        k_win = sb("k_win", [P, NP_])
        k_cmp = sb("k_cmp", [P, NCK])
        v_sel = sb("v_sel", [P, QT, P])
        v_win = sb("v_win", [P, QT, P])
        v_cmp = sb("v_cmp", [NCK, P])
        near = sb("near", [P, G, R, 2 * P])
        wmask = sb("wmask", [P, P])
        cstrip = sb("cstrip", [P, G, R, CU])
        cmask = sb("cmask", [P, CU])
        q = sb("q", [P, 2, P])
        pr = sb("pr", [P, 2, NP_])
        ptr = sb("ptr", [P, 4, 4 * P])
        gsl = sb("gsl", [P, 2, G, 3])
        nmx = sb("nmx", [P, 2])
        rs = sb("rs", [P, 2])
        cf = sb("cf", [P, 2, 2])
        oacc = sb("oacc", [P, 2, P])
        oT = sb("oT", [P, 2, P])
        S = [ps(f"S{s}", [P, NP_]) for s in range(2)]
        tp = [ps(f"tp{s}", [P, 512]) for s in range(2)]
        O = ps("O", [P, 512])
        facc = ps("facc", [P, 512])
        raw = sb("raw", [P, KT, P])
        w_hi = sb("w_hi", [P, KT, P], F32R)
        w_lo = sb("w_lo", [P, KT, P], F32R)
        zf = sb("zf", [P, T])
        c_in, m_done = sem("c_in"), sem("m_done")
        f_in, f_hi, f_lo, f_mm, f_ev, f_out = (sem(x) for x in ("f_in", "f_hi", "f_lo", "f_mm", "f_ev", "f_out"))
        q_in = [sem("q_in0"), sem("q_in1")]
        o_out = [sem("o_out0"), sem("o_out1")]
        s_mm, s_exp, s_max, s_pm, s_tp, s_te, s_pvg, s_acc, s_ch = (
            sem(x) for x in ("s_mm", "s_exp", "s_max", "s_pm", "s_tp", "s_te", "s_pvg", "s_acc", "s_ch"))
        block = ctx.enter_context(nc.Block())
        HALF = [(g, br) for g in range(G) for br in ("sel", "win", "cmp")]
        NH = len(HALF)
        NJ = 2 * NH

        def tiles(qt, br):
            return {"sel": (0, qt + 1), "win": (max(0, qt - 4), min(qt + 1, 5)), "cmp": (0, 1)}[br]

        def groups(qt, j):
            return -(-tiles(qt, HALF[j % NH][1])[1] // 4)

        def before(qt, j):
            return sum(groups(qt, x) for x in range(j))

        def vbase(qt):
            return sum(2 * before(x, NJ) for x in range(qt))

        def tbase(qt):
            return vbase(qt) + 4 * qt

        def turn_at(qt, s):
            return before(qt, 9) if s == 0 else before(qt, NJ) + 1

        def tgroup(qt, j, a):
            return before(qt, j) + a + (1 if j > 8 else 0)

        @block.sync
        def _(sp):
            clear_last(sp)
            sp.dma_start(raw[:], d["w_in"][U_LX]).then_inc(f_in, 16)
            sp.sem_inc(f_out, 16)
            sp.dma_start(k_sel[:], d["zn"][0][:, 0:NP_]).then_inc(c_in, 16)
            sp.dma_start(k_win[:], d["zn"][1][:, 0:NP_]).then_inc(c_in, 16)
            sp.dma_start(k_cmp[:], d["kcT"][:, NS * NCK:]).then_inc(c_in, 16)
            sp.dma_start(v_sel[:], d["vtok"][0].rearrange("t p n -> p t n")).then_inc(c_in, 16)
            sp.dma_start(v_win[:], d["vtok"][1].rearrange("t p n -> p t n")).then_inc(c_in, 16)
            sp.dma_start(v_cmp[:], d["vc"][:, NS, :]).then_inc(c_in, 16)
            sp.dma_start(near[:].rearrange("p g r n -> p (g r) n"),
                         bass.AP(d["dist"].tensor, RMAX - P, [[8 * RLEN - 1, P], [RLEN, 8], [1, 2 * P]])).then_inc(c_in, 16)
            sp.dma_start(wmask[:], d["wmask"]).then_inc(c_in, 16)
            sp.dma_start(cmask[:], d["cmask"]).then_inc(c_in, 16)
            sp.wait_ge(m_done, 2)
            for h in range(8):
                sp.dma_start(cstrip[:, h // R, h % R, 40:64],
                             bass.AP(d["dist"].tensor, h * RLEN + 16 * 40 - 505, [[8 * RLEN - 1, P], [16, 24]]), allow_slow_non_contiguous=True).then_inc(c_in, 16)

            def load_q(b, s):
                sp.dma_start(q[:, s], d["zn"][2 + 2 * (b % 2) + s][:, (b // 2) * P:(b // 2 + 1) * P]).then_inc(q_in[s], 16)

            sp.sem_inc(o_out[0], 16)
            sp.sem_inc(o_out[1], 16)
            load_q(0, 0)
            load_q(0, 1)
            for b in range(2 * QT):
                qt = b // 2
                sp.wait_ge(f_lo, b + 1)
                sp.dma_start(raw[:], d["w_in"][U_LX + b + 1]).then_inc(f_in, 16)
                if b >= 1:
                    sp.wait_ge(f_ev, 3 * b + 1)
                    sp.dma_start(d["z"][U_LX + b - 1], zf[:]).then_inc(f_out, 16)
                for s in range(2):
                    if b + 1 < 2 * QT:
                        sp.wait_ge(s_mm, NJ * b + NH * s + NH)
                        load_q(b + 1, s)
                    sp.wait_ge(s_te, tbase(qt) + (b % 2) * (before(qt, NJ) + 2) + turn_at(qt, s) + 3)
                    sp.dma_start(d["o_nsa"][2 * (b % 2) + s][:, qt * P:(qt + 1) * P], oT[:, s]).then_inc(o_out[s], 16)
            sp.wait_ge(f_ev, 3 * 2 * QT + 1)
            sp.dma_start(d["z"][U_LX + 2 * QT - 1], zf[:]).then_inc(f_out, 16)
            sp.wait_ge(f_out, 16 * (2 * QT + 1))
            sp.wait_ge(f_in, 16 * (2 * QT + 1))
            sp.wait_ge(o_out[0], 16 * (2 * QT + 1))
            sp.wait_ge(o_out[1], 16 * (2 * QT + 1))

        @block.gpsimd
        def _(pool):
            pool.memset(cstrip[:, :, :, 0:64], 0.0).then_inc(m_done, 1)
            pool.memset(cstrip[:, :, :, 64:CU], NEGV).then_inc(m_done, 1)
            pool.memset(pr[:, :, 0:P], 0.0).then_inc(m_done, 1)

            pool.wait_ge(f_hi, 1)
            pool.tensor_tensor(w_lo[:], raw[:], w_hi[:].bitcast(F32), ALU.subtract).then_inc(f_lo, 1)
            with pool.Fori(0, 2 * QT) as i:
                pool.wait_ge(f_hi, i * 1 + 2)
                pool.tensor_tensor(w_lo[:], raw[:], w_hi[:].bitcast(F32), ALU.subtract).then_inc(f_lo, 1)

        @block.tensor
        def _(pe):
            pe.sem_inc(s_pvg, 4)
            pe.wait_ge(c_in, 16 * 17)
            for qt in range(QT):
                nv = before(qt, NJ)
                nt = nv + 2
                with pe.Fori(0, 2) as i:

                    def scores(j):
                        s, (g, br) = j // NH, HALF[j % NH]
                        k0, nk = tiles(qt, br)
                        keys = {"sel": k_sel, "win": k_win, "cmp": k_cmp}[br]
                        n = NCMP if br == "cmp" else nk * P
                        if j % NH == 0:
                            pe.wait_ge(q_in[s], i * 16 + (32 * qt + 16))
                        pe.wait_ge(s_exp, i * NJ + (2 * NJ * qt + j + 1))
                        for c in range(0, n, 512):
                            w = min(512, n - c)
                            mm = pe.matmul(S[j % 2][:, c:c + w], q[g * HD:(g + 1) * HD, s, :],
                                           keys[g * HD:(g + 1) * HD, k0 * P + c:k0 * P + c + w], start=True, stop=True)
                        mm.then_inc(s_mm, 1)

                    def transposes(j):
                        br = HALF[j % NH][1]
                        if br == "cmp":
                            pe.wait_ge(s_pm, i * 4 + (8 * qt + 2 * (j // NH) + HALF[j % NH][0] + 1))
                        else:
                            pe.wait_ge(s_exp, i * NJ + (2 * NJ * qt + j + 3))
                        for a in range(groups(qt, j)):
                            tg = tgroup(qt, j, a)
                            pe.wait_ge(s_te, i * nt + (tbase(qt) + tg + 1))
                            for t in range(4 * a, min(4 * a + 4, tiles(qt, br)[1])):
                                mm = pe.transpose(tp[tg % 2][:, (t % 4) * P:(t % 4 + 1) * P],
                                                  pr[:, j % 2, t * P:(t + 1) * P], per["ident"][:])
                            mm.then_inc(s_tp, 1)

                    def values(j):
                        g, br = HALF[j % NH]
                        k0, nk = tiles(qt, br)
                        vals = {"sel": v_sel, "win": v_win}.get(br)
                        pe.wait_ge(s_acc, i * NJ + (2 * NJ * qt + j + 2))
                        for a in range(groups(qt, j)):
                            vg = before(qt, j) + a
                            pe.wait_ge(s_te, i * nt + (tbase(qt) + tgroup(qt, j, a) + 3))
                            for t in range(4 * a, min(4 * a + 4, nk)):
                                if br == "cmp":
                                    lhs, rhs = ptr[0:NCMP, vg % 4, 0:P], v_cmp[0:NCMP, g * HD:(g + 1) * HD]
                                else:
                                    lhs = ptr[:, vg % 4, (t % 4) * P:(t % 4 + 1) * P]
                                    rhs = vals[:, k0 + t, g * HD:(g + 1) * HD]
                                mm = pe.matmul(O[:, 0:HD], lhs, rhs, start=(t == 0), stop=(t == nk - 1))
                            mm.then_inc(s_pvg, 1)

                    def turn(s):
                        tg = turn_at(qt, s)
                        pe.wait_ge(s_te, i * nt + (tbase(qt) + tg + 1))
                        pe.wait_ge(s_acc, i * NJ + (2 * NJ * qt + NH * s + NH + 2))
                        pe.transpose(tp[tg % 2][:, 0:P], oacc[:, s], per["ident"][:]).then_inc(s_tp, 1)

                    def filler(f):
                        c = f // 3
                        if f == 0:
                            pe.wait_ge(f_lo, i * 1 + (2 * qt + 1))
                        if f % 3 == 0:
                            pe.wait_ge(f_ev, i * 3 + (6 * qt + c + 1))
                        for x in range(8 * (f % 3), 8 * (f % 3) + 8):
                            k, n = x // 3, x % 3
                            w, h = ((w_hi, h_hi), (w_hi, h_lo), (w_lo, h_hi))[n]
                            mm = pe.matmul(facc[:, 0:CW], w[:, k, :], h[:, k, c * CW:(c + 1) * CW], start=(x == 0), stop=(x == 23))
                        if f % 3 == 2:
                            mm.then_inc(f_mm, 1)

                    scores(0)
                    filler(0)
                    for j in range(NJ):
                        if j + 1 < NJ:
                            scores(j + 1)
                        if j < 8:
                            filler(j + 1)
                        if j >= 1:
                            values(j - 1)
                        transposes(j)
                        if j == 8:
                            turn(0)
                    values(NJ - 1)
                    turn(1)

        @block.scalar
        def _(act):
            act.sem_inc(s_exp, 2)
            act.sem_inc(s_te, 2)
            act.wait_ge(m_done, 3)
            act.wait_ge(f_in, 16)
            act.activation(w_hi[:], raw[:], ACT.Copy).then_inc(f_hi, 1)
            for qt in range(QT):
                nv = before(qt, NJ)
                nt = nv + 2
                with act.Fori(0, 2) as i:

                    def probs(j):
                        br = HALF[j % NH][1]
                        n = NCMP if br == "cmp" else tiles(qt, br)[1] * P
                        act.wait_ge(s_max, i * NJ + (2 * NJ * qt + j + 1))
                        act.activation(pr[:, j % 2, 0:n], S[j % 2][:, 0:n], ACT.Exp, bias=nmx[:, j % 2:j % 2 + 1],
                                       accum_out=rs[:, j % 2:j % 2 + 1]).then_inc(s_exp, 1)

                    def copies(j):
                        k0, nk = tiles(qt, HALF[j % NH][1])
                        cmp = HALF[j % NH][1] == "cmp"
                        for a in range(groups(qt, j)):
                            vg, tg = before(qt, j) + a, tgroup(qt, j, a)
                            m = min(4, nk - 4 * a) * P
                            w = NCMP if cmp else P
                            act.wait_ge(s_pvg, i * nv + (vbase(qt) + vg + 1))
                            act.wait_ge(s_tp, i * nt + (tbase(qt) + tg + 1))
                            act.activation(ptr[0:w, vg % 4, 0:m], tp[tg % 2][0:w, 0:m], ACT.Copy).then_inc(s_te, 1)

                    def turned(s):
                        tg = turn_at(qt, s)
                        act.wait_ge(o_out[s], i * 16 + (32 * qt + 16))
                        act.wait_ge(s_tp, i * nt + (tbase(qt) + tg + 1))
                        act.activation(oT[:, s], tp[tg % 2][:, 0:P], ACT.Copy).then_inc(s_te, 1)

                    probs(0)
                    for j in range(NJ):
                        if j + 1 < NJ:
                            probs(j + 1)
                        copies(j)
                        if j == 8:
                            turned(0)
                        if j == 10:
                            act.wait_ge(f_in, i * 16 + (32 * qt + 32))
                            act.wait_ge(f_mm, i * 3 + (6 * qt + 3))
                            act.activation(w_hi[:], raw[:], ACT.Copy).then_inc(f_hi, 1)
                    turned(1)

        @block.vector
        def _(dve):
            dve.sem_inc(s_acc, 2)
            dve.wait_ge(c_in, 16 * 17)
            dve.sem_inc(f_ev, 1)
            chb = 0
            for qt in range(QT):
                per_body = 46 + (4 if qt >= 4 else 0)
                with dve.Fori(0, 2) as i:
                    count = [0]

                    def chain(ins):
                        count[0] += 1
                        ins.then_inc(s_ch, 1)
                        dve.wait_ge(s_ch, i * per_body + (chb + count[0]))

                    def maxima(j):
                        s, (g, br) = j // NH, HALF[j % NH]
                        k0, nk = tiles(qt, br)
                        x = S[j % 2]
                        n = NCMP if br == "cmp" else nk * P
                        r = i * 2 + s
                        dve.wait_ge(s_mm, i * NJ + (2 * NJ * qt + j + 1))
                        if br == "cmp":
                            c0 = 56 - 8 * qt
                            chain(dve.tensor_tensor(x[:, 0:n], x[:, 0:n], cstrip[:, g, bass.ds(r, 1), c0:c0 + n].rearrange(
                                "p a n -> p (a n)"), ALU.add))
                        else:
                            m = min(nk, 2) * P
                            chain(dve.tensor_tensor(x[:, n - m:n], x[:, n - m:n], near[:, g, bass.ds(r, 1), 2 * P - m:].rearrange(
                                "p a n -> p (a n)"), ALU.add))
                            if br == "win" and qt >= 4:
                                chain(dve.tensor_tensor(x[:, 0:P], x[:, 0:P], wmask[:], ALU.add))
                        dve.tensor_reduce(nmx[:, j % 2:j % 2 + 1], x[:, 0:n], AX, ALU.max, negate=True).then_inc(s_max, 1)

                    def coefficient(j):
                        s, (g, br) = j // NH, HALF[j % NH]
                        bi = ("cmp", "sel", "win").index(br)
                        v = rs[:, j % 2:j % 2 + 1]
                        dve.wait_ge(s_exp, i * NJ + (2 * NJ * qt + j + 3))
                        if br == "cmp":
                            c0 = 56 - 8 * qt
                            pm = pr[:, j % 2, 0:NCMP]
                            dve.tensor_tensor(pm, pm, cmask[:, c0:c0 + NCMP], ALU.mult).then_inc(s_pm, 1)
                            dve.wait_ge(s_pm, i * 4 + (8 * qt + 2 * s + g + 1))
                            chain(dve.tensor_reduce(v, pm, AX, ALU.add))
                            chain(dve.tensor_scalar(v, v, 1e-30, None, ALU.max))
                        chain(dve.reciprocal(cf[:, j % 2, 0:1], v))
                        chain(dve.tensor_tensor(cf[:, j % 2, 1:2], cf[:, j % 2, 0:1], gsl[:, s, g, bi:bi + 1], ALU.mult))

                    def accumulate(j):
                        s, (g, br) = j // NH, HALF[j % NH]
                        dve.wait_ge(s_pvg, i * before(qt, NJ) + (vbase(qt) + before(qt, j + 1) + 4))
                        o = oacc[:, s, g * HD:(g + 1) * HD]
                        c = cf[:, j % 2, 1:2]
                        if br == "sel":
                            dve.tensor_scalar(o, O[:, 0:HD], c, None, ALU.mult).then_inc(s_acc, 1)
                        else:
                            dve.wait_ge(s_acc, i * NJ + (2 * NJ * qt + j + 2))
                            dve.scalar_tensor_tensor(o, O[:, 0:HD], c, o, ALU.mult, ALU.add).then_inc(s_acc, 1)

                    for j in range(NJ + 2):
                        if j < NJ:
                            if j % NH == 0:
                                r = i * 2 + j // NH
                                gt = per["gate"][:, qt, :].rearrange("p (g r c) -> p g r c", g=G, r=R)
                                chain(dve.tensor_copy(gsl[:, j // NH], gt[:, :, bass.ds(r, 1), :].rearrange("p g a c -> p g (a c)")))
                            maxima(j)
                        if j >= 2:
                            accumulate(j - 2)
                        if 1 <= j <= NJ:
                            coefficient(j - 1)
                        if j in (2, 5, 8):
                            c = j // 3
                            if c == 0:
                                dve.wait_ge(f_out, i * 16 + (32 * qt + 16))
                            dve.wait_ge(f_mm, i * 3 + (6 * qt + c + 1))
                            dve.tensor_copy(zf[:, c * CW:(c + 1) * CW], facc[:, 0:CW]).then_inc(f_ev, 1)
                    assert count[0] == per_body, count[0]
                chb += 2 * per_body


def memory_attention(nc, d, per):
    SC = P ** -0.5
    NJ = 2 * MH
    with ExitStack() as ctx:
        sb, ps, sem = sb_of(nc, ctx, "mat"), ps_of(nc, ctx, "mat"), sem_of(nc, ctx, "mat")
        km = sb("km", [P, MH, NMEM])
        vm = sb("vm", [P, MH, 2, P])
        q = sb("q", [P, 2, MH, P])
        pr = sb("pr", [P, 2, NMEM])
        ptr = sb("ptr", [P, 2, NMEM])
        mx = sb("mx", [P, 2, 2])
        rs = sb("rs", [P, 2, 2])
        oT = sb("oT", [P, 2, MH, P])
        S = [ps(f"S{s}", [P, 512]) for s in range(2)]
        tp = [ps(f"tp{s}", [P, 512]) for s in range(2)]
        O = [ps(f"O{s}", [P, 512]) for s in range(2)]
        c_in = sem("c_in")
        q_in = [sem("q_in0"), sem("q_in1")]
        o_out = [sem("o_out0"), sem("o_out1")]
        s_mm, s_mx, s_neg, s_exp, s_rc, s_pn, s_tp, s_te, s_pv, s_oe = (
            sem(x) for x in ("s_mm", "s_mx", "s_neg", "s_exp", "s_rc", "s_pn", "s_tp", "s_te", "s_pv", "s_oe"))
        block = ctx.enter_context(nc.Block())

        @block.sync
        def _(sp):
            clear_last(sp)
            sp.dma_start(km[:], d["memn"].rearrange("h p n -> p h n")).then_inc(c_in, 16)
            sp.dma_start(vm[:], d["memv"].rearrange("h t p n -> p h t n")).then_inc(c_in, 16)
            sp.sem_inc(o_out[0], 16)
            sp.sem_inc(o_out[1], 16)

            def tile_of(a, m):
                return a[:, :, m * P:(m + 1) * P].rearrange("h p n -> p h n")

            def store(m):
                sp.wait_ge(s_oe, MH * (m + 1) + 2)
                sp.dma_start(tile_of(d["o_mem"], m), oT[:, m % 2]).then_inc(o_out[m % 2], 16)

            for m in range(QT):
                if m >= 2:
                    sp.wait_ge(s_mm, MH * (m - 1))
                sp.dma_start(q[:, m % 2], tile_of(d["zn"][6:10], m)).then_inc(q_in[m % 2], 16)
                if m >= 2:
                    store(m - 2)
            store(QT - 2)
            store(QT - 1)
            sp.wait_ge(o_out[0], 16 * (QT // 2 + 1))
            sp.wait_ge(o_out[1], 16 * (QT // 2 + 1))

        @block.tensor
        def _(pe):
            pe.wait_ge(c_in, 32)
            with pe.Fori(0, QT // 2) as i:

                def scores(j):
                    t, h = j // MH, j % MH
                    if h == 0:
                        pe.wait_ge(q_in[t], i * 16 + 16)
                    pe.wait_ge(s_exp, i * NJ + (j + 1))
                    pe.matmul(S[j % 2][:, 0:NMEM], q[:, t, h], km[:, h], start=True, stop=True).then_inc(s_mm, 1)

                def turn(j):
                    pe.wait_ge(s_pn, i * NJ + (j + 1))
                    for t in range(2):
                        mm = pe.transpose(tp[j % 2][:, t * P:(t + 1) * P], pr[:, j % 2, t * P:(t + 1) * P], per["ident"][:])
                    mm.then_inc(s_tp, 1)

                def values(j):
                    pe.wait_ge(s_te, i * NJ + (j + 1))
                    pe.wait_ge(s_oe, i * NJ + (j + 1))
                    for t in range(2):
                        mm = pe.matmul(O[j % 2][:, 0:P], vm[:, j % MH, t], ptr[:, j % 2, t * P:(t + 1) * P],
                                       start=(t == 0), stop=(t == 1))
                    mm.then_inc(s_pv, 1)

                scores(0)
                for j in range(NJ):
                    if j + 1 < NJ:
                        scores(j + 1)
                    if j >= 1:
                        values(j - 1)
                    turn(j)
                values(NJ - 1)

        @block.vector
        def _(dve):
            with dve.Fori(0, QT // 2) as i:

                def maximum(j):
                    s = j % 2
                    dve.wait_ge(s_mm, i * NJ + (j + 1))
                    dve.tensor_reduce(mx[:, s, 0:1], S[s][:, 0:NMEM], AX, ALU.max).then_inc(s_mx, 1)
                    dve.wait_ge(s_mx, i * NJ + (j + 1))
                    dve.tensor_scalar(mx[:, s, 1:2], mx[:, s, 0:1], -SC, None, ALU.mult).then_inc(s_neg, 1)

                def normal(j):
                    s = j % 2
                    dve.wait_ge(s_exp, i * NJ + (j + 3))
                    dve.reciprocal(rs[:, s, 1:2], rs[:, s, 0:1]).then_inc(s_rc, 1)
                    dve.wait_ge(s_rc, i * NJ + (j + 1))
                    dve.tensor_scalar(pr[:, s], pr[:, s], rs[:, s, 1:2], None, ALU.mult).then_inc(s_pn, 1)

                maximum(0)
                for j in range(NJ):
                    if j + 1 < NJ:
                        maximum(j + 1)
                    normal(j)

        @block.scalar
        def _(act):
            act.sem_inc(s_exp, 2)
            act.sem_inc(s_oe, 2)
            with act.Fori(0, QT // 2) as i:

                def exponentials(j):
                    s = j % 2
                    act.wait_ge(s_neg, i * NJ + (j + 1))
                    act.activation(pr[:, s], S[s][:, 0:NMEM], ACT.Exp, bias=mx[:, s, 1:2], scale=SC,
                                   accum_out=rs[:, s, 0:1]).then_inc(s_exp, 1)

                def turned(j):
                    act.wait_ge(s_tp, i * NJ + (j + 1))
                    act.activation(ptr[:, j % 2], tp[j % 2][:, 0:NMEM], ACT.Copy).then_inc(s_te, 1)

                def output(j):
                    if j % MH == 0:
                        act.wait_ge(o_out[j // MH], i * 16 + 16)
                    act.wait_ge(s_pv, i * NJ + (j + 1))
                    act.activation(oT[:, j // MH, j % MH], O[j % 2][:, 0:P], ACT.Copy).then_inc(s_oe, 1)

                exponentials(0)
                for j in range(NJ):
                    if j + 1 < NJ:
                        exponentials(j + 1)
                    if j >= 1:
                        output(j - 1)
                    turned(j)
                output(NJ - 1)


def sample_attention(nc, d, per):
    RW = NS * 8
    LS = NP_ + 1
    LW = WIN + 1
    NB = 16
    with ExitStack() as ctx:
        sb, ps, sem = sb_of(nc, ctx, "sat"), ps_of(nc, ctx, "sat"), sem_of(nc, ctx, "sat")
        pt = sb("pt", [1, NS * PAGES], I32)
        qs = sb("qs", [P, R, NS])
        qb = sb("qb", [P, NS, RW])
        knew = sb("knew", [P, NS, 2])
        vnew = sb("vnew", [1, NS, 2, P])
        kc = sb("kc", [P, NS, NCK])
        ks = sb("ks", [P, NS, PAGES, P])
        kw = sb("kw", [P, NS, WIN])
        vs = sb("vs", [P, 4, PAGES, P])
        vw = sb("vw", [P, 4, WIN // P, P])
        vc = sb("vc", [NCK, 4, P])
        b_far = sb("b_far", [RW, P + 1])
        b_cmp = sb("b_cmp", [RW, 23])
        gt = sb("gt", [RW, 3])
        grp = sb("grp", [RW, RW])
        blk = sb("blk", [RW, NB])
        ls = sb("ls", [RW, LS + 7])
        lw = sb("lw", [RW, LW + 7])
        lc = sb("lc", [RW, NCK])
        sc = sb("sc", [RW, 16])
        sel = sb("sel", [RW, 4, NB])
        keep = sb("keep", [RW, NCK])
        pT = sb("pT", [P, 13, RW])
        nT = sb("nT", [1, 2, RW])
        oT = sb("oT", [P, R, NS])
        S0, S1, S2, S3, S4 = (ps(f"S{n}", [P, 512]) for n in range(5))
        S5, S6, S7 = (ps(f"S{n}", [P, 512]) for n in range(5, 8))
        c_in, b_in, z_done, qb_done, vn_in, pt_in = sem("c_in"), sem("b_in"), sem("z_done"), sem("qb_done"), sem("vn_in"), sem("pt_in")
        k_in = [sem(f"k_in{b}") for b in range(NS)]
        v_in = [sem(f"v_in{s}") for s in range(4)]
        s_mm, ch, e_done, a_done, g_mm, tp_done, te_done, o_mm, o_done, o_out, s_all, m_done = (
            sem(x) for x in ("s_mm", "ch", "e_done", "a_done", "g_mm", "tp_done", "te_done", "o_mm", "o_done", "o_out",
                             "s_all", "m_done"))
        block = ctx.enter_context(nc.Block())
        dist = d["dist"].tensor

        @block.sync
        def _(sp):
            clear_last(sp)
            sp.dma_start(pt[:], d["page_table"]).then_inc(pt_in, 16)
            sp.dma_start(qs[:], d["zn"][2:6][:, :, NP_:T].rearrange("r p b -> p r b")).then_inc(c_in, 16)
            sp.dma_start(knew[:, :, 0], d["zn"][0][:, NP_:T], allow_slow_non_contiguous=True).then_inc(c_in, 16)
            sp.dma_start(knew[:, :, 1], d["zn"][1][:, NP_:T], allow_slow_non_contiguous=True).then_inc(c_in, 16)
            sp.dma_start(kc[:].rearrange("p b c -> p (b c)"), d["kcT"][:, 0:NS * NCK]).then_inc(c_in, 16)
            sp.dma_start(grp[:], d["grp"]).then_inc(c_in, 16)
            sp.dma_start(blk[:], d["blk"]).then_inc(c_in, 16)
            sp.dma_start(gt[:], d["gate_s"].rearrange("(r c) o -> r (c o)", c=3)).then_inc(c_in, 16)
            sp.wait_ge(pt_in, 16)
            for b in range(NS):
                sp.dma_start(kw[:, b], d["winkT"][b]).then_inc(k_in[b], 16)
                with sp.Fori(0, PAGES) as i:
                    page = sp.value_load(pt[0:1, bass.ds(i + b * PAGES, 1)], min_val=0, max_val=d["sel_kT"].shape[0] - 1)
                    sp.dma_start(ks[:, b, bass.ds(i, 1), :].rearrange("p a n -> p (a n)"),
                                 d["sel_kT"][bass.ds(page, 1)].rearrange("a p n -> p (a n)")).then_inc(k_in[b], 16)
            for b in range(NS):
                sp.dma_start(b_far[b * 8:(b + 1) * 8, :],
                             bass.AP(dist, RMAX - P, [[RLEN, 8], [1, P + 1]])).then_inc(b_in, 16)
                sp.dma_start(b_cmp[b * 8:(b + 1) * 8, :],
                             bass.AP(dist, 16 * 40 - 633, [[RLEN, 8], [16, 23]]), allow_slow_non_contiguous=True).then_inc(b_in, 16)
                for j, u in enumerate((U_SELV, U_WINV)):
                    sp.dma_start(vnew[0:1, b, j, :], bass.AP(d["z"].tensor, u * P * T + NP_ + b, [[0, 1], [T, P]]),
                                 allow_slow_non_contiguous=True).then_inc(vn_in, 16)
            sp.wait_ge(o_done, 2)
            sp.dma_start(d["o_nsa"][:, :, NP_:T].rearrange("r p b -> p r b"), oT[:]).then_inc(o_out, 16)
            sp.wait_ge(o_out, 16)

        @block.gpsimd
        def _(pool):
            pool.wait_ge(pt_in, 16)
            for b in range(NS):
                s = b % 4
                if b >= 4:
                    pool.wait_ge(o_mm, b - 3)
                pool.dma_start(vw[:, s], d["win_v"][b].rearrange("t p n -> p t n")).then_inc(v_in[s], 16)
                pool.dma_start(vc[:, s], d["vc"][:, b, :]).then_inc(v_in[s], 16)
                with pool.Fori(0, PAGES) as i:
                    page = pool.value_load(pt[0:1, bass.ds(i + b * PAGES, 1)], min_val=0, max_val=d["sel_v"].shape[0] - 1)
                    pool.dma_start(vs[:, s, bass.ds(i, 1), :].rearrange("p a n -> p (a n)"),
                                   d["sel_v"][bass.ds(page, 1)].rearrange("a p n -> p (a n)")).then_inc(v_in[s], 16)

        @block.tensor
        def _(pe):
            pe.wait_ge(qb_done, 2)
            pe.wait_ge(c_in, 16 * 7)
            for b in range(NS):
                st, sp_ = b == 0, b == NS - 1
                lhs = qb[:, b, :]
                pe.wait_ge(k_in[b], 16 * 9)
                pe.matmul(S0[0:RW, :], lhs, ks[:, b, 0:4].rearrange("p a n -> p (a n)"), start=st, stop=sp_)
                pe.matmul(S1[0:RW, :], lhs, ks[:, b, 4:8].rearrange("p a n -> p (a n)"), start=st, stop=sp_)
                pe.matmul(S2[0:RW, :], lhs, kw[:, b], start=st, stop=sp_)
                pe.matmul(S3[0:RW, 0:2], lhs, knew[:, b, :], start=st, stop=sp_)
                pe.matmul(S4[0:RW, 0:NCK], lhs, kc[:, b, :], start=st, stop=sp_).then_inc(s_mm, 1)
            pe.wait_ge(g_mm, 1)
            pe.matmul(S5[0:RW, 0:NCMP], grp[:], lc[:, 0:NCMP], start=True, stop=True).then_inc(tp_done, 1)
            pe.wait_ge(m_done, 1)
            idn = per["ident"][0:RW, 0:RW]
            for t in range(8):
                pe.transpose(S6[:, t * RW:(t + 1) * RW], ls[:, t * P:(t + 1) * P], idn)
            for t in range(4):
                pe.transpose(S7[:, t * RW:(t + 1) * RW], lw[:, t * P:(t + 1) * P], idn)
            pe.transpose(S7[0:NCMP, 4 * RW:5 * RW], lc[:, 0:NCMP], idn)
            pe.transpose(S5[0:1, 128:128 + RW], ls[:, NP_:LS], idn)
            pe.transpose(S5[0:1, 256:256 + RW], lw[:, WIN:LW], idn).then_inc(tp_done, 1)
            pe.wait_ge(te_done, 4)
            pe.wait_ge(vn_in, 16 * 2 * NS)
            for b in range(NS):
                s, c = b % 4, slice(b * 8, (b + 1) * 8)
                pe.wait_ge(v_in[s], 16 * 10 * (b // 4 + 1))
                for t in range(8):
                    pe.matmul(S0[:, c], vs[:, s, t], pT[:, t, c], start=(t == 0), stop=False)
                for t in range(4):
                    pe.matmul(S0[:, c], vw[:, s, t], pT[:, 8 + t, c], start=False, stop=False)
                pe.matmul(S0[:, c], vc[0:NCMP, s], pT[0:NCMP, 12, c], start=False, stop=False)
                pe.matmul(S0[:, c], vnew[0:1, b, 0, :], nT[0:1, 0, c], start=False, stop=False)
                pe.matmul(S0[:, c], vnew[0:1, b, 1, :], nT[0:1, 1, c], start=False, stop=True).then_inc(o_mm, 1)

        @block.scalar
        def _(act):
            act.wait_ge(a_done, 1)
            act.activation(lc[:, 0:NCMP], lc[:, 0:NCMP], ACT.Exp, bias=sc[:, 0:1], accum_out=sc[:, 1:2]).then_inc(e_done, 1)
            act.wait_ge(a_done, 2)
            act.activation(ls[:, 0:LS], ls[:, 0:LS], ACT.Exp, bias=sc[:, 2:3], accum_out=sc[:, 3:4]).then_inc(e_done, 1)
            act.wait_ge(a_done, 3)
            act.activation(lw[:, 0:LW], lw[:, 0:LW], ACT.Exp, bias=sc[:, 4:5], accum_out=sc[:, 5:6]).then_inc(e_done, 1)

        @block.vector
        def _(dve):
            n = [0]

            def chain(ins):
                n[0] += 1
                ins.then_inc(ch, 1)
                dve.wait_ge(ch, n[0])

            chain(dve.memset(qb[:], 0.0))
            dve.wait_ge(c_in, 16 * 7)
            for g in range(G):
                rows = slice(g * HD, (g + 1) * HD)
                q0 = qb[rows].rearrange("p b c -> p (b c)")
                for b in range(NS):
                    ins = dve.tensor_copy(q0[:, b * (RW + 8) + g * R:b * (RW + 8) + (g + 1) * R], qs[rows, :, b])
                ins.then_inc(qb_done, 1)
            dve.wait_ge(s_mm, NS)
            dve.wait_ge(b_in, 16 * 2 * NS)
            chain(dve.tensor_copy(lc[:, 0:40], S4[0:RW, 0:40]))
            chain(dve.tensor_tensor(lc[:, 40:NCMP], S4[0:RW, 40:NCMP], b_cmp[:], ALU.add))
            dve.tensor_reduce(sc[:, 0:1], lc[:, 0:NCMP], AX, ALU.max, negate=True).then_inc(a_done, 1)
            dve.wait_ge(e_done, 1)
            chain(dve.reciprocal(sc[:, 6:7], sc[:, 1:2]))
            dve.tensor_scalar(lc[:, 0:NCMP], lc[:, 0:NCMP], sc[:, 6:7], None, ALU.mult).then_inc(g_mm, 1)
            dve.wait_ge(tp_done, 1)
            ssum = keep[:]
            chain(dve.memset(ssum[:, NCMP:NCK], 0.0))
            chain(dve.tensor_copy(ssum[:, 0:NCMP], S5[0:RW, 0:NCMP]))
            chain(dve.tensor_reduce(sel[:, 0], ssum.rearrange("p (s c) -> p s c", c=4), AX, ALU.add))
            chain(dve.tensor_tensor(sel[:, 0, 1:NB], sel[:, 0, 1:NB], ssum.rearrange("p (s c) -> p s c", c=4)[:, 0:NB - 1, 3], ALU.add))
            chain(dve.tensor_reduce(sc[:, 7:8], sel[:, 0, 1:NB - 1], AX, ALU.min))
            chain(dve.memset(sel[:, 1], 0.0))
            chain(dve.tensor_scalar(sel[:, 1, 1:NB - 1], sel[:, 0, 1:NB - 1], sc[:, 7:8], None, ALU.is_le))
            chain(dve.tensor_tensor(sel[:, 1], sel[:, 1], blk[:], ALU.mult))
            chain(dve.tensor_reduce(sc[:, 8:9], sel[:, 1], AX, ALU.max))
            chain(dve.tensor_scalar(sel[:, 2], blk[:], sc[:, 8:9], NEGV, ALU.is_equal, ALU.mult))
            chain(dve.tensor_copy(ls[:, 0:512], S0[0:RW, :]))
            chain(dve.tensor_copy(ls[:, 512:NP_ - P], S1[0:RW, 0:512 - P]))
            chain(dve.tensor_tensor(ls[:, NP_ - P:NP_], S1[0:RW, 512 - P:512], b_far[:, 0:P], ALU.add))
            chain(dve.tensor_tensor(ls[:, NP_:LS], S3[0:RW, 0:1], b_far[:, P:P + 1], ALU.add))
            chain(dve.tensor_tensor(ls[:, 0:NP_].rearrange("p (s c) -> p s c", s=NB), ls[:, 0:NP_].rearrange("p (s c) -> p s c", s=NB),
                                    sel[:, 2].rearrange("p (s a) -> p s a", a=1).to_broadcast([RW, NB, NP_ // NB]), ALU.add))
            dve.tensor_reduce(sc[:, 2:3], ls[:, 0:LS], AX, ALU.max, negate=True).then_inc(a_done, 1)
            chain(dve.tensor_copy(lw[:, 0:WIN - P], S2[0:RW, 0:WIN - P]))
            chain(dve.tensor_tensor(lw[:, WIN - P:WIN], S2[0:RW, WIN - P:WIN], b_far[:, 0:P], ALU.add))
            chain(dve.tensor_tensor(lw[:, WIN:LW], S3[0:RW, 1:2], b_far[:, P:P + 1], ALU.add))
            chain(dve.memset(lw[:, 0:1], NEGV))
            dve.tensor_reduce(sc[:, 4:5], lw[:, 0:LW], AX, ALU.max, negate=True).then_inc(a_done, 1)
            chain(dve.tensor_scalar(lc[:, 0:NCMP], lc[:, 0:NCMP], gt[:, 0:1], None, ALU.mult))
            dve.wait_ge(e_done, 2)
            chain(dve.reciprocal(sc[:, 9:10], sc[:, 3:4]))
            chain(dve.tensor_scalar(ls[:, 0:LS], ls[:, 0:LS], sc[:, 9:10], gt[:, 1:2], ALU.mult, ALU.mult))
            dve.wait_ge(e_done, 3)
            chain(dve.reciprocal(sc[:, 10:11], sc[:, 5:6]))
            dve.tensor_scalar(lw[:, 0:LW], lw[:, 0:LW], sc[:, 10:11], gt[:, 2:3], ALU.mult, ALU.mult).then_inc(m_done, 1)
            dve.wait_ge(tp_done, 2)
            dve.tensor_copy(pT[:, 0:8].rearrange("p t r -> p (t r)"), S6[:, 0:8 * RW]).then_inc(te_done, 1)
            dve.tensor_copy(pT[:, 8:12].rearrange("p t r -> p (t r)"), S7[:, 0:4 * RW]).then_inc(te_done, 1)
            dve.tensor_copy(pT[0:NCMP, 12], S7[0:NCMP, 4 * RW:5 * RW]).then_inc(te_done, 1)
            dve.tensor_copy(nT[:], S5[0:1, 128:384].rearrange("p (j n) -> p j n", j=2)[:, :, 0:RW]).then_inc(te_done, 1)
            dve.wait_ge(o_mm, NS)
            for g in range(G):
                rows = slice(g * HD, (g + 1) * HD)
                dve.tensor_copy(oT[rows], S0[rows, 0:RW].rearrange("p (b h) -> p h b", h=8)[:, g * R:(g + 1) * R, :]).then_inc(o_done, 1)


def sample_memory(nc, d, per):
    RW = NS * MH
    RP = 64
    SC = P ** -0.5
    with ExitStack() as ctx:
        sb, ps, sem = sb_of(nc, ctx, "sme"), ps_of(nc, ctx, "sme"), sem_of(nc, ctx, "sme")
        qs = sb("qs", [P, MH, NS])
        qb = sb("qb", [P, RW, RP])
        km = sb("km", [P, 2, MH, NMEM])
        vm = sb("vm", [P, 2, 2, MH, P])
        pr = sb("pr", [RW, NMEM])
        pT = sb("pT", [P, 2, RW])
        sc = sb("sc", [RW, 4])
        oT = sb("oT", [P, MH, NS])
        O, tp, S = ps("O", [P, 512]), ps("tp", [P, 512]), ps("S", [P, 512])
        c_in, z_done, qb_done = sem("c_in"), sem("z_done"), sem("qb_done")
        k_in = [sem("k_in0"), sem("k_in1")]
        v_in = [sem("v_in0"), sem("v_in1")]
        s_mm, ch, a_done, e_done, p_done, tp_done, te_done, o_mm, o_done, o_out = (
            sem(x) for x in ("s_mm", "ch", "a_done", "e_done", "p_done", "tp_done", "te_done", "o_mm", "o_done", "o_out"))
        block = ctx.enter_context(nc.Block())

        @block.sync
        def _(sp):
            clear_last(sp)
            sp.dma_start(qs[:], d["zn"][6:10][:, :, NP_:T].rearrange("r p b -> p r b")).then_inc(c_in, 16)
            for b in range(NS):
                if b >= 2:
                    sp.wait_ge(s_mm, b - 1)
                sp.dma_start(km[:, b % 2], d["mem_kT"][b]).then_inc(k_in[b % 2], 16)
            for b in range(NS):
                if b >= 2:
                    sp.wait_ge(o_mm, b - 1)
                sp.dma_start(vm[:, b % 2], d["mem_v"][b].rearrange("t p h n -> p t h n")).then_inc(v_in[b % 2], 16)
            sp.wait_ge(o_done, 1)
            sp.dma_start(d["o_mem"][:, :, NP_:T].rearrange("r p b -> p r b"), oT[:]).then_inc(o_out, 16)
            sp.wait_ge(o_out, 16)

        @block.tensor
        def _(pe):
            pe.wait_ge(qb_done, 1)
            for b in range(NS):
                pe.wait_ge(k_in[b % 2], 16 * (b // 2 + 1))
                for h in range(MH):
                    n = b * MH + h
                    mm = pe.matmul(S[0:RP, 0:NMEM], qb[:, n, :], km[:, b % 2, h, :], start=(n == 0), stop=(n == RW - 1))
                mm.then_inc(s_mm, 1)
            pe.wait_ge(p_done, 1)
            for t in range(2):
                mm = pe.transpose(tp[:, t * RW:(t + 1) * RW], pr[:, t * P:(t + 1) * P], per["ident"][0:RW, 0:RW])
            mm.then_inc(tp_done, 1)
            pe.wait_ge(te_done, 1)
            for b in range(NS):
                pe.wait_ge(v_in[b % 2], 16 * (b // 2 + 1))
                for h in range(MH):
                    n = b * MH + h
                    for t in range(2):
                        mm = pe.matmul(O[:, n:n + 1], vm[:, b % 2, t, h, :], pT[:, t, n:n + 1], start=(t == 0), stop=(t == 1))
                mm.then_inc(o_mm, 1)

        @block.scalar
        def _(act):
            act.wait_ge(a_done, 1)
            act.activation(pr[:], S[0:RW, 0:NMEM], ACT.Exp, bias=sc[:, 1:2], scale=SC, accum_out=sc[:, 2:3]).then_inc(e_done, 1)

        @block.vector
        def _(dve):
            dve.memset(qb[:], 0.0).then_inc(z_done, 1)
            dve.wait_ge(z_done, 1)
            dve.wait_ge(c_in, 16)
            q0 = qb[:].rearrange("p n c -> p (n c)")
            for n in range(RW):
                ins = dve.tensor_copy(q0[:, n * (RP + 1):n * (RP + 1) + 1], qs[:, n % MH, n // MH:n // MH + 1])
            ins.then_inc(qb_done, 1)
            dve.wait_ge(s_mm, NS)
            dve.tensor_reduce(sc[:, 0:1], S[0:RW, 0:NMEM], AX, ALU.max).then_inc(ch, 1)
            dve.wait_ge(ch, 1)
            dve.tensor_scalar(sc[:, 1:2], sc[:, 0:1], -SC, None, ALU.mult).then_inc(a_done, 1)
            dve.wait_ge(e_done, 1)
            dve.reciprocal(sc[:, 3:4], sc[:, 2:3]).then_inc(ch, 1)
            dve.wait_ge(ch, 2)
            dve.tensor_scalar(pr[:], pr[:], sc[:, 3:4], None, ALU.mult).then_inc(p_done, 1)
            dve.wait_ge(tp_done, 1)
            dve.tensor_copy(pT[:].rearrange("p t n -> p (t n)"), tp[:, 0:2 * RW]).then_inc(te_done, 1)
            dve.wait_ge(o_mm, NS)
            dve.tensor_copy(oT[:], O[:, 0:RW].rearrange("p (b h) -> p h b", h=MH)).then_inc(o_done, 1)


def load_split(nc, tag, tiles, hi, lo, cols):
    with ExitStack() as ctx:
        sb, sem = sb_of(nc, ctx, tag), sem_of(nc, ctx, tag)
        raw = sb("raw", [P, 2, cols])
        t_in = [sem("t_in0"), sem("t_in1")]
        hi_done, lo_done = sem("hi_done"), sem("lo_done")
        block = ctx.enter_context(nc.Block())

        @block.sync
        def _(sp):
            clear_last(sp)
            for k, t in enumerate(tiles):
                if k >= 2:
                    sp.wait_ge(lo_done, k - 1)
                sp.dma_start(raw[:, k % 2], t).then_inc(t_in[k % 2], 16)

        @block.scalar
        def _(act):
            for k in range(len(tiles)):
                act.wait_ge(t_in[k % 2], 16 * (k // 2 + 1))
                act.activation(hi[:, k], raw[:, k % 2], ACT.Copy).then_inc(hi_done, 1)

        @block.vector
        def _(dve):
            for k in range(len(tiles)):
                dve.wait_ge(hi_done, k + 1)
                dve.tensor_tensor(lo[:, k], raw[:, k % 2], hi[:, k].bitcast(F32), ALU.subtract).then_inc(lo_done, 1)


def merge(nc, d, x_hi, x_lo):
    with ExitStack() as ctx:
        sb, ps, sem = sb_of(nc, ctx, "mrg"), ps_of(nc, ctx, "mrg"), sem_of(nc, ctx, "mrg")
        raw = sb("raw", [P, 2, KT, P])
        w_hi = sb("w_hi", [P, 2, KT, P], F32R)
        w_lo = sb("w_lo", [P, 2, KT, P], F32R)
        mg = sb("mg", [P, 2, 3, T])
        z = sb("z", [P, 2, T])
        acc = [ps(f"acc{s}", [P, NCH, 512]) for s in range(2)]
        raw_in = [sem("raw_in0"), sem("raw_in1")]
        mg_in = [sem("mg_in0"), sem("mg_in1")]
        z_out = [sem("z_out0"), sem("z_out1")]
        hi_done, lo_done, mm_done, ev_done, sg_done, z_done, ch = (
            sem(x) for x in ("hi_done", "lo_done", "mm_done", "ev_done", "sg_done", "z_done", "ch"))
        block = ctx.enter_context(nc.Block())
        GROUPS = [(0, 0, KT, 0), (1, 0, 4, 8), (1, 4, 4, 12), (2, 0, KT, 0), (3, 0, 4, 8), (3, 4, 4, 12)]
        UNIT_FREE = {0: 3 + 1, 1: 5 + 1, 2: 6 + 0 + 1, 3: 6 + 2 + 1}

        @block.sync
        def _(sp):
            clear_last(sp)
            sp.sem_inc(z_out[0], 16)
            sp.sem_inc(z_out[1], 16)
            sp.sem_inc(z_done, 2)
            for s in range(2):
                sp.dma_start(raw[:, s], d["w_up"][s]).then_inc(raw_in[s], 16)
            with sp.Fori(0, KT // 2) as i:
                for m in range(2):
                    row = [sp.snap(i * 2 + (U_MG + 8 * b + m)) for b in range(3)]
                    sp.wait_ge(z_done, i * 2 + (m + 1))
                    for b in range(3):
                        sp.dma_start(mg[:, m, b], d["z"][bass.ds(row[b], 1)].rearrange("a p n -> p (a n)")).then_inc(mg_in[m], 16)
                for u in range(4):
                    nxt = sp.snap(i * 4 + (u + 2))
                    sp.wait_ge(lo_done, i * 4 + (u + 1))
                    sp.dma_start(raw[:, u % 2], d["w_up"][bass.ds(nxt, 1)].rearrange("a p k n -> p (a k) n")).then_inc(raw_in[u % 2], 16)
                    if u % 2:
                        cur = sp.snap(i * 2 + u // 2)
                        sp.wait_ge(z_done, i * 2 + (u // 2 + 3))
                        sp.dma_start(d["zm"][bass.ds(cur, 1)].rearrange("a p n -> p (a n)"), z[:, u // 2]).then_inc(z_out[u // 2], 16)
            for s in range(2):
                sp.wait_ge(z_out[s], 16 * (KT // 2 + 1))
                sp.wait_ge(raw_in[s], 16 * (KT + 1))

        @block.scalar
        def _(act):
            with act.Fori(0, KT // 2) as i:
                for u in range(4):
                    if u % 2 == 0:
                        m = u // 2
                        act.wait_ge(mg_in[m], i * 48 + 48)
                        act.activation(mg[:, m], mg[:, m], ACT.Sigmoid).then_inc(sg_done, 1)
                    act.wait_ge(raw_in[u % 2], i * 32 + (16 * (u // 2) + 16))
                    act.wait_ge(mm_done, i * 6 + UNIT_FREE[u])
                    act.activation(w_hi[:, u % 2], raw[:, u % 2], ACT.Copy).then_inc(hi_done, 1)

        @block.gpsimd
        def _(pool):
            with pool.Fori(0, KT // 2) as i:
                for u in range(4):
                    pool.wait_ge(hi_done, i * 4 + (u + 1))
                    pool.tensor_tensor(w_lo[:, u % 2], raw[:, u % 2], w_hi[:, u % 2].bitcast(F32), ALU.subtract).then_inc(lo_done, 1)

        @block.tensor
        def _(pe):
            pe.sem_inc(mm_done, 6)
            with pe.Fori(0, KT // 2) as i:
                for g, (u, k0, nk, x0) in enumerate(GROUPS):
                    pe.wait_ge(lo_done, i * 4 + (u + 1))
                    pe.wait_ge(ev_done, i * 6 + (g + 1))
                    for k in range(nk):
                        for n, (w, x) in enumerate(((w_hi, x_hi), (w_hi, x_lo), (w_lo, x_hi))):
                            for c in range(NCH):
                                mm = pe.matmul(acc[g % 2][:, c, 0:CW], w[:, u % 2, k0 + k, :], x[:, x0 + k, c * CW:(c + 1) * CW],
                                               start=(k + n == 0), stop=(k == nk - 1 and n == 2))
                    mm.then_inc(mm_done, 1)

        @block.vector
        def _(dve):
            dve.sem_inc(ev_done, 2)
            with dve.Fori(0, KT // 2) as i:
                for g in range(6):
                    m, b = g // 3, g % 3
                    a = acc[g % 2][:, :, 0:CW]
                    gate = mg[:, m, b].rearrange("p (c n) -> p c n", c=NCH)
                    zz = z[:, m].rearrange("p (c n) -> p c n", c=NCH)
                    if b == 0:
                        dve.wait_ge(sg_done, i * 2 + (m + 1))
                        dve.wait_ge(z_out[m], i * 16 + 16)
                        dve.wait_ge(mm_done, i * 6 + (g + 7))
                        dve.tensor_tensor(zz, a, gate, ALU.mult).then_inc(ev_done, 1)
                    else:
                        dve.wait_ge(mm_done, i * 6 + (g + 7))
                        dve.tensor_tensor(gate, a, gate, ALU.mult).then_inc(ev_done, 1)
                        dve.wait_ge(ev_done, i * 6 + (g + 3))
                        if b == 2:
                            dve.wait_ge(ch, i * 2 + (m + 1))
                        ins = dve.tensor_tensor(zz, zz, gate, ALU.add)
                        ins.then_inc(ch if b == 1 else z_done, 1)


def residual_norm(nc, d, per, h, f_hi, f_lo):
    with ExitStack() as ctx:
        sb, ps, sem = sb_of(nc, ctx, "res"), ps_of(nc, ctx, "res"), sem_of(nc, ctx, "res")
        zo = sb("zo", [P, 2, T])
        sq = sb("sq", [P, 2, T])
        rstd = sb("rstd", [P, T])
        ss = ps("ss", [P, NCH, 512])
        x_in = sem("x_in")
        z_in = [sem("z_in0"), sem("z_in1")]
        h_done, sq_done, ss_done, rt_done, rs_done, n_done, hi_done, lo_done = (
            sem(x) for x in ("h_done", "sq_done", "ss_done", "rt_done", "rs_done", "n_done", "hi_done", "lo_done"))
        block = ctx.enter_context(nc.Block())

        @block.sync
        def _(sp):
            clear_last(sp)
            for k in range(KT):
                sp.dma_start(h[:, k], d["xT"][:, k, 0:T]).then_inc(x_in, 16)
            for k in range(KT):
                if k >= 2:
                    sp.wait_ge(h_done, k - 1)
                sp.dma_start(zo[:, k % 2], d["zo"][k]).then_inc(z_in[k % 2], 16)

        @block.scalar
        def _(act):
            for k in range(KT):
                act.wait_ge(h_done, k + 1)
                if k >= 2:
                    act.wait_ge(ss_done, k - 1)
                act.activation(sq[:, k % 2], h[:, k], ACT.Square).then_inc(sq_done, 1)
            act.wait_ge(ss_done, KT)
            act.activation(rstd[:].rearrange("p (c n) -> p c n", c=NCH), ss[:, :, 0:CW], ACT.Sqrt,
                           bias=per["eps"][:, 0:1], scale=1.0 / D).then_inc(rt_done, 1)
            for k in range(KT):
                act.wait_ge(n_done, k + 1)
                act.activation(f_hi[:, k], sq[:, k % 2], ACT.Copy).then_inc(hi_done, 1)

        @block.tensor
        def _(pe):
            for k in range(KT):
                pe.wait_ge(sq_done, k + 1)
                for c in range(NCH):
                    mm = pe.matmul(ss[:, c, 0:CW], per["ones"][:], sq[:, k % 2, c * CW:(c + 1) * CW],
                                   start=(k == 0), stop=(k == KT - 1))
                mm.then_inc(ss_done, 1)

        @block.vector
        def _(dve):
            dve.wait_ge(x_in, 16 * KT)
            for k in range(KT):
                dve.wait_ge(z_in[k % 2], 16 * (k // 2 + 1))
                dve.tensor_tensor(h[:, k], h[:, k], zo[:, k % 2], ALU.add).then_inc(h_done, 1)
            dve.wait_ge(rt_done, 1)
            dve.reciprocal(rstd[:], rstd[:]).then_inc(rs_done, 1)
            dve.wait_ge(rs_done, 1)
            for k in range(KT):
                if k >= 2:
                    dve.wait_ge(lo_done, k - 1)
                dve.scalar_tensor_tensor(sq[:, k % 2], h[:, k], per["vec"][:, V_FFN + k:V_FFN + k + 1], rstd[:],
                                         ALU.mult, ALU.mult).then_inc(n_done, 1)

        @block.gpsimd
        def _(pool):
            for k in range(KT):
                pool.wait_ge(hi_done, k + 1)
                pool.tensor_tensor(f_lo[:, k], sq[:, k % 2], f_hi[:, k].bitcast(F32), ALU.subtract).then_inc(lo_done, 1)


def ffn(nc, d, h, f_hi, f_lo):
    NG = 20
    with ExitStack() as ctx:
        sb, ps, sem = sb_of(nc, ctx, "ffn"), ps_of(nc, ctx, "ffn"), sem_of(nc, ctx, "ffn")
        raw = sb("raw", [P, 2, KT, P])
        w_hi = sb("w_hi", [P, 2, KT, P], F32R)
        w_lo = sb("w_lo", [P, 2, KT, P], F32R)
        sg = sb("sg", [P, 2, T])
        a = sb("a", [P, 2, T])
        a_hi = sb("a_hi", [P, 2, T], F32R)
        a_lo = sb("a_lo", [P, 2, T], F32R)
        acc = [ps(f"acc{s}", [P, NCH, 512]) for s in range(2)]
        raw_in = [sem("raw_in0"), sem("raw_in1")]
        hi_done, lo_done, mm_done, ev_done, sg_done, ahi_done, alo_done, y_out = (
            sem(x) for x in ("hi_done", "lo_done", "mm_done", "ev_done", "sg_done", "ahi_done", "alo_done", "y_out"))
        block = ctx.enter_context(nc.Block())
        UNIT_FREE = (12, 20, NG + 1, NG + 2, NG + 3, NG + 4)

        @block.sync
        def _(sp):
            clear_last(sp)
            for s in range(2):
                sp.dma_start(raw[:, s], d["w_ff"][s]).then_inc(raw_in[s], 16)
            with sp.Fori(0, FFG) as i:
                for u in range(6):
                    nxt = sp.snap(i * 6 + (u + 2))
                    sp.wait_ge(lo_done, i * 6 + (u + 1))
                    sp.dma_start(raw[:, u % 2], d["w_ff"][bass.ds(nxt, 1)].rearrange("a p k n -> p (a k) n")).then_inc(raw_in[u % 2], 16)
            sp.wait_ge(ev_done, FFG * NG + 2)
            for k in range(KT):
                sp.dma_start(d["yT"][k], h[:, k]).then_inc(y_out, 16)
            sp.wait_ge(y_out, 16 * KT)
            for s in range(2):
                sp.wait_ge(raw_in[s], 16 * (3 * FFG + 1))

        @block.scalar
        def _(act):
            with act.Fori(0, FFG) as i:

                def w_part(u):
                    act.wait_ge(raw_in[u % 2], i * 48 + (16 * (u // 2) + 16))
                    act.wait_ge(mm_done, i * NG + UNIT_FREE[u])
                    act.activation(w_hi[:, u % 2], raw[:, u % 2], ACT.Copy).then_inc(hi_done, 1)

                def sigma(j):
                    act.wait_ge(mm_done, i * NG + (NG + 2 * j + 1))
                    act.activation(sg[:, j].rearrange("p (c n) -> p c n", c=NCH), acc[0][:, :, 0:CW], ACT.Sigmoid).then_inc(sg_done, 1)

                def a_part(j):
                    act.wait_ge(ev_done, i * NG + (2 * j + 4))
                    act.wait_ge(mm_done, i * NG + (12 + 8 * j))
                    act.activation(a_hi[:, j], a[:, j], ACT.Copy).then_inc(ahi_done, 1)

                w_part(0)
                w_part(1)
                sigma(0)
                w_part(2)
                a_part(0)
                w_part(3)
                sigma(1)
                w_part(4)
                a_part(1)
                w_part(5)

        @block.gpsimd
        def _(pool):
            with pool.Fori(0, FFG) as i:

                def w_part(u):
                    pool.wait_ge(hi_done, i * 6 + (u + 1))
                    pool.tensor_tensor(w_lo[:, u % 2], raw[:, u % 2], w_hi[:, u % 2].bitcast(F32), ALU.subtract).then_inc(lo_done, 1)

                def a_part(j):
                    pool.wait_ge(ahi_done, i * 2 + (j + 1))
                    pool.tensor_tensor(a_lo[:, j], a[:, j], a_hi[:, j].bitcast(F32), ALU.subtract).then_inc(alo_done, 1)

                w_part(0)
                w_part(1)
                w_part(2)
                a_part(0)
                w_part(3)
                w_part(4)
                a_part(1)
                w_part(5)

        @block.tensor
        def _(pe):
            pe.sem_inc(mm_done, NG)
            with pe.Fori(0, FFG) as i:
                for u in range(4):
                    pe.wait_ge(lo_done, i * 6 + (u + 1))
                    pe.wait_ge(ev_done, i * NG + (u + 1))
                    for k in range(KT):
                        for n, (w, x) in enumerate(((w_hi, f_hi), (w_hi, f_lo), (w_lo, f_hi))):
                            for c in range(NCH):
                                mm = pe.matmul(acc[u % 2][:, c, 0:CW], w[:, u % 2, k, :], x[:, k, c * CW:(c + 1) * CW],
                                               start=(k + n == 0), stop=(k == KT - 1 and n == 2))
                    mm.then_inc(mm_done, 1)
                for j in range(2):
                    pe.wait_ge(lo_done, i * 6 + (5 + j))
                    pe.wait_ge(alo_done, i * 2 + (j + 1))
                    for m in range(KT):
                        pe.wait_ge(ev_done, i * NG + (4 + 8 * j + m + 1))
                        for n, (w, x) in enumerate(((w_hi, a_hi), (w_hi, a_lo), (w_lo, a_hi))):
                            for c in range(NCH):
                                mm = pe.matmul(acc[m % 2][:, c, 0:CW], w[:, j, m, :], x[:, j, c * CW:(c + 1) * CW],
                                               start=(n == 0), stop=(n == 2))
                        mm.then_inc(mm_done, 1)

        @block.vector
        def _(dve):
            dve.sem_inc(ev_done, 2)
            with dve.Fori(0, FFG) as i:
                for j in range(2):
                    aj = a[:, j].rearrange("p (c n) -> p c n", c=NCH)
                    dve.wait_ge(sg_done, i * 2 + (j + 1))
                    dve.wait_ge(mm_done, i * NG + (12 + 8 * j))
                    dve.tensor_tensor(aj, acc[0][:, :, 0:CW], sg[:, j].rearrange("p (c n) -> p c n", c=NCH), ALU.mult).then_inc(ev_done, 1)
                    dve.wait_ge(ev_done, i * NG + (2 * j + 3))
                    dve.wait_ge(mm_done, i * NG + (NG + 2 * j + 2))
                    dve.tensor_tensor(aj, acc[1][:, :, 0:CW], aj, ALU.mult).then_inc(ev_done, 1)
                for g in range(16):
                    m = g % 8
                    dve.wait_ge(mm_done, i * NG + (NG + 5 + g))
                    hm = h[:, m].rearrange("p (c n) -> p c n", c=NCH)
                    dve.tensor_tensor(hm, acc[m % 2][:, :, 0:CW], hm, ALU.add).then_inc(ev_done, 1)


def outputs(nc, d):
    with ExitStack() as ctx:
        sem = sem_of(nc, ctx, "out")
        o = sem("o")
        block = ctx.enter_context(nc.Block())

        @block.sync
        def _(sp):
            clear_last(sp)
            for n, src in enumerate((d["z"][U_CMPK], d["z"][U_CMPV], d["zn"][0], d["z"][U_SELV], d["zn"][1], d["z"][U_WINV])):
                sp.dma_start(d["kvT"][n], src).then_inc(o, 16)
            for h in range(MH):
                sp.dma_start(d["memT"][h], d["memn"][h]).then_inc(o, 16)
                sp.dma_start(d["memT"][MH + h], d["memz"][MH + h]).then_inc(o, 16)
            for b in range(NS):
                sp.dma_start(d["win_out"][b, 0:WIN - 1], d["win_in"][b, 1:WIN]).then_inc(o, 16)
            for j, src in enumerate((d["zn"][1], d["z"][U_WINV])):
                sp.dma_start(d["win_out"][:, WIN - 1, j * P:(j + 1) * P].rearrange("b p -> p b"), src[:, NP_:T],
                             allow_slow_non_contiguous=True).then_inc(o, 16)
            sp.wait_ge(o, 16 * 24)


def program(nc, d):
    PHASE_SEMS["last"], PHASE_SEMS["now"] = [], []
    scratch = lambda name, shape: nc.dram_tensor(name, shape, F32, kind="Internal").ap()
    d["z"] = scratch("z", [NU_IN, P, T])
    d["zn"] = scratch("zn", [NHN, P, T])
    d["memz"] = scratch("memz", [2 * MH, P, NMEM])
    d["memn"] = scratch("memn", [MH, P, NMEM])
    d["gate_s"] = scratch("gate_s", [NS * 24, 1])
    d["vtok"] = scratch("vtok", [2, QT, P, P])
    d["memv"] = scratch("memv", [MH, 2, P, P])
    d["o_lru"] = scratch("o_lru", [KT, P, T])
    d["o_nsa"] = scratch("o_nsa", [R, P, T])
    d["o_mem"] = scratch("o_mem", [MH, P, T])
    d["zm"] = scratch("zm", [KT, P, T])
    d["zo"] = scratch("zo", [KT, P, T])
    d["dist"] = scratch("dist", [P, 8, RLEN])
    d["kcT"] = scratch("kcT", [P, (NS + 1) * NCK])
    d["vc"] = scratch("vc", [NCK, NS + 1, P])
    with ExitStack() as ctx:
        sb = sb_of(nc, ctx, "per")
        per = {"ident": sb("ident", [P, P]), "ones": sb("ones", [P, P]), "vec": sb("vec", [P, NV]), "eps": sb("eps", [P, 1]),
               "gate": sb("gate", [P, QT, 24])}
        with ExitStack() as part:
            sbh = sb_of(nc, part, "h")
            h_hi, h_lo = sbh("hi", [P, KT, XC], F32R), sbh("lo", [P, KT, XC], F32R)
            normalise(nc, d, per, h_hi, h_lo)
            project(nc, "pin", d["w_in"], U_LX, h_hi, h_lo, 0, NCH, CW, d["z"])
            project(nc, "pmem", d["w_mem"], 2 * MH, h_hi, h_lo, T, 1, NMEM, d["memz"])
            gates(nc, d, per, h_hi, h_lo)
            head_norm(nc, "hn", d, d["z"], U_SELK, NHN, T, NCH, d["mats"], d["gains"], d["zn"])
            head_norm(nc, "hm", d, d["memz"], 0, MH, NMEM, 1, d["mats_m"], d["gains_m"], d["memn"])
            to_tokens(nc, "tv", per, d["z"], U_SELV, 2, NP_, d["vtok"])
            to_tokens(nc, "tm", per, d["memz"], MH, MH, NMEM, d["memv"])
            outputs(nc, d)
            distance_bias(nc, d)
            compress(nc, d, per)
            prompt_attention(nc, d, per, h_hi, h_lo)
            merge_gates_and_recurrence(nc, d, h_hi, h_lo)
        memory_attention(nc, d, per)
        sample_attention(nc, d, per)
        sample_memory(nc, d, per)
        with ExitStack() as part:
            sbx = sb_of(nc, part, "x")
            x_hi, x_lo = sbx("hi", [P, 16, T], F32R), sbx("lo", [P, 16, T], F32R)
            load_split(nc, "lsx", [d["o_lru"][k] for k in range(8)] + [d["o_nsa"][k] for k in range(4)]
                       + [d["o_mem"][k] for k in range(4)], x_hi, x_lo, T)
            merge(nc, d, x_hi, x_lo)
        with ExitStack() as part:
            sbx = sb_of(nc, part, "m")
            x_hi, x_lo = sbx("hi", [P, KT, T], F32R), sbx("lo", [P, KT, T], F32R)
            load_split(nc, "lsm", [d["zm"][k] for k in range(8)], x_hi, x_lo, T)
            project(nc, "pwo", d["w_o"], KT, x_hi, x_lo, 0, NCH, CW, d["zo"])
        with ExitStack() as part:
            sbx = sb_of(nc, part, "f")
            h = sbx("h", [P, KT, T])
            f_hi, f_lo = sbx("hi", [P, KT, T], F32R), sbx("lo", [P, KT, T], F32R)
            residual_norm(nc, d, per, h, f_hi, f_lo)
            ffn(nc, d, h, f_hi, f_lo)



def _bucket(n):
    if n < 16:
        return n
    return min(31, 16 + int(math.log(n / 16) / math.log(8) * 16 + 1e-9))


def _constants():
    f = np.float32
    hot = np.zeros((33, RLEN), f)
    for i in range(RLEN):
        dist = RMAX - i
        if dist < 0:
            hot[32, i] = NEGV
        else:
            hot[_bucket(dist), i] += 1
            hot[31, i] -= 1
    blk64 = np.kron(np.eye(2, dtype=f), np.ones((HD, HD), f))
    one = np.ones((P, P), f)

    def mat(m, eps):
        return np.concatenate([m, np.full((P, 1), eps, f)], 1)

    qi, xi, ui = np.arange(P)[:, None], np.arange(P)[None, :], np.arange(CU)[None, :]
    return {
        "ident": np.eye(P, dtype=f), "ones": one, "hot": hot,
        "mats": np.stack([mat(blk64 / 64, EPS)] * 2 + [mat(blk64, 64 * EPS)] * 4 + [mat(one / 128, EPS)] * 4),
        "mats_m": np.stack([mat(one / 128, EPS)] * 4),
        "avg": mat(blk64 / 64, EPS),
        "wmask": np.where(xi > qi, 0, NEGV).astype(f),
        "cmask": (qi >= 16 * (ui - 56) + 31).astype(f),
        "grp": np.kron(np.eye(16, dtype=f), np.ones((4, 4), f)),
        "blk": np.tile(np.arange(1, 17, dtype=f), (64, 1)),
    }


def _layout(x):
    x = {k: np.asarray(v) for k, v in x.items()}
    c = _constants()

    def fm(a):
        return a.T.reshape(-1, P, a.shape[0]).transpose(1, 0, 2)

    def units(w, cols=None):
        w = w if cols is None else w[:, cols]
        return w.reshape(-1, P, w.shape[1] // P, P).transpose(2, 1, 0, 3)

    def cols8(v):
        return v.reshape(-1, P).T

    w_in = x["w_in"][0]
    zero = np.zeros((2, P, KT, P), np.float32)
    starts = [2560, 2688, 2944, 3200, 2816, 3072]
    cols = [np.arange(s, s + P) for s in starts]
    cols += [np.concatenate([2048 + r * HD + np.arange(HD), 2048 + (R + r) * HD + np.arange(HD)]) for r in range(R)]
    cols += [np.arange(3352 + P * h, 3352 + P * (h + 1)) for h in range(MH)]
    cols += [np.arange(P * m, P * (m + 1)) for m in range(16)]
    cols += [np.arange(3864 + P * m, 3864 + P * (m + 1)) for m in range(24)]
    order = np.concatenate([np.concatenate([r * HD + np.arange(HD), (R + r) * HD + np.arange(HD)]) for r in range(R)])
    ua, ub, um = units(x["w_up_a"][0]), units(x["w_up_b"][0][order]), units(x["w_up_m"][0])
    ubm = np.concatenate([ub, um], 2)
    w_up = np.concatenate([np.stack([ua, ubm], 1).reshape(16, P, KT, P), zero])
    gu = np.stack([units(x["w_ffn_gate"][0]), units(x["w_ffn_up"][0])], 1).reshape(FFG, 4, P, KT, P)
    dn = x["w_ffn_down"][0].reshape(FFG, 2, P, KT, P)
    w_ff = np.concatenate([np.concatenate([gu, dn], 1).reshape(6 * FFG, P, KT, P), zero])
    dup = lambda g: np.concatenate([g, g])[:, None]
    gk = x["g_nsa_k"][0]
    gq, gm = dup(x["g_nsa_q"][0]), x["g_mem_q"][0][:, None]
    pool = x["cache_cmp_kv"][0]
    npool = pool.shape[0]
    sel = x["cache_sel_kv"][0].reshape(npool, P, 2, P)
    win = x["cache_win_kv"][0]
    wk = win.reshape(NS, WIN, 2, P)
    mem = x["cache_mem_kv"][0]
    out = {
        "xT": np.concatenate([fm(x["x_prompt"][0]), fm(x["x_sample"][:, 0]), fm(x["mem_prompt"][0])], 2),
        "vec": np.concatenate([cols8(x["norm_mix"][0]), cols8(x["norm_mem"][0]), cols8(x["norm_ffn"][0]),
                               x["g_mem_k"][0][:, None], cols8(x["pe_cmp_k"][0]), cols8(x["pe_cmp_v"][0])], 1),
        "w_in": np.concatenate([units(w_in, np.concatenate(cols)), zero]), "w_mem": units(x["w_mem_kv"][0]),
        "w_ng": w_in[:, 3328:3352].reshape(KT, P, 24).transpose(1, 0, 2),
        "gains": np.stack([dup(gk[1]), dup(gk[2])] + [gq] * 4 + [gm] * 4),
        "gains_m": np.stack([x["g_mem_k"][0][:, None]] * 4),
        "nm_kc": np.concatenate([c.pop("avg"), dup(gk[0])], 1),
        "rel": np.concatenate([np.repeat(x["rel_bias"][:, :, None], P, 2), np.ones((1, 8, P), np.float32)]),
        "st": np.concatenate([x["state_conv"][0].transpose(2, 1, 0).reshape(KT, P, 3 * NS).transpose(1, 0, 2),
                              fm(x["state_lru_h"][0])], 2),
        "par": np.stack([cols8(v) for v in (*x["conv_w"][0], x["conv_b"][0], x["b_lru_a"][0], x["b_lru_i"][0],
                                            x["lru_lambda"][0])], 2),
        "w_a": x["w_lru_a"][0].reshape(4, 2, P, 256).transpose(0, 2, 1, 3),
        "w_i": x["w_lru_i"][0].reshape(4, 2, P, 256).transpose(0, 2, 1, 3),
        "w_c1": np.stack([x["w_cmp_k1"][0], x["w_cmp_v1"][0]]).reshape(2, 16, P, P).transpose(0, 2, 1, 3),
        "w_c2": np.stack([x["w_cmp_k2"][0], x["w_cmp_v2"][0]]),
        "cmp_pool": pool.reshape(npool, 8, 8, 2, 2, 2, HD).transpose(0, 3, 6, 4, 5, 2, 1).reshape(npool, P, 256),
        "sel_kT": sel[:, :, 0].transpose(0, 2, 1), "sel_v": sel[:, :, 1],
        "winkT": wk[:, :, 0].transpose(0, 2, 1), "win_v": wk[:, :, 1].reshape(NS, WIN // P, P, P),
        "win_in": win.reshape(NS, WIN, 256),
        "mem_kT": mem[:, :, 0].transpose(0, 3, 2, 1), "mem_v": mem[:, :, 1].reshape(NS, 2, P, MH, P),
        "page_table": x["page_table"].reshape(1, NS * PAGES),
        "w_up": w_up, "w_o": units(x["w_o"][0]), "w_ff": w_ff,
    }
    out.update(c)
    return {k: np.ascontiguousarray(v) for k, v in out.items()}


_OUTS = {"yT": (KT, P, T), "kvT": (6, P, T), "memT": (2 * MH, P, NMEM), "win_out": (NS, WIN, 256),
         "hT": (KT, P, 1 + NS), "cvT": (KT, P, 3), "cvsT": (KT, P, 3 * NS)}


def kernel(**inputs):
    import concourse.bacc as _bacc
    from concourse.bass_utils import run_bass_kernel_spmd as _run

    nc = _bacc.Bacc("TRN2", target_bir_lowering=False, num_devices=1)
    arrays, d = {}, {}
    for name, a in _layout(inputs).items():
        arrays[f"in_{name}"] = a
        d[name] = nc.dram_tensor(f"in_{name}", a.shape, mybir.dt.from_np(a.dtype), kind="ExternalInput").ap()
    for name, shape in _OUTS.items():
        d[name] = nc.dram_tensor(f"out_{name}", shape, F32, kind="ExternalOutput").ap()
    program(nc, d)
    r = _run(nc, [arrays], core_ids=[0]).results[0]
    got = {name: np.asarray(r[f"out_{name}"]) for name in _OUTS}

    y = got["yT"].reshape(D, T).T
    kv = got["kvT"].reshape(3, 2, P, T).transpose(0, 3, 1, 2).reshape(3, T, 2, G, HD)
    mem = got["memT"].reshape(2, MH, P, NMEM).transpose(3, 0, 1, 2)
    h = got["hT"].reshape(D, 1 + NS).T
    cv = got["cvT"].reshape(D, 3).T
    cvs = got["cvsT"].reshape(D, 3, NS).transpose(2, 1, 0)
    res = (y[None, :NP_], y[NP_:, None], kv[0][None, None, :NP_], kv[0][None, NP_:, None],
           kv[1][None, None, :NP_], kv[1][None, NP_:, None], kv[2][None, None, NP_ - WIN:NP_],
           got["win_out"].reshape(1, NS, WIN, 2, G, HD), mem[None, None], h[None, 0:1], h[None, 1:], cv[None, None], cvs[None])
    return tuple(np.ascontiguousarray(a) for a in res)
```

```python
from contextlib import ExitStack
import math

import numpy as np
import concourse.bass as bass
from concourse import mybir

F32 = mybir.dt.float32
F32R = mybir.dt.float32r
I32 = mybir.dt.int32
ACT = mybir.ActivationFunctionType
ALU = mybir.AluOpType
AX = mybir.AxisListType.X

P = 128
D = 1024
KT = D // P
NP_ = 1024
NS = 8
T = NP_ + NS
NCH, CW = 3, T // 3
NMEM = 256
XC = T + NMEM
G, R, HD = 2, 4, 64
MH = 4
QT = NP_ // P
PAGES = 8
NCMP = 63
NCK = 64
WIN = 512
FFG = 11
EPS = 1e-6
NEGV = -1e30
RLEN, RMAX = 512, 360
CU = 120

U_CMPK, U_CMPV, U_SELV, U_WINV, U_SELK, U_WINK, U_Q, U_MQ, U_LX, U_LG, U_MG = 0, 1, 2, 3, 4, 5, 6, 10, 14, 22, 30
NU_IN = 54
NHN = 10
V_MIX, V_MEM, V_FFN, V_GMK, V_PEK, V_PEV, NV = 0, 8, 16, 24, 25, 41, 57
L_CW, L_CB, L_BA, L_BI, L_LAM, NL = 0, 4, 5, 6, 7, 8


def sb_of(nc, ctx, tag):
    return lambda name, shape, dt=F32: ctx.enter_context(nc.sbuf_tensor(f"{tag}_{name}", shape, dt))


def ps_of(nc, ctx, tag):
    return lambda name, shape: ctx.enter_context(nc.psum_tensor(f"{tag}_{name}", shape, F32))


PHASE_SEMS = {"last": [], "now": []}


def sem_of(nc, ctx, tag, new_phase=True):
    if new_phase:
        PHASE_SEMS["last"], PHASE_SEMS["now"] = PHASE_SEMS["now"], []

    def sem(name):
        s = ctx.enter_context(nc.semaphore(f"{tag}_{name}"))
        PHASE_SEMS["now"].append(s)
        return s

    return sem


def clear_last(sp):
    for s in PHASE_SEMS["last"]:
        sp.sem_clear(s)


def start_phase(nc, ctx, block, tag):
    sem_of(nc, ctx, tag)

    @block.sync
    def _(sp):
        clear_last(sp)


def normalise(nc, d, per, ctx, block, bank, h_hi, h_lo):
    sb, sem = sb_of(nc, ctx, "nrm"), sem_of(nc, ctx, "nrm", new_phase=False)
    x = sb("x", [P, KT, XC])
    sq = sb("sq", [P, 2, XC])
    rstd = sb("rstd", [P, XC])
    nrm = sq
    ss = bank[:, 0:4]
    w = XC // 4
    x_in = [sem(f"x_in{k}") for k in range(KT)]
    c_in, sq_done, ss_done = sem("c_in"), sem("sq_done"), sem("ss_done")
    rt_done, rs_done, n_done, hi_done, lo_done = (sem("rt_done"), sem("rs_done"), sem("n_done"),
                                                  sem("hi_done"), sem("lo_done"))
    eps_done = sem("eps_done")

    @block.sync
    def _(sp):
        sp.dma_start(per["ones"][:], d["ones"]).then_inc(c_in, 16)
        sp.dma_start(per["vec"][:], d["vec"]).then_inc(c_in, 16)
        for k in range(KT):
            sp.dma_start(x[:, k, :], d["xT"][:, k, :]).then_inc(x_in[k], 16)
        sp.dma_start(per["ident"][:], d["ident"]).then_inc(c_in, 16)
        sp.wait_ge(c_in, 48)

    @block.scalar
    def _(act):
        for k in range(KT):
            act.wait_ge(x_in[k], 16)
            if k >= 2:
                act.wait_ge(ss_done, k - 1)
            act.activation(sq[:, k % 2, :], x[:, k, :], ACT.Square).then_inc(sq_done, 1)
        act.wait_ge(ss_done, KT)
        act.wait_ge(eps_done, 1)
        act.activation(rstd[:].rearrange("p (c n) -> p c n", c=4), ss[:, :, 0:w], ACT.Sqrt,
                       bias=per["eps"][:, 0:1], scale=1.0 / D).then_inc(rt_done, 1)
        for k in range(KT):
            act.wait_ge(n_done, 2 * k + 2)
            act.activation(h_hi[:, k, :], nrm[:, k % 2, :], ACT.Copy).then_inc(hi_done, 1)

    @block.tensor
    def _(pe):
        pe.wait_ge(c_in, 32)
        for k in range(KT):
            pe.wait_ge(sq_done, k + 1)
            for c in range(4):
                mm = pe.matmul(ss[:, c, 0:w], per["ones"][:], sq[:, k % 2, c * w:c * w + w],
                               start=(k == 0), stop=(k == KT - 1))
            mm.then_inc(ss_done, 1)

    @block.vector
    def _(dve):
        dve.memset(per["eps"][:], EPS).then_inc(eps_done, 1)
        dve.wait_ge(rt_done, 1)
        dve.reciprocal(rstd[:], rstd[:]).then_inc(rs_done, 1)
        dve.wait_ge(rs_done, 1)
        dve.wait_ge(c_in, 32)
        for k in range(KT):
            dve.wait_ge(x_in[k], 16)
        for k in range(KT):
            if k >= 2:
                dve.wait_ge(lo_done, k - 1)
            dve.scalar_tensor_tensor(nrm[:, k % 2, 0:T], x[:, k, 0:T], per["vec"][:, V_MIX + k:V_MIX + k + 1],
                                     rstd[:, 0:T], ALU.mult, ALU.mult).then_inc(n_done, 1)
            dve.scalar_tensor_tensor(nrm[:, k % 2, T:XC], x[:, k, T:XC], per["vec"][:, V_MEM + k:V_MEM + k + 1],
                                     rstd[:, T:XC], ALU.mult, ALU.mult).then_inc(n_done, 1)

    @block.gpsimd
    def _(pool):
        for k in range(KT):
            pool.wait_ge(hi_done, k + 1)
            pool.tensor_tensor(h_lo[:, k, :], nrm[:, k % 2, :], h_hi[:, k, :].bitcast(F32),
                               ALU.subtract).then_inc(lo_done, 1)

    return lambda pe, k: pe.wait_ge(lo_done, k + 1)


def project(nc, tag, ctx, block, units, n_units, h_hi, h_lo, col, chunks, cw, out, acc, make_h):
    cols = chunks * cw
    sb, sem = sb_of(nc, ctx, tag), sem_of(nc, ctx, tag, new_phase=False)
    raw = sb("raw", [P, 2, KT, P])
    w_hi = sb("w_hi", [P, 2, KT, P], F32R)
    w_lo = sb("w_lo", [P, 2, KT, P], F32R)
    z = sb("z", [P, 2, cols])
    raw_in = [sem("raw_in0"), sem("raw_in1")]
    z_out = [sem("z_out0"), sem("z_out1")]
    hi_done, lo_done, mm_done, ev_done = sem("hi_done"), sem("lo_done"), sem("mm_done"), sem("ev_done")
    pairs = n_units // 2

    def lo_part(pool, s):
        pool.tensor_tensor(w_lo[:, s], raw[:, s], w_hi[:, s].bitcast(F32), ALU.subtract).then_inc(lo_done, 1)

    @block.sync
    def _(sp):
        sp.sem_inc(ev_done, 2)
        for s in range(2):
            sp.dma_start(raw[:, s], units[s]).then_inc(raw_in[s], 16)

    @block.scalar
    def _(act):
        for s in range(2):
            act.wait_ge(raw_in[s], 16)
            act.activation(w_hi[:, s], raw[:, s], ACT.Copy).then_inc(hi_done, 1)

    @block.gpsimd
    def _(pool):
        for s in range(2):
            pool.wait_ge(hi_done, s + 1)
            lo_part(pool, s)

    ready = make_h()

    @block.sync
    def _(sp):
        sp.sem_inc(z_out[0], 16)
        sp.sem_inc(z_out[1], 16)

        def store(s, row, n):
            sp.wait_ge(ev_done, n + 2)
            sp.dma_start(out[row], z[:, s]).then_inc(z_out[s], 16)

        with sp.Fori(0, pairs - 1) as i:
            for s in range(2):
                nxt = sp.snap(i * 2 + (s + 2))
                cur = sp.snap(i * 2 + s)
                sp.wait_ge(lo_done, i * 2 + (s + 1))
                sp.dma_start(raw[:, s], units[bass.ds(nxt, 1)].rearrange("a p k m -> p (a k) m")).then_inc(raw_in[s], 16)
                sp.wait_ge(ev_done, i * 2 + (s + 3))
                sp.dma_start(out[bass.ds(cur, 1)].rearrange("a p n -> p (a n)"), z[:, s]).then_inc(z_out[s], 16)
        for s in range(2):
            store(s, n_units - 2 + s, n_units - 1 + s)
        for s in range(2):
            sp.wait_ge(z_out[s], 16 * (pairs + 1))

    @block.scalar
    def _(act):
        with act.Fori(0, pairs - 1) as i:
            for s in range(2):
                act.wait_ge(raw_in[s], i * 16 + 32)
                act.wait_ge(mm_done, i * 2 + (s + 1))
                act.activation(w_hi[:, s], raw[:, s], ACT.Copy).then_inc(hi_done, 1)

    @block.gpsimd
    def _(pool):
        with pool.Fori(0, pairs - 1) as i:
            for s in range(2):
                pool.wait_ge(hi_done, i * 2 + (s + 3))
                lo_part(pool, s)

    @block.tensor
    def _(pe):
        with pe.Fori(0, pairs) as i:
            for s in range(2):
                pe.wait_ge(lo_done, i * 2 + (s + 1))
                pe.wait_ge(ev_done, i * 2 + (s + 1))
                for k in range(KT):
                    ready(pe, k)
                    for n, (w, h) in enumerate(((w_hi, h_hi), (w_hi, h_lo), (w_lo, h_hi))):
                        for c in range(chunks):
                            mm = pe.matmul(acc[s][:, c, 0:cw], w[:, s, k, :],
                                           h[:, k, col + c * cw:col + (c + 1) * cw],
                                           start=(k + n == 0), stop=(k == KT - 1 and n == 2))
                mm.then_inc(mm_done, 1)

    @block.vector
    def _(dve):
        with dve.Fori(0, pairs) as i:
            for s in range(2):
                dve.wait_ge(z_out[s], i * 16 + 16)
                dve.wait_ge(mm_done, i * 2 + (s + 1))
                dve.tensor_copy(z[:, s].rearrange("p (c n) -> p c n", c=chunks), acc[s][:, :, 0:cw]).then_inc(ev_done, 1)


def gates(nc, d, per, ctx, block, bank, soft, h_hi, h_lo):
    NGT = 24
    sb, sem = sb_of(nc, ctx, "gat"), sem_of(nc, ctx, "gat", new_phase=False)
    raw = sb("raw", [P, KT, NGT])
    hi = sb("hi", [P, KT, NGT], F32R)
    lo = sb("lo", [P, KT, NGT], F32R)
    gf = sb("gf", [P, T])
    gs = sb("gs", [NS, NGT])
    acc = bank[:, 0:3]
    tp = bank[:, 3, 0:32 * (QT + 1)].rearrange("p (t n) -> p t n", n=32)
    w_in, g_out = soft
    hi_done, lo_done, mm_done, sig_done, tp_done, ev_done, z_done = (
        sem(x) for x in ("hi_done", "lo_done", "mm_done", "sig_done", "tp_done", "ev_done", "z_done"))

    @block.gpsimd
    def _(pool):
        pool.dma_start(raw[:], d["w_ng"]).then_inc(w_in, 16)
        pool.wait_ge(ev_done, 2)
        pool.dma_start(d["gate_s"].rearrange("(b n) c -> b (n c)", b=NS), gs[:]).then_inc(g_out, 16)
        pool.wait_ge(g_out, 16)

    @block.vector
    def _(dve):
        dve.memset(gf[:], 0.0).then_inc(z_done, 1)
        dve.wait_ge(w_in, 16)
        dve.tensor_copy(hi[:], raw[:]).then_inc(hi_done, 1)
        dve.wait_ge(hi_done, 1)
        dve.tensor_tensor(lo[:], raw[:], hi[:].bitcast(F32), ALU.subtract).then_inc(lo_done, 1)
        dve.wait_ge(tp_done, 1)
        dve.tensor_copy(per["gate"][:], tp[:, 0:QT, 0:NGT]).then_inc(ev_done, 1)
        dve.tensor_copy(gs[:], tp[0:NS, QT, 0:NGT]).then_inc(ev_done, 1)

    @block.tensor
    def _(pe):
        pe.wait_ge(lo_done, 1)
        for k in range(KT):
            for n, (w, h) in enumerate(((hi, h_hi), (hi, h_lo), (lo, h_hi))):
                for c in range(NCH):
                    mm = pe.matmul(acc[0:NGT, c, 0:CW], w[:, k, :], h[:, k, c * CW:(c + 1) * CW],
                                   start=(k + n == 0), stop=(k == KT - 1 and n == 2))
        mm.then_inc(mm_done, 1)
        pe.wait_ge(sig_done, 1)
        for t in range(QT + 1):
            m = P if t < QT else NS
            mm = pe.transpose(tp[0:m, t, :], gf[0:32, t * P:t * P + m], per["ident"][0:32, 0:32])
        mm.then_inc(tp_done, 1)

    @block.scalar
    def _(act):
        act.wait_ge(z_done, 1)
        act.wait_ge(mm_done, 1)
        act.activation(gf[0:NGT].rearrange("p (c n) -> p c n", c=NCH), acc[0:NGT, :, 0:CW], ACT.Sigmoid).then_inc(sig_done, 1)

    return lambda pe: pe.wait_ge(ev_done, 2)


def head_norm(nc, tag, ctx, block, ms, src, row0, n, cols, chunks, mats, gains, dst):
    cw = cols // chunks
    sb, sem = sb_of(nc, ctx, tag), sem_of(nc, ctx, tag, new_phase=False)
    z = sb("z", [P, 2, cols])
    m = sb("m", [P, 2, P + 1])
    g = sb("g", [P, 2, 1])
    sq = sb("sq", [P, 2, cols])
    o = sb("o", [P, 2, cols])
    t_in = [sem("t_in0"), sem("t_in1")]
    t_out = [sem("t_out0"), sem("t_out1")]
    sq_done, mm_done, rt_done, rc_done, n_done = sem("sq_done"), sem("mm_done"), sem("rt_done"), sem("rc_done"), sem("n_done")

    @block.sync
    def _(sp):
        sp.sem_inc(t_out[0], 16)
        sp.sem_inc(t_out[1], 16)
        def load(j, jr, s):
            sp.dma_start(z[:, s], src[bass.ds(jr, 1)].rearrange("a p n -> p (a n)")).then_inc(t_in[s], 16)
            sp.dma_start(m[:, s], mats[bass.ds(j, 1)].rearrange("a p n -> p (a n)")).then_inc(t_in[s], 16)
            sp.dma_start(g[:, s], gains[bass.ds(j, 1)].rearrange("a p n -> p (a n)")).then_inc(t_in[s], 16)

        for s in range(2):
            load(s, row0 + s, s)
        with sp.Fori(0, n // 2 - 1) as i:
            for s in range(2):
                last, nxt, row = sp.snap(i * 2 + s), sp.snap(i * 2 + (s + 2)), sp.snap(i * 2 + (s + 2 + row0))
                sp.wait_ge(n_done, i * 2 + (s + 1))
                sp.dma_start(dst[bass.ds(last, 1)].rearrange("a p n -> p (a n)"), o[:, s]).then_inc(t_out[s], 16)
                load(nxt, row, s)
        for s in range(2):
            sp.wait_ge(n_done, n - 1 + s)
            sp.dma_start(dst[n - 2 + s], o[:, s]).then_inc(t_out[s], 16)
        for s in range(2):
            sp.wait_ge(t_out[s], 16 * (n // 2 + 1))

    @block.scalar
    def _(act):
        with act.Fori(0, n // 2) as i:
            for s in range(2):
                act.wait_ge(t_in[s], i * 48 + 48)
                act.activation(sq[:, s], z[:, s], ACT.Square).then_inc(sq_done, 1)
                act.wait_ge(mm_done, i * 2 + (s + 1))
                act.activation(sq[:, s].rearrange("p (c n) -> p c n", c=chunks), ms[s][:, :, 0:cw], ACT.Sqrt,
                               bias=m[:, s, P:P + 1]).then_inc(rt_done, 1)

    @block.tensor
    def _(pe):
        with pe.Fori(0, n // 2) as i:
            for s in range(2):
                pe.wait_ge(sq_done, i * 2 + (s + 1))
                for c in range(chunks):
                    mm = pe.matmul(ms[s][:, c, 0:cw], m[:, s, 0:P], sq[:, s, c * cw:(c + 1) * cw], start=True, stop=True)
                mm.then_inc(mm_done, 1)

    @block.vector
    def _(dve):
        with dve.Fori(0, n // 2) as i:
            for s in range(2):
                dve.wait_ge(rt_done, i * 2 + (s + 1))
                dve.reciprocal(sq[:, s], sq[:, s]).then_inc(rc_done, 1)
                dve.wait_ge(t_out[s], i * 16 + 16)
                dve.wait_ge(rc_done, i * 2 + (s + 1))
                dve.scalar_tensor_tensor(o[:, s], z[:, s], g[:, s], sq[:, s], ALU.mult, ALU.mult).then_inc(n_done, 1)

    return lambda pe: pe.wait_ge(rt_done, n)


def to_tokens(nc, tag, per, ctx, block, tp, soft, src, row0, n, cols, dst):
    nt = cols // P
    sb, sem = sb_of(nc, ctx, tag), sem_of(nc, ctx, tag, new_phase=False)
    z = sb("z", [P, 2, cols])
    o = sb("o", [P, 2, cols])
    t_in, t_out = soft[0:2], soft[2:4]
    tp_done, ev_done = sem("tp_done"), sem("ev_done")

    def store(pool, j):
        pool.wait_ge(ev_done, j + 1)
        pool.dma_start(dst[j].rearrange("t p n -> p t n"), o[:, j % 2].rearrange("p (t n) -> p t n", n=P)).then_inc(t_out[j % 2], 16)

    @block.gpsimd
    def _(pool):
        for j in range(n):
            s = j % 2
            if j >= 2:
                pool.wait_ge(tp_done, j - 1)
            pool.dma_start(z[:, s], src[row0 + j][:, 0:cols]).then_inc(t_in[s], 16)
            if j >= 1:
                store(pool, j - 1)
        store(pool, n - 1)
        for s in range(2):
            pool.wait_ge(t_out[s], 16 * ((n - s + 1) // 2))

    @block.tensor
    def _(pe):
        for j in range(n):
            s = j % 2
            pe.wait_ge(t_in[s], 16 * (j // 2 + 1))
            if j >= 2:
                pe.wait_ge(ev_done, j - 1)
            for t in range(nt):
                mm = pe.transpose(tp[s][:, t, :], z[:, s, t * P:(t + 1) * P], per["ident"][:])
            mm.then_inc(tp_done, 1)

    @block.vector
    def _(dve):
        for j in range(n):
            s = j % 2
            dve.wait_ge(tp_done, j + 1)
            if j >= 2:
                dve.wait_ge(t_out[s], 16 * (j // 2))
            dve.tensor_copy(o[:, s].rearrange("p (t n) -> p t n", n=P), tp[s][:]).then_inc(ev_done, 1)


def merge_gates_and_recurrence(nc, d, h_hi, h_lo):
    CWD = 4
    NBLK = 4
    NU = (NU_IN - U_MG) // NBLK
    with ExitStack() as ctx:
        sb, ps, sem = sb_of(nc, ctx, "lru"), ps_of(nc, ctx, "lru"), sem_of(nc, ctx, "lru")
        raw = sb("raw", [P, 2, KT, P])
        w_hi = sb("w_hi", [P, 2, KT, P], F32R)
        w_lo = sb("w_lo", [P, 2, KT, P], F32R)
        z = sb("z", [P, 2, T])
        acc = [ps(f"acc{s}", [P, NCH, 512]) for s in range(2)]
        raw_in = [sem("raw_in0"), sem("raw_in1")]
        z_out = [sem("z_out0"), sem("z_out1")]
        hi_done, lo_done, mm_done, ev_done = sem("hi_done"), sem("lo_done"), sem("mm_done"), sem("ev_done")

        xp = sb("xp", [P, 2, CWD - 1 + T])
        st = sb("st", [P, 2, 4 * NS])
        par = sb("par", [P, 2, NL])
        wa = sb("wa", [P, 2, 256])
        wi = sb("wi", [P, 2, 256])
        gate = sb("gate", [P, 2, T])
        xc = sb("xc", [P, 2, T])
        r = sb("r", [P, 2, T])
        ig = sb("ig", [P, 2, T])
        a = sb("a", [P, 2, T])
        th = sb("th", [P, 2, T])
        h = sb("h", [P, 2, T])
        lam = sb("lam", [P, 8, 2])
        ps_r = ps("ps_r", [P, 512])
        ps_i = ps("ps_i", [P, 512])
        b_in, b_out, pad_done, ch, xc_done, gm_done, sig_done, lam_done, ex_done, act_done, sq_in, rt_done, o_done = (
            sem(x) for x in ("b_in", "b_out", "pad_done", "ch", "xc_done", "gm_done", "sig_done", "lam_done", "ex_done",
                             "act_done", "sq_in", "rt_done", "o_done"))
        block = ctx.enter_context(nc.Block())

        @block.sync
        def _(sp):
            clear_last(sp)
            sp.sem_inc(b_out, 80)
            sp.sem_inc(z_out[0], 16)
            sp.sem_inc(z_out[1], 16)
            for s in range(2):
                sp.dma_start(raw[:, s], d["w_in"][U_MG + s]).then_inc(raw_in[s], 16)
            with sp.Fori(0, NBLK) as n:
                t2 = sp.snap(n * 2)
                for u in range(NU):
                    nxt, cur = sp.snap(n * NU + (U_MG + u + 2)), sp.snap(n * NU + (U_MG + u))
                    sp.wait_ge(lo_done, n * NU + (u + 1))
                    sp.dma_start(raw[:, u % 2], d["w_in"][bass.ds(nxt, 1)].rearrange("a p k m -> p (a k) m")).then_inc(raw_in[u % 2], 16)
                    if u == 4:
                        sp.wait_ge(o_done, n * 2 + 2)
                        sp.dma_start(d["o_lru"][bass.ds(t2, 2)].rearrange("a p n -> p a n"), r[:]).then_inc(b_out, 16)
                        sp.dma_start(d["hT"][bass.ds(t2, 2)].rearrange("a p n -> p a n"), h[:, :, NP_ - 1:T]).then_inc(b_out, 16)
                        sp.dma_start(d["cvT"][bass.ds(t2, 2)].rearrange("a p n -> p a n"), xp[:, :, NP_:NP_ + 3]).then_inc(b_out, 16)
                        sp.dma_start(d["cvsT"][bass.ds(t2, 2), :, 0:2 * NS].rearrange("a p n -> p a n"),
                                     st[:, :, NS:3 * NS]).then_inc(b_out, 16)
                        sp.dma_start(d["cvsT"][bass.ds(t2, 2), :, 2 * NS:].rearrange("a p n -> p a n"),
                                     xp[:, :, CWD - 1 + NP_:]).then_inc(b_out, 16)
                    sp.wait_ge(ev_done, n * NU + (u + 3))
                    sp.dma_start(d["z"][bass.ds(cur, 1)].rearrange("a p n -> p (a n)"), z[:, u % 2]).then_inc(z_out[u % 2], 16)
            sp.wait_ge(b_out, 80 * (NBLK + 1))
            for s in range(2):
                sp.wait_ge(z_out[s], 16 * (NBLK * NU // 2 + 1))
                sp.wait_ge(raw_in[s], 16 * (NBLK * NU // 2 + 1))

        @block.gpsimd
        def _(pool):
            with pool.Fori(0, NBLK * NU // 2) as i:
                for s in range(2):
                    pool.wait_ge(hi_done, i * 2 + (s + 1))
                    pool.tensor_tensor(w_lo[:, s], raw[:, s], w_hi[:, s].bitcast(F32), ALU.subtract).then_inc(lo_done, 1)

        @block.tensor
        def _(pe):
            pe.sem_inc(mm_done, 2)
            with pe.Fori(0, NBLK) as n:

                def gate_products(t, c):
                    if t == 0 and c == 0:
                        pe.wait_ge(xc_done, n * 4 + 4)
                    pe.wait_ge(sig_done, n * 12 + (2 * (NCH * t + c) + 2))
                    for w, o in ((wa, ps_r), (wi, ps_i)):
                        for k in range(2):
                            mm = pe.matmul(o[:, 0:CW], w[:, k, t * P:(t + 1) * P], xc[:, k, c * CW:(c + 1) * CW],
                                           start=(k == 0), stop=(k == 1))
                    mm.then_inc(gm_done, 1)

                for u in range(NU):
                    s = u % 2
                    pe.wait_ge(lo_done, n * NU + (u + 1))
                    pe.wait_ge(ev_done, n * NU + (u + 1))
                    for k in range(KT):
                        for p, (w, x) in enumerate(((w_hi, h_hi), (w_hi, h_lo), (w_lo, h_hi))):
                            for c in range(NCH):
                                mm = pe.matmul(acc[s][:, c, 0:CW], w[:, s, k, :], x[:, k, c * CW:(c + 1) * CW],
                                               start=(k + p == 0), stop=(k == KT - 1 and p == 2))
                        if u in (2, 3) and k in (1, 3, 5):
                            gate_products(u - 2, k // 2)
                    mm.then_inc(mm_done, 1)

        @block.scalar
        def _(act):
            with act.Fori(0, NBLK) as n:
                lx, lg = act.snap(n * 2 + U_LX), act.snap(n * 2 + U_LG)
                t2, blk = act.snap(n * 2), act.snap(n * 1)

                def w_part(u):
                    act.wait_ge(raw_in[u % 2], n * (8 * NU) + (16 * (u // 2) + 16))
                    act.wait_ge(mm_done, n * NU + (u + 1))
                    act.activation(w_hi[:, u % 2], raw[:, u % 2], ACT.Copy).then_inc(hi_done, 1)

                def sigmoids(t, c):
                    act.wait_ge(gm_done, n * 6 + (NCH * t + c + 1))
                    for o, v, b in ((ps_r, r, L_BA), (ps_i, ig, L_BI)):
                        act.activation(v[:, t, c * CW:(c + 1) * CW], o[:, 0:CW], ACT.Sigmoid,
                                       bias=par[:, t, b:b + 1]).then_inc(sig_done, 1)

                def decay(t):
                    act.wait_ge(sig_done, n * 12 + (6 * t + 8))
                    act.activation(th[:, t], r[:, t], ACT.Tanh, scale=lam[:, 7, t:t + 1])
                    act.activation(a[:, t], r[:, t], ACT.Exp, scale=lam[:, 6, t:t + 1]).then_inc(act_done, 1)

                def root(t):
                    act.wait_ge(sq_in, n * 2 + (t + 1))
                    act.activation(th[:, t], th[:, t], ACT.Sqrt).then_inc(rt_done, 1)

                w_part(0)
                act.wait_ge(b_out, n * 80 + 80)
                act.dma_start(par[:], d["par"][:, bass.ds(t2, 2), :]).then_inc(b_in, 16)
                act.dma_start(xp[:, :, CWD - 1:], d["z"][bass.ds(lx, 2)].rearrange("a p n -> p a n")).then_inc(b_in, 16)
                act.dma_start(st[:], d["st"][:, bass.ds(t2, 2), :]).then_inc(b_in, 16)
                act.dma_start(gate[:], d["z"][bass.ds(lg, 2)].rearrange("a p n -> p a n")).then_inc(b_in, 16)
                act.dma_start(wa[:], d["w_a"][bass.ds(blk, 1)].rearrange("a p k n -> p (a k) n")).then_inc(b_in, 16)
                act.dma_start(wi[:], d["w_i"][bass.ds(blk, 1)].rearrange("a p k n -> p (a k) n")).then_inc(b_in, 16)
                w_part(1)
                act.wait_ge(lam_done, n * 2 + 1)
                act.activation(lam[:, 3], lam[:, 1], ACT.Exp, scale=-1.0).then_inc(ex_done, 1)
                act.activation(gate[:], gate[:], ACT.Gelu_apprx_tanh)
                w_part(2)
                w_part(3)
                act.wait_ge(lam_done, n * 2 + 2)
                for c in range(NCH):
                    sigmoids(0, c)
                decay(0)
                w_part(4)
                sigmoids(1, 0)
                root(0)
                sigmoids(1, 1)
                sigmoids(1, 2)
                decay(1)
                w_part(5)
                root(1)

        @block.vector
        def _(dve):
            per_block = [0]

            def chain(ins, n):
                per_block[0] += 1
                ins.then_inc(ch, 1)
                dve.wait_ge(ch, n * CH + per_block[0])

            dve.sem_inc(ev_done, 2)
            dve.sem_inc(sig_done, 2)
            dve.memset(xp[:, :, 0:CWD - 1], 0.0).then_inc(pad_done, 1)
            dve.wait_ge(pad_done, 1)
            CH = 52
            with dve.Fori(0, NBLK) as n:

                def store(u):
                    s = u % 2
                    dve.wait_ge(z_out[s], n * (8 * NU) + (16 * (u // 2) + 16))
                    dve.wait_ge(mm_done, n * NU + (u + 3))
                    dve.tensor_copy(z[:, s].rearrange("p (c n) -> p c n", c=NCH), acc[s][:, :, 0:CW]).then_inc(ev_done, 1)

                def scan(t):
                    dve.wait_ge(xc_done, n * 4 + (2 * t + 2))
                    dve.wait_ge(act_done, n * 2 + (t + 1))
                    chain(dve.tensor_tensor(r[:, t], a[:, t], a[:, t], ALU.mult), n)
                    dve.scalar_tensor_tensor(th[:, t], r[:, t], 1.0, th[:, t], ALU.add, ALU.mult).then_inc(sq_in, 1)
                    chain(dve.tensor_tensor(ig[:, t], ig[:, t], xc[:, t], ALU.mult), n)
                    dve.wait_ge(rt_done, n * 2 + (t + 1))
                    chain(dve.tensor_tensor(ig[:, t], ig[:, t], th[:, t], ALU.mult), n)
                    chain(dve.tensor_tensor(h[:, t, NP_:T], a[:, t, NP_:T], st[:, t, 3 * NS:4 * NS], ALU.mult), n)
                    chain(dve.tensor_tensor(h[:, t, NP_:T], h[:, t, NP_:T], ig[:, t, NP_:T], ALU.add), n)
                    chain(dve.tensor_tensor_scan(h[:, t, 0:NP_], a[:, t, 0:NP_], ig[:, t, 0:NP_], 0.0, ALU.mult, ALU.add), n)
                    dve.tensor_tensor(r[:, t], h[:, t], gate[:, t], ALU.mult).then_inc(o_done, 1)

                dve.wait_ge(b_in, n * 96 + 96)
                L = par[:, :, L_LAM]
                chain(dve.tensor_scalar(lam[:, 0], L, -1.0, None, ALU.mult), n)
                chain(dve.tensor_tensor(lam[:, 1], L, lam[:, 0], ALU.max), n)
                dve.tensor_scalar(lam[:, 2], lam[:, 0], 0.0, None, ALU.max).then_inc(lam_done, 1)
                dve.wait_ge(ex_done, n + 1)
                chain(dve.tensor_scalar(lam[:, 4], lam[:, 3], 2.0, None, ALU.add), n)
                chain(dve.reciprocal(lam[:, 4], lam[:, 4]), n)
                chain(dve.tensor_tensor(lam[:, 4], lam[:, 3], lam[:, 4], ALU.mult), n)
                chain(dve.tensor_tensor(lam[:, 5], lam[:, 4], lam[:, 4], ALU.mult), n)
                chain(dve.memset(lam[:, 6], 1.0 / 19), n)
                for q in range(17, 0, -2):
                    chain(dve.tensor_tensor(lam[:, 6], lam[:, 6], lam[:, 5], ALU.mult), n)
                    chain(dve.tensor_scalar(lam[:, 6], lam[:, 6], 1.0 / q, None, ALU.add), n)
                chain(dve.tensor_tensor(lam[:, 6], lam[:, 6], lam[:, 4], ALU.mult), n)
                chain(dve.scalar_tensor_tensor(lam[:, 6], lam[:, 6], 2.0, lam[:, 2], ALU.mult, ALU.add), n)
                chain(dve.tensor_scalar(lam[:, 6], lam[:, 6], -8.0, None, ALU.mult), n)
                dve.tensor_scalar(lam[:, 7], lam[:, 6], -1.0, None, ALU.mult).then_inc(lam_done, 1)
                for t in range(2):
                    w = [par[:, t, L_CW + j:L_CW + j + 1] for j in range(CWD)]
                    chain(dve.tensor_scalar(xc[:, t, 0:NP_], xp[:, t, 0:NP_], w[0], par[:, t, L_CB:L_CB + 1],
                                            ALU.mult, ALU.add), n)
                    chain(dve.tensor_scalar(xc[:, t, NP_:T], st[:, t, 0:NS], w[0], par[:, t, L_CB:L_CB + 1],
                                            ALU.mult, ALU.add), n)
                    for j in range(1, CWD):
                        x_s = st[:, t, j * NS:(j + 1) * NS] if j < CWD - 1 else xp[:, t, CWD - 1 + NP_:]
                        p = dve.scalar_tensor_tensor(xc[:, t, 0:NP_], xp[:, t, j:j + NP_], w[j], xc[:, t, 0:NP_],
                                                     ALU.mult, ALU.add)
                        if j < CWD - 1:
                            chain(p, n)
                        else:
                            p.then_inc(xc_done, 1)
                        p = dve.scalar_tensor_tensor(xc[:, t, NP_:T], x_s, w[j], xc[:, t, NP_:T], ALU.mult, ALU.add)
                        if j < CWD - 1:
                            chain(p, n)
                        else:
                            p.then_inc(xc_done, 1)
                store(0)
                store(1)
                store(2)
                scan(0)
                store(3)
                scan(1)
                store(4)
                store(5)
                assert per_block[0] == CH, per_block[0]


def distance_bias(nc, d, ctx, block, acc, soft):
    sb, sem = sb_of(nc, ctx, "dst"), sem_of(nc, ctx, "dst", new_phase=False)
    rel = sb("rel", [33, 8, P])
    hot = sb("hot", [33, RLEN])
    f = sb("f", [P, 8, RLEN])
    r_in, f_out = soft
    mm_done, ev_done = sem("mm_done"), sem("ev_done")

    @block.gpsimd
    def _(pool):
        pool.dma_start(rel[:], d["rel"]).then_inc(r_in, 16)
        pool.dma_start(hot[:], d["hot"]).then_inc(r_in, 16)
        pool.wait_ge(ev_done, 8)
        pool.dma_start(d["dist"].rearrange("p h n -> p (h n)"), f[:].rearrange("p h n -> p (h n)")).then_inc(f_out, 16)
        pool.wait_ge(f_out, 16)

    @block.tensor
    def _(pe):
        pe.wait_ge(r_in, 32)
        for h in range(8):
            if h >= 2:
                pe.wait_ge(ev_done, h - 1)
            pe.matmul(acc[:, h % 2, :], rel[:, h, :], hot[:], start=True, stop=True).then_inc(mm_done, 1)

    @block.vector
    def _(dve):
        for h in range(8):
            dve.wait_ge(mm_done, h + 1)
            dve.tensor_copy(f[:, h, :], acc[:, h % 2, :]).then_inc(ev_done, 1)


def compress(nc, d, per):
    SEQ = NS + 1
    with ExitStack() as ctx:
        sb, ps, sem = sb_of(nc, ctx, "cmp"), ps_of(nc, ctx, "cmp"), sem_of(nc, ctx, "cmp")
        pt = sb("pt", [1, NS * PAGES], I32)
        pool_x = sb("pool_x", [P, NS * PAGES, 256])
        zc = sb("zc", [P, 2, NP_])
        zr = sb("zr", [P, 2, 2, 8 * NCK])
        cp = sb("cp", [P, 2, 2, 8, NCK])
        w1 = sb("w1", [P, 2, 16, P])
        w2 = sb("w2", [P, 2, HD])
        pos = sb("pos", [P, 2])
        lo = sb("lo", [P, 2, SEQ, NCK])
        hd = sb("hd", [P, 2, SEQ, NCK])
        kc = sb("kc", [P, SEQ * NCK])
        sq = sb("sq", [P, SEQ * NCK])
        vc = sb("vc", [NCK, SEQ, P])
        nm = sb("nm", [P, P + 2])
        ps_lo = [ps(f"lo{s}", [P, NS, NCK]) for s in range(2)]
        ps_hi = [ps(f"hi{s}", [P, NS, NCK]) for s in range(2)]
        ps_pr = [ps(f"pr{s}", [P, 8, NCK]) for s in range(2)]
        ps_o = ps("o", [P, NS * NCK])
        ps_p = ps("p", [P, 8, NCK])
        pt_in, pg_in, zc_in, zr_done, cp_in, w_in, pos_mm, pos_done = (sem("pt_in"), [sem("pg_in0"), sem("pg_in1"), per["soft"][0]], sem("zc_in"), sem("zr_done"),
                                                              sem("cp_in"), sem("w_in"), sem("pos_mm"), sem("pos_done"))
        mm_done, lo_ev, sum_done, act_done, o_mm, o_ev, z_done, c_out = (sem("mm_done"), sem("lo_ev"), sem("sum_done"),
                                                                 sem("act_done"), sem("o_mm"), sem("o_ev"), sem("z_done"),
                                                                 sem("c_out"))
        sq_done, ms_mm, rt_done, rc_done, kc_done = sem("sq_done"), sem("ms_mm"), sem("rt_done"), sem("rc_done"), sem("kc_done")
        block = ctx.enter_context(nc.Block())
        COMBOS = [(kv, g) for kv in range(2) for g in range(2)]

        CUTS = (0, 24, 48, NS * PAGES)

        def pages(eng, part):
            eng.wait_ge(pt_in, 16)
            with eng.Fori(CUTS[part], CUTS[part + 1]) as i:
                page = eng.value_load(pt[0:1, bass.ds(i, 1)], min_val=0, max_val=d["cmp_pool"].shape[0] - 1)
                eng.dma_start(pool_x[:, bass.ds(i, 1), :].rearrange("p a n -> p (a n)"),
                              d["cmp_pool"][bass.ds(page, 1)].rearrange("a p n -> p (a n)")).then_inc(pg_in[part], 16)

        @block.gpsimd
        def _(pool):
            pages(pool, 2)

        @block.sync
        def _(sp):
            clear_last(sp)
            sp.dma_start(pt[:], d["page_table"]).then_inc(pt_in, 16)
            sp.dma_start(zc[:, 0, :], d["z"][U_CMPK][:, 0:NP_]).then_inc(zc_in, 16)
            sp.dma_start(zc[:, 1, :], d["z"][U_CMPV][:, 0:NP_]).then_inc(zc_in, 16)
            for kv in range(2):
                sp.dma_start(w1[:, kv], d["w_c1"][kv]).then_inc(w_in, 16)
                sp.dma_start(w2[:, kv], d["w_c2"][kv]).then_inc(w_in, 16)
            sp.dma_start(nm[:], d["nm_kc"]).then_inc(w_in, 16)
            pages(sp, 0)
            sp.wait_ge(zr_done, 2)
            for g in range(2):
                for s in range(2):
                    sp.dma_start(cp[s * HD:(s + 1) * HD, :, g].rearrange("p k a c -> p k (a c)"),
                                 zr[g * HD:(g + 1) * HD, :, s]).then_inc(cp_in, 16)
            sp.wait_ge(kc_done, 1)
            sp.dma_start(d["kcT"], kc[:]).then_inc(c_out, 16)
            sp.wait_ge(o_ev, 6)
            sp.dma_start(d["vc"], vc[:]).then_inc(c_out, 16)
            sp.wait_ge(c_out, 32)

        @block.vector
        def _(dve):
            dve.memset(hd[:], 0.0).then_inc(z_done, 1)
            dve.wait_ge(zc_in, 32)
            for kv in range(2):
                dve.tensor_copy(zr[:, kv].rearrange("p s (a c) -> p s a c", a=8),
                                zc[:, kv].rearrange("p (c a s) -> p s a c", a=8, s=2)).then_inc(zr_done, 1)
            dve.wait_ge(pos_mm, 1)
            dve.tensor_copy(pos[:], ps_p[:, 0, 0:2]).then_inc(pos_done, 1)
            dve.wait_ge(z_done, 1)
            for n, (kv, g) in enumerate(COMBOS):
                s = n % 2
                dve.wait_ge(lo_ev, 2 * n + 2)
                dve.tensor_tensor(hd[:, s, 0:NS, 0:NCMP], lo[:, s, 0:NS, 0:NCMP], ps_hi[s][:, :, 1:NCK], ALU.add).then_inc(sum_done, 1)
                dve.tensor_tensor(hd[:, s, NS, 0:NCMP], lo[:, s, NS, 0:NCMP], ps_pr[s][:, 1, 1:NCK], ALU.add).then_inc(sum_done, 1)
                if kv == 0:
                    if g == 1:
                        dve.wait_ge(o_mm, 2)
                        dve.tensor_copy(kc[:, 0:NS * NCK], ps_o[:]).then_inc(o_ev, 1)
                        dve.tensor_copy(kc[:, NS * NCK:], ps_p[:, 0, :]).then_inc(o_ev, 1)
                        dve.wait_ge(rt_done, 1)
                        dve.reciprocal(sq[:], sq[:]).then_inc(rc_done, 1)
                        dve.wait_ge(rc_done, 1)
                        dve.scalar_tensor_tensor(kc[:], kc[:], nm[:, P + 1:P + 2], sq[:], ALU.mult, ALU.mult).then_inc(kc_done, 1)
                else:
                    dve.wait_ge(o_mm, n + 1)
                    dve.tensor_copy(vc[:, 0:NS, g * HD:(g + 1) * HD], ps_o[0:NCK, :].rearrange("p (b n) -> p b n", b=NS)).then_inc(o_ev, 1)
                    dve.tensor_copy(vc[:, NS, g * HD:(g + 1) * HD], ps_p[0:NCK, 0, :]).then_inc(o_ev, 1)
                    if n == 3:
                        dve.wait_ge(o_ev, 6)

        @block.scalar
        def _(act):
            pages(act, 1)
            act.wait_ge(pos_done, 1)
            for n, (kv, g) in enumerate(COMBOS):
                s = n % 2
                act.wait_ge(mm_done, n + 1)
                if n >= 2:
                    act.wait_ge(sum_done, 2 * (n - 1))
                act.activation(lo[:, s, 0:NS], ps_lo[s][:], ACT.Identity, bias=pos[:, kv:kv + 1]).then_inc(lo_ev, 1)
                act.activation(lo[:, s, NS], ps_pr[s][:, 0], ACT.Identity, bias=pos[:, kv:kv + 1]).then_inc(lo_ev, 1)
                act.wait_ge(sum_done, 2 * n + 2)
                act.activation(hd[:, s, :, 0:NCMP], hd[:, s, :, 0:NCMP], ACT.Gelu_apprx_tanh).then_inc(act_done, 1)
                if n == 1:
                    act.wait_ge(o_ev, 2)
                    act.activation(sq[:], kc[:], ACT.Square).then_inc(sq_done, 1)
                    act.wait_ge(ms_mm, 1)
                    act.activation(sq[:, 0:NS * NCK], ps_o[:], ACT.Sqrt, bias=nm[:, P:P + 1])
                    act.activation(sq[:, NS * NCK:], ps_p[:, 0, :], ACT.Sqrt, bias=nm[:, P:P + 1]).then_inc(rt_done, 1)

        @block.tensor
        def _(pe):
            pe.wait_ge(w_in, 80)
            for kv, v0 in enumerate((V_PEK, V_PEV)):
                for i in range(16):
                    mm = pe.matmul(ps_p[:, 0, kv:kv + 1], w1[:, kv, i, :], per["vec"][:, v0 + i:v0 + i + 1],
                                   start=(i == 0), stop=(i == 15))
            mm.then_inc(pos_mm, 1)
            for part in range(3):
                pe.wait_ge(pg_in[part], 16 * (CUTS[part + 1] - CUTS[part]))
            pe.wait_ge(cp_in, 64)

            def hidden(n):
                kv, g = COMBOS[n]
                s = n % 2
                if n >= 2:
                    pe.wait_ge(sum_done, 2 * (n - 1))
                for half, o in ((0, ps_lo[s]), (1, ps_hi[s])):
                    for a in range(8):
                        c0 = ((kv * 2 + g) * 8 + a) * 8
                        pe.matmul(o[:].rearrange("p b c -> p (b c)").rearrange("p (i c) -> p i c", c=8),
                                  w1[:, kv, half * 8 + a, :], pool_x[:, :, c0:c0 + 8], start=(a == 0), stop=(a == 7))
                for half in range(2):
                    for a in range(8):
                        mm = pe.matmul(ps_pr[s][:, half, :], w1[:, kv, half * 8 + a, :], cp[:, kv, g, a, :],
                                       start=(a == 0), stop=(a == 7))
                mm.then_inc(mm_done, 1)

            def output(n):
                kv, g = COMBOS[n]
                s = n % 2
                pe.wait_ge(act_done, n + 1)
                if kv == 0:
                    pe.wait_ge(pos_done, 1)
                    pe.matmul(ps_o[g * HD:(g + 1) * HD, :], w2[:, 0, :], hd[:, s, 0:NS].rearrange("p b c -> p (b c)"),
                              start=True, stop=True)
                    mm = pe.matmul(ps_p[g * HD:(g + 1) * HD, 0, :], w2[:, 0, :], hd[:, s, NS], start=True, stop=True)
                else:
                    if n == 2:
                        pe.wait_ge(rt_done, 1)
                    else:
                        pe.wait_ge(o_ev, 4)
                    for b in range(NS):
                        pe.matmul(ps_o[0:NCK, b * HD:(b + 1) * HD], hd[:, s, b], w2[:, 1, :], start=True, stop=True)
                    mm = pe.matmul(ps_p[0:NCK, 0, :], hd[:, s, NS], w2[:, 1, :], start=True, stop=True)
                mm.then_inc(o_mm, 1)

            hidden(0)
            hidden(1)
            output(0)
            output(1)
            hidden(2)
            pe.wait_ge(sq_done, 1)
            pe.wait_ge(o_ev, 2)
            pe.matmul(ps_o[:], nm[:, 0:P], sq[:, 0:NS * NCK], start=True, stop=True)
            pe.matmul(ps_p[:, 0, :], nm[:, 0:P], sq[:, NS * NCK:], start=True, stop=True).then_inc(ms_mm, 1)
            hidden(3)
            output(2)
            output(3)


def prompt_attention(nc, d, per, h_hi, h_lo):
    with ExitStack() as ctx:
        sb, ps, sem = sb_of(nc, ctx, "att"), ps_of(nc, ctx, "att"), sem_of(nc, ctx, "att")
        k_sel = sb("k_sel", [P, NP_])
        k_win = sb("k_win", [P, NP_])
        k_cmp = sb("k_cmp", [P, NCK])
        v_sel = sb("v_sel", [P, QT, P])
        v_win = sb("v_win", [P, QT, P])
        v_cmp = sb("v_cmp", [NCK, P])
        near = sb("near", [P, G, R, 2 * P])
        wmask = sb("wmask", [P, P])
        cstrip = sb("cstrip", [P, G, R, CU])
        cmask = sb("cmask", [P, CU])
        q = sb("q", [P, 2, P])
        pr = sb("pr", [P, 2, NP_])
        ptr = sb("ptr", [P, 4, 4 * P])
        gsl = sb("gsl", [P, 2, G, 3])
        nmx = sb("nmx", [P, 2])
        rs = sb("rs", [P, 2])
        cf = sb("cf", [P, 2, 2])
        oacc = sb("oacc", [P, 2, P])
        oT = sb("oT", [P, 2, P])
        S = [ps(f"S{s}", [P, NP_]) for s in range(2)]
        tp = [ps(f"tp{s}", [P, 512]) for s in range(2)]
        O = ps("O", [P, 512])
        facc = ps("facc", [P, 512])
        raw = sb("raw", [P, KT, P])
        w_hi = sb("w_hi", [P, KT, P], F32R)
        w_lo = sb("w_lo", [P, KT, P], F32R)
        zf = sb("zf", [P, T])
        c_in, m_done = sem("c_in"), sem("m_done")
        f_in, f_hi, f_lo, f_mm, f_ev, f_out = (sem(x) for x in ("f_in", "f_hi", "f_lo", "f_mm", "f_ev", "f_out"))
        q_in = [sem("q_in0"), sem("q_in1")]
        o_out = [sem("o_out0"), sem("o_out1")]
        s_mm, s_exp, s_max, s_pm, s_tp, s_te, s_pvg, s_acc, s_ch = (
            sem(x) for x in ("s_mm", "s_exp", "s_max", "s_pm", "s_tp", "s_te", "s_pvg", "s_acc", "s_ch"))
        block = ctx.enter_context(nc.Block())
        HALF = [(g, br) for g in range(G) for br in ("sel", "win", "cmp")]
        NH = len(HALF)
        NJ = 2 * NH
        FILLED = {0: [1], 1: [2], 2: [3], 3: [4], 4: [5], 5: [6], 6: [7], 7: [8], 8: [9], 9: [10], 10: [11]}

        def tiles(qt, br):
            return {"sel": (0, qt + 1), "win": (max(0, qt - 4), min(qt + 1, 5)), "cmp": (0, 1)}[br]

        def groups(qt, j):
            return -(-tiles(qt, HALF[j % NH][1])[1] // 4)

        def before(qt, j):
            return sum(groups(qt, x) for x in range(j))

        def vbase(qt):
            return sum(2 * before(x, NJ) for x in range(qt))

        def tbase(qt):
            return vbase(qt) + 4 * qt

        def turn_at(qt, s):
            return before(qt, 9) if s == 0 else before(qt, NJ) + 1

        def tgroup(qt, j, a):
            return before(qt, j) + a + (1 if j > 8 else 0)

        @block.sync
        def _(sp):
            clear_last(sp)
            sp.dma_start(raw[:], d["w_in"][U_LX]).then_inc(f_in, 16)
            sp.sem_inc(f_out, 16)
            sp.dma_start(k_sel[:], d["zn"][0][:, 0:NP_]).then_inc(c_in, 16)
            sp.dma_start(k_win[:], d["zn"][1][:, 0:NP_]).then_inc(c_in, 16)
            sp.dma_start(k_cmp[:], d["kcT"][:, NS * NCK:]).then_inc(c_in, 16)
            sp.dma_start(v_sel[:], d["vtok"][0].rearrange("t p n -> p t n")).then_inc(c_in, 16)
            sp.dma_start(v_win[:], d["vtok"][1].rearrange("t p n -> p t n")).then_inc(c_in, 16)
            sp.dma_start(v_cmp[:], d["vc"][:, NS, :]).then_inc(c_in, 16)
            sp.dma_start(near[:].rearrange("p g r n -> p (g r) n"),
                         bass.AP(d["dist"].tensor, RMAX - P, [[8 * RLEN - 1, P], [RLEN, 8], [1, 2 * P]])).then_inc(c_in, 16)
            sp.dma_start(wmask[:], d["wmask"]).then_inc(c_in, 16)
            sp.dma_start(cmask[:], d["cmask"]).then_inc(c_in, 16)
            sp.wait_ge(m_done, 2)
            for h in range(8):
                sp.dma_start(cstrip[:, h // R, h % R, 40:64],
                             bass.AP(d["dist"].tensor, h * RLEN + 16 * 40 - 505, [[8 * RLEN - 1, P], [16, 24]]), allow_slow_non_contiguous=True).then_inc(c_in, 16)

            def load_q(b, s):
                sp.dma_start(q[:, s], d["zn"][2 + 2 * (b % 2) + s][:, (b // 2) * P:(b // 2 + 1) * P]).then_inc(q_in[s], 16)

            sp.sem_inc(o_out[0], 16)
            sp.sem_inc(o_out[1], 16)
            load_q(0, 0)
            load_q(0, 1)
            for b in range(2 * QT):
                qt = b // 2
                sp.wait_ge(f_lo, b + 1)
                sp.dma_start(raw[:], d["w_in"][U_LX + b + 1]).then_inc(f_in, 16)
                if b >= 1:
                    sp.wait_ge(f_ev, 3 * b + 1)
                    sp.dma_start(d["z"][U_LX + b - 1], zf[:]).then_inc(f_out, 16)
                for s in range(2):
                    if b + 1 < 2 * QT:
                        sp.wait_ge(s_mm, NJ * b + NH * s + NH)
                        load_q(b + 1, s)
                    sp.wait_ge(s_te, tbase(qt) + (b % 2) * (before(qt, NJ) + 2) + turn_at(qt, s) + 3)
                    sp.dma_start(d["o_nsa"][2 * (b % 2) + s][:, qt * P:(qt + 1) * P], oT[:, s]).then_inc(o_out[s], 16)
            sp.wait_ge(f_ev, 3 * 2 * QT + 1)
            sp.dma_start(d["z"][U_LX + 2 * QT - 1], zf[:]).then_inc(f_out, 16)
            sp.wait_ge(f_out, 16 * (2 * QT + 1))
            sp.wait_ge(f_in, 16 * (2 * QT + 1))
            sp.wait_ge(o_out[0], 16 * (2 * QT + 1))
            sp.wait_ge(o_out[1], 16 * (2 * QT + 1))

        @block.gpsimd
        def _(pool):
            pool.memset(cstrip[:, :, :, 0:64], 0.0).then_inc(m_done, 1)
            pool.memset(cstrip[:, :, :, 64:CU], NEGV).then_inc(m_done, 1)
            pool.memset(pr[:, :, 0:P], 0.0).then_inc(m_done, 1)

            pool.wait_ge(f_hi, 1)
            pool.tensor_tensor(w_lo[:], raw[:], w_hi[:].bitcast(F32), ALU.subtract).then_inc(f_lo, 1)
            with pool.Fori(0, 2 * QT) as i:
                pool.wait_ge(f_hi, i * 1 + 2)
                pool.tensor_tensor(w_lo[:], raw[:], w_hi[:].bitcast(F32), ALU.subtract).then_inc(f_lo, 1)

        @block.tensor
        def _(pe):
            pe.sem_inc(s_pvg, 4)
            pe.wait_ge(c_in, 16 * 17)
            for qt in range(QT):
                nv = before(qt, NJ)
                nt = nv + 2
                with pe.Fori(0, 2) as i:

                    def scores(j):
                        s, (g, br) = j // NH, HALF[j % NH]
                        k0, nk = tiles(qt, br)
                        keys = {"sel": k_sel, "win": k_win, "cmp": k_cmp}[br]
                        n = NCMP if br == "cmp" else nk * P
                        if j % NH == 0:
                            pe.wait_ge(q_in[s], i * 16 + (32 * qt + 16))
                        pe.wait_ge(s_exp, i * NJ + (2 * NJ * qt + j + 1))
                        for c in range(0, n, 512):
                            w = min(512, n - c)
                            mm = pe.matmul(S[j % 2][:, c:c + w], q[g * HD:(g + 1) * HD, s, :],
                                           keys[g * HD:(g + 1) * HD, k0 * P + c:k0 * P + c + w], start=True, stop=True)
                        mm.then_inc(s_mm, 1)

                    def transposes(j):
                        br = HALF[j % NH][1]
                        if br == "cmp":
                            pe.wait_ge(s_pm, i * 4 + (8 * qt + 2 * (j // NH) + HALF[j % NH][0] + 1))
                        else:
                            pe.wait_ge(s_exp, i * NJ + (2 * NJ * qt + j + 3))
                        for a in range(groups(qt, j)):
                            tg = tgroup(qt, j, a)
                            pe.wait_ge(s_te, i * nt + (tbase(qt) + tg + 1))
                            for t in range(4 * a, min(4 * a + 4, tiles(qt, br)[1])):
                                mm = pe.transpose(tp[tg % 2][:, (t % 4) * P:(t % 4 + 1) * P],
                                                  pr[:, j % 2, t * P:(t + 1) * P], per["ident"][:])
                            mm.then_inc(s_tp, 1)

                    def values(j):
                        g, br = HALF[j % NH]
                        k0, nk = tiles(qt, br)
                        vals = {"sel": v_sel, "win": v_win}.get(br)
                        pe.wait_ge(s_acc, i * NJ + (2 * NJ * qt + j + 2))
                        for a in range(groups(qt, j)):
                            vg = before(qt, j) + a
                            pe.wait_ge(s_te, i * nt + (tbase(qt) + tgroup(qt, j, a) + 3))
                            for t in range(4 * a, min(4 * a + 4, nk)):
                                if br == "cmp":
                                    lhs, rhs = ptr[0:NCMP, vg % 4, 0:P], v_cmp[0:NCMP, g * HD:(g + 1) * HD]
                                else:
                                    lhs = ptr[:, vg % 4, (t % 4) * P:(t % 4 + 1) * P]
                                    rhs = vals[:, k0 + t, g * HD:(g + 1) * HD]
                                mm = pe.matmul(O[:, 0:HD], lhs, rhs, start=(t == 0), stop=(t == nk - 1))
                            mm.then_inc(s_pvg, 1)

                    def turn(s):
                        tg = turn_at(qt, s)
                        pe.wait_ge(s_te, i * nt + (tbase(qt) + tg + 1))
                        pe.wait_ge(s_acc, i * NJ + (2 * NJ * qt + NH * s + NH + 2))
                        pe.transpose(tp[tg % 2][:, 0:P], oacc[:, s], per["ident"][:]).then_inc(s_tp, 1)

                    def filler(f):
                        c = f // 4
                        if f == 0:
                            pe.wait_ge(f_lo, i * 1 + (2 * qt + 1))
                        if f % 4 == 0:
                            pe.wait_ge(f_ev, i * 3 + (6 * qt + c + 1))
                        for x in range(6 * (f % 4), 6 * (f % 4) + 6):
                            k, n = x // 3, x % 3
                            w, h = ((w_hi, h_hi), (w_hi, h_lo), (w_lo, h_hi))[n]
                            mm = pe.matmul(facc[:, 0:CW], w[:, k, :], h[:, k, c * CW:(c + 1) * CW], start=(x == 0), stop=(x == 23))
                        if f % 4 == 3:
                            mm.then_inc(f_mm, 1)

                    scores(0)
                    filler(0)
                    for j in range(NJ):
                        if j + 1 < NJ:
                            scores(j + 1)
                        if j in FILLED:
                            for f in FILLED[j]:
                                filler(f)
                        if j >= 1:
                            values(j - 1)
                        transposes(j)
                        if j == 8:
                            turn(0)
                    values(NJ - 1)
                    turn(1)

        @block.scalar
        def _(act):
            act.sem_inc(s_exp, 2)
            act.sem_inc(s_te, 2)
            act.wait_ge(m_done, 3)
            act.wait_ge(f_in, 16)
            act.activation(w_hi[:], raw[:], ACT.Copy).then_inc(f_hi, 1)
            for qt in range(QT):
                nv = before(qt, NJ)
                nt = nv + 2
                with act.Fori(0, 2) as i:

                    def probs(j):
                        br = HALF[j % NH][1]
                        n = NCMP if br == "cmp" else tiles(qt, br)[1] * P
                        act.wait_ge(s_max, i * NJ + (2 * NJ * qt + j + 1))
                        act.activation(pr[:, j % 2, 0:n], S[j % 2][:, 0:n], ACT.Exp, bias=nmx[:, j % 2:j % 2 + 1],
                                       accum_out=rs[:, j % 2:j % 2 + 1]).then_inc(s_exp, 1)

                    def copies(j):
                        k0, nk = tiles(qt, HALF[j % NH][1])
                        cmp = HALF[j % NH][1] == "cmp"
                        for a in range(groups(qt, j)):
                            vg, tg = before(qt, j) + a, tgroup(qt, j, a)
                            m = min(4, nk - 4 * a) * P
                            w = NCMP if cmp else P
                            act.wait_ge(s_pvg, i * nv + (vbase(qt) + vg + 1))
                            act.wait_ge(s_tp, i * nt + (tbase(qt) + tg + 1))
                            act.activation(ptr[0:w, vg % 4, 0:m], tp[tg % 2][0:w, 0:m], ACT.Copy).then_inc(s_te, 1)

                    def turned(s):
                        tg = turn_at(qt, s)
                        act.wait_ge(o_out[s], i * 16 + (32 * qt + 16))
                        act.wait_ge(s_tp, i * nt + (tbase(qt) + tg + 1))
                        act.activation(oT[:, s], tp[tg % 2][:, 0:P], ACT.Copy).then_inc(s_te, 1)

                    probs(0)
                    for j in range(NJ):
                        if j + 1 < NJ:
                            probs(j + 1)
                        copies(j)
                        if j == 8:
                            turned(0)
                        if j == 11:
                            act.wait_ge(f_in, i * 16 + (32 * qt + 32))
                            act.wait_ge(f_mm, i * 3 + (6 * qt + 3))
                            act.activation(w_hi[:], raw[:], ACT.Copy).then_inc(f_hi, 1)
                    turned(1)

        @block.vector
        def _(dve):
            dve.sem_inc(s_acc, 2)
            dve.wait_ge(c_in, 16 * 17)
            dve.sem_inc(f_ev, 1)
            chb = 0
            for qt in range(QT):
                per_body = 46 + (4 if qt >= 4 else 0)
                with dve.Fori(0, 2) as i:
                    count = [0]

                    def chain(ins):
                        count[0] += 1
                        ins.then_inc(s_ch, 1)
                        dve.wait_ge(s_ch, i * per_body + (chb + count[0]))

                    def maxima(j):
                        s, (g, br) = j // NH, HALF[j % NH]
                        k0, nk = tiles(qt, br)
                        x = S[j % 2]
                        n = NCMP if br == "cmp" else nk * P
                        r = i * 2 + s
                        dve.wait_ge(s_mm, i * NJ + (2 * NJ * qt + j + 1))
                        if br == "cmp":
                            c0 = 56 - 8 * qt
                            chain(dve.tensor_tensor(x[:, 0:n], x[:, 0:n], cstrip[:, g, bass.ds(r, 1), c0:c0 + n].rearrange(
                                "p a n -> p (a n)"), ALU.add))
                        else:
                            m = min(nk, 2) * P
                            chain(dve.tensor_tensor(x[:, n - m:n], x[:, n - m:n], near[:, g, bass.ds(r, 1), 2 * P - m:].rearrange(
                                "p a n -> p (a n)"), ALU.add))
                            if br == "win" and qt >= 4:
                                chain(dve.tensor_tensor(x[:, 0:P], x[:, 0:P], wmask[:], ALU.add))
                        dve.tensor_reduce(nmx[:, j % 2:j % 2 + 1], x[:, 0:n], AX, ALU.max, negate=True).then_inc(s_max, 1)

                    def coefficient(j):
                        s, (g, br) = j // NH, HALF[j % NH]
                        bi = ("cmp", "sel", "win").index(br)
                        v = rs[:, j % 2:j % 2 + 1]
                        dve.wait_ge(s_exp, i * NJ + (2 * NJ * qt + j + 3))
                        if br == "cmp":
                            c0 = 56 - 8 * qt
                            pm = pr[:, j % 2, 0:NCMP]
                            dve.tensor_tensor(pm, pm, cmask[:, c0:c0 + NCMP], ALU.mult).then_inc(s_pm, 1)
                            dve.wait_ge(s_pm, i * 4 + (8 * qt + 2 * s + g + 1))
                            chain(dve.tensor_reduce(v, pm, AX, ALU.add))
                            chain(dve.tensor_scalar(v, v, 1e-30, None, ALU.max))
                        chain(dve.reciprocal(cf[:, j % 2, 0:1], v))
                        chain(dve.tensor_tensor(cf[:, j % 2, 1:2], cf[:, j % 2, 0:1], gsl[:, s, g, bi:bi + 1], ALU.mult))

                    def accumulate(j):
                        s, (g, br) = j // NH, HALF[j % NH]
                        dve.wait_ge(s_pvg, i * before(qt, NJ) + (vbase(qt) + before(qt, j + 1) + 4))
                        o = oacc[:, s, g * HD:(g + 1) * HD]
                        c = cf[:, j % 2, 1:2]
                        if br == "sel":
                            dve.tensor_scalar(o, O[:, 0:HD], c, None, ALU.mult).then_inc(s_acc, 1)
                        else:
                            dve.wait_ge(s_acc, i * NJ + (2 * NJ * qt + j + 2))
                            dve.scalar_tensor_tensor(o, O[:, 0:HD], c, o, ALU.mult, ALU.add).then_inc(s_acc, 1)

                    for j in range(NJ + 2):
                        if j < NJ:
                            if j % NH == 0:
                                r = i * 2 + j // NH
                                gt = per["gate"][:, qt, :].rearrange("p (g r c) -> p g r c", g=G, r=R)
                                chain(dve.tensor_copy(gsl[:, j // NH], gt[:, :, bass.ds(r, 1), :].rearrange("p g a c -> p g (a c)")))
                            maxima(j)
                        if j >= 2:
                            accumulate(j - 2)
                        if 1 <= j <= NJ:
                            coefficient(j - 1)
                        if j in (3, 7, 11):
                            c = j // 4
                            if c == 0:
                                dve.wait_ge(f_out, i * 16 + (32 * qt + 16))
                            dve.wait_ge(f_mm, i * 3 + (6 * qt + c + 1))
                            dve.tensor_copy(zf[:, c * CW:(c + 1) * CW], facc[:, 0:CW]).then_inc(f_ev, 1)
                    assert count[0] == per_body, count[0]
                chb += 2 * per_body


def memory_attention(nc, d, per, ctx, block, bank, between):
    SC = P ** -0.5
    NJ = 2 * MH
    sb, sem = sb_of(nc, ctx, "mat"), sem_of(nc, ctx, "mat", new_phase=False)
    km = sb("km", [P, MH, NMEM])
    vm = sb("vm", [P, MH, 2, P])
    q = sb("q", [P, 2, MH, P])
    pr = sb("pr", [P, 2, NMEM])
    ptr = sb("ptr", [P, 2, NMEM])
    mx = sb("mx", [P, 2, 2])
    rs = sb("rs", [P, 2, 2])
    oT = sb("oT", [P, 2, MH, P])
    S, tp, O = bank[0:2], bank[2:4], bank[4:6]
    c_in = sem("c_in")
    q_in = [sem("q_in0"), sem("q_in1")]
    o_out = [sem("o_out0"), sem("o_out1")]
    s_mm, s_mx, s_neg, s_exp, s_rc, s_pn, s_tp, s_te, s_pv, s_oe = (
        sem(x) for x in ("s_mm", "s_mx", "s_neg", "s_exp", "s_rc", "s_pn", "s_tp", "s_te", "s_pv", "s_oe"))

    @block.sync
    def _(sp):
        sp.dma_start(km[:], d["memn"].rearrange("h p n -> p h n")).then_inc(c_in, 16)
        sp.dma_start(vm[:], d["memv"].rearrange("h t p n -> p h t n")).then_inc(c_in, 16)
        sp.sem_inc(o_out[0], 16)
        sp.sem_inc(o_out[1], 16)

        def tile_of(a, m):
            return a[:, :, m * P:(m + 1) * P].rearrange("h p n -> p h n")

        def store(m):
            sp.wait_ge(s_oe, MH * (m + 1) + 2)
            sp.dma_start(tile_of(d["o_mem"], m), oT[:, m % 2]).then_inc(o_out[m % 2], 16)

        for m in range(QT):
            if m >= 2:
                sp.wait_ge(s_mm, MH * (m - 1))
            sp.dma_start(q[:, m % 2], tile_of(d["zn"][6:10], m)).then_inc(q_in[m % 2], 16)
            between(sp, m)
            if m >= 2:
                store(m - 2)
        store(QT - 2)
        store(QT - 1)
        sp.wait_ge(o_out[0], 16 * (QT // 2 + 1))
        sp.wait_ge(o_out[1], 16 * (QT // 2 + 1))

    @block.tensor
    def _(pe):
        pe.wait_ge(c_in, 32)
        with pe.Fori(0, QT // 2) as i:

            def scores(j):
                t, h = j // MH, j % MH
                if h == 0:
                    pe.wait_ge(q_in[t], i * 16 + 16)
                pe.wait_ge(s_exp, i * NJ + (j + 1))
                pe.matmul(S[j % 2][:, 0:NMEM], q[:, t, h], km[:, h], start=True, stop=True).then_inc(s_mm, 1)

            def turn(j):
                pe.wait_ge(s_pn, i * NJ + (j + 1))
                for t in range(2):
                    mm = pe.transpose(tp[j % 2][:, t * P:(t + 1) * P], pr[:, j % 2, t * P:(t + 1) * P], per["ident"][:])
                mm.then_inc(s_tp, 1)

            def values(j):
                pe.wait_ge(s_te, i * NJ + (j + 1))
                pe.wait_ge(s_oe, i * NJ + (j + 1))
                for t in range(2):
                    mm = pe.matmul(O[j % 2][:, 0:P], vm[:, j % MH, t], ptr[:, j % 2, t * P:(t + 1) * P],
                                   start=(t == 0), stop=(t == 1))
                mm.then_inc(s_pv, 1)

            scores(0)
            for j in range(NJ):
                if j + 1 < NJ:
                    scores(j + 1)
                if j >= 1:
                    values(j - 1)
                turn(j)
            values(NJ - 1)

    @block.vector
    def _(dve):
        with dve.Fori(0, QT // 2) as i:

            def maximum(j):
                s = j % 2
                dve.wait_ge(s_mm, i * NJ + (j + 1))
                dve.tensor_reduce(mx[:, s, 0:1], S[s][:, 0:NMEM], AX, ALU.max).then_inc(s_mx, 1)
                dve.wait_ge(s_mx, i * NJ + (j + 1))
                dve.tensor_scalar(mx[:, s, 1:2], mx[:, s, 0:1], -SC, None, ALU.mult).then_inc(s_neg, 1)

            def normal(j):
                s = j % 2
                dve.wait_ge(s_exp, i * NJ + (j + 3))
                dve.reciprocal(rs[:, s, 1:2], rs[:, s, 0:1]).then_inc(s_rc, 1)
                dve.wait_ge(s_rc, i * NJ + (j + 1))
                dve.tensor_scalar(pr[:, s], pr[:, s], rs[:, s, 1:2], None, ALU.mult).then_inc(s_pn, 1)

            maximum(0)
            for j in range(NJ):
                if j + 1 < NJ:
                    maximum(j + 1)
                normal(j)

    @block.scalar
    def _(act):
        act.sem_inc(s_exp, 2)
        act.sem_inc(s_oe, 2)
        with act.Fori(0, QT // 2) as i:

            def exponentials(j):
                s = j % 2
                act.wait_ge(s_neg, i * NJ + (j + 1))
                act.activation(pr[:, s], S[s][:, 0:NMEM], ACT.Exp, bias=mx[:, s, 1:2], scale=SC,
                               accum_out=rs[:, s, 0:1]).then_inc(s_exp, 1)

            def turned(j):
                act.wait_ge(s_tp, i * NJ + (j + 1))
                act.activation(ptr[:, j % 2], tp[j % 2][:, 0:NMEM], ACT.Copy).then_inc(s_te, 1)

            def output(j):
                if j % MH == 0:
                    act.wait_ge(o_out[j // MH], i * 16 + 16)
                act.wait_ge(s_pv, i * NJ + (j + 1))
                act.activation(oT[:, j // MH, j % MH], O[j % 2][:, 0:P], ACT.Copy).then_inc(s_oe, 1)

            exponentials(0)
            for j in range(NJ):
                if j + 1 < NJ:
                    exponentials(j + 1)
                if j >= 1:
                    output(j - 1)
                turned(j)
            output(NJ - 1)

    return lambda pe: pe.wait_ge(s_oe, MH * QT + 2)


def sample_attention(nc, d, per, ctx, block, bank):
    RW = NS * 8
    LS = NP_ + 1
    LW = WIN + 1
    NB = 16
    sb, sem = sb_of(nc, ctx, "sat"), sem_of(nc, ctx, "sat", new_phase=False)
    pt = sb("pt", [1, NS * PAGES], I32)
    qs = sb("qs", [P, R, NS])
    qb = sb("qb", [P, NS, RW])
    knew = sb("knew", [P, NS, 2])
    vnew = sb("vnew", [1, NS, 2, P])
    kc = sb("kc", [P, NS, NCK])
    ks = sb("ks", [P, NS, PAGES, P])
    kw = sb("kw", [P, NS, WIN])
    VSL = 7
    vs = sb("vs", [P, VSL, PAGES, P])
    vw = sb("vw", [P, VSL, WIN // P, P])
    vc = sb("vc", [NCK, NS, P])
    b_far = sb("b_far", [RW, P + 1])
    b_cmp = sb("b_cmp", [RW, 23])
    gt = sb("gt", [RW, 3])
    grp = sb("grp", [RW, RW])
    blk = sb("blk", [RW, NB])
    ls = sb("ls", [RW, LS + 7])
    lw = sb("lw", [RW, LW + 7])
    lc = sb("lc", [RW, NCK])
    sc = sb("sc", [RW, 16])
    sel = sb("sel", [RW, 4, NB])
    keep = sb("keep", [RW, NCK])
    pT = sb("pT", [P, 13, RW])
    nT = sb("nT", [1, 2, RW])
    oT = sb("oT", [P, R, NS])
    S0, S1, S2, S3, S4, S5, S6, S7 = bank
    c_in, b_in, z_done, qb_done, vn_in, pt_in = sem("c_in"), sem("b_in"), sem("z_done"), sem("qb_done"), sem("vn_in"), sem("pt_in")
    k_in = per["soft"][1:9]
    v_in = [sem(f"v_in{b}") for b in range(NS)]
    s_mm, ch, e_done, a_done, g_mm, tp_done, te_done, o_mm, o_done, o_out, s_all, m_done = (
        sem(x) for x in ("s_mm", "ch", "e_done", "a_done", "g_mm", "tp_done", "te_done", "o_mm", "o_done", "o_out",
                         "s_all", "m_done"))
    dist = d["dist"].tensor

    def pages(eng, b, src, slot, in_sem):
        with eng.Fori(0, PAGES) as i:
            page = eng.value_load(pt[0:1, bass.ds(i + b * PAGES, 1)], min_val=0, max_val=src.shape[0] - 1)
            eng.dma_start(slot[:, bass.ds(i, 1), :].rearrange("p a n -> p (a n)"),
                          src[bass.ds(page, 1)].rearrange("a p n -> p (a n)")).then_inc(in_sem, 16)

    def values_of(eng, seqs):
        eng.wait_ge(pt_in, 16)
        for b in seqs:
            s = b % VSL
            if b >= VSL:
                eng.wait_ge(o_mm, b - VSL + 1)
            eng.dma_start(vw[:, s], d["win_v"][b].rearrange("t p n -> p t n")).then_inc(v_in[b], 16)
            eng.dma_start(vc[:, b], d["vc"][:, b, :]).then_inc(v_in[b], 16)
            pages(eng, b, d["sel_v"], vs[:, s], v_in[b])

    def constants(sp, b):
        if b == 0:
            shared(sp)
        sp.dma_start(b_far[b * 8:(b + 1) * 8, :],
                     bass.AP(dist, RMAX - P, [[RLEN, 8], [1, P + 1]])).then_inc(b_in, 16)
        sp.dma_start(b_cmp[b * 8:(b + 1) * 8, :],
                     bass.AP(dist, 16 * 40 - 633, [[RLEN, 8], [16, 23]]), allow_slow_non_contiguous=True).then_inc(b_in, 16)
        for j, u in enumerate((U_SELV, U_WINV)):
            sp.dma_start(vnew[0:1, b, j, :], bass.AP(d["z"].tensor, u * P * T + NP_ + b, [[0, 1], [T, P]]),
                         allow_slow_non_contiguous=True).then_inc(vn_in, 16)

    def shared(sp):
        sp.dma_start(qs[:], d["zn"][2:6][:, :, NP_:T].rearrange("r p b -> p r b")).then_inc(c_in, 16)
        sp.dma_start(knew[:, :, 0], d["zn"][0][:, NP_:T], allow_slow_non_contiguous=True).then_inc(c_in, 16)
        sp.dma_start(knew[:, :, 1], d["zn"][1][:, NP_:T], allow_slow_non_contiguous=True).then_inc(c_in, 16)
        sp.dma_start(kc[:].rearrange("p b c -> p (b c)"), d["kcT"][:, 0:NS * NCK]).then_inc(c_in, 16)
        sp.dma_start(grp[:], d["grp"]).then_inc(c_in, 16)
        sp.dma_start(blk[:], d["blk"]).then_inc(c_in, 16)
        sp.dma_start(gt[:], d["gate_s"].rearrange("(r c) o -> r (c o)", c=3)).then_inc(c_in, 16)

    @block.sync
    def _(sp):
        sp.dma_start(pt[:], d["page_table"]).then_inc(pt_in, 16)

    banks_read = memory_attention(nc, d, per, ctx, block, bank, constants)

    @block.sync
    def _(sp):
        values_of(sp, (0, 1, 2, 3, 4, 6))
        sp.wait_ge(o_done, 2)
        sp.dma_start(d["o_nsa"][:, :, NP_:T].rearrange("r p b -> p r b"), oT[:]).then_inc(o_out, 16)
        sp.wait_ge(o_out, 16)

    @block.gpsimd
    def _(pool):
        pool.wait_ge(pt_in, 16)
        for b in range(NS):
            pool.dma_start(kw[:, b], d["winkT"][b]).then_inc(k_in[b], 16)
            pages(pool, b, d["sel_kT"], ks[:, b], k_in[b])

    @block.tensor
    def _(pe):
        banks_read(pe)
        pe.wait_ge(qb_done, 2)
        pe.wait_ge(c_in, 16 * 7)
        for b in range(NS):
            st, sp_ = b == 0, b == NS - 1
            lhs = qb[:, b, :]
            pe.wait_ge(k_in[b], 16 * 9)
            pe.matmul(S0[0:RW, :], lhs, ks[:, b, 0:4].rearrange("p a n -> p (a n)"), start=st, stop=sp_)
            pe.matmul(S1[0:RW, :], lhs, ks[:, b, 4:8].rearrange("p a n -> p (a n)"), start=st, stop=sp_)
            pe.matmul(S2[0:RW, :], lhs, kw[:, b], start=st, stop=sp_)
            pe.matmul(S3[0:RW, 0:2], lhs, knew[:, b, :], start=st, stop=sp_)
            pe.matmul(S4[0:RW, 0:NCK], lhs, kc[:, b, :], start=st, stop=sp_).then_inc(s_mm, 1)
        pe.wait_ge(g_mm, 1)
        pe.matmul(S5[0:RW, 0:NCMP], grp[:], lc[:, 0:NCMP], start=True, stop=True).then_inc(tp_done, 1)
        pe.wait_ge(m_done, 1)
        idn = per["ident"][0:RW, 0:RW]
        for t in range(8):
            pe.transpose(S6[:, t * RW:(t + 1) * RW], ls[:, t * P:(t + 1) * P], idn)
        for t in range(4):
            pe.transpose(S7[:, t * RW:(t + 1) * RW], lw[:, t * P:(t + 1) * P], idn)
        pe.transpose(S7[0:NCMP, 4 * RW:5 * RW], lc[:, 0:NCMP], idn)
        pe.transpose(S5[0:1, 128:128 + RW], ls[:, NP_:LS], idn)
        pe.transpose(S5[0:1, 256:256 + RW], lw[:, WIN:LW], idn).then_inc(tp_done, 1)
        pe.wait_ge(te_done, 4)
        pe.wait_ge(vn_in, 16 * 2 * NS)
        for b in range(NS):
            s, c = b % VSL, slice(b * 8, (b + 1) * 8)
            pe.wait_ge(v_in[b], 16 * 10)
            for t in range(8):
                pe.matmul(S0[:, c], vs[:, s, t], pT[:, t, c], start=(t == 0), stop=False)
            for t in range(4):
                pe.matmul(S0[:, c], vw[:, s, t], pT[:, 8 + t, c], start=False, stop=False)
            pe.matmul(S0[:, c], vc[0:NCMP, b], pT[0:NCMP, 12, c], start=False, stop=False)
            pe.matmul(S0[:, c], vnew[0:1, b, 0, :], nT[0:1, 0, c], start=False, stop=False)
            pe.matmul(S0[:, c], vnew[0:1, b, 1, :], nT[0:1, 1, c], start=False, stop=True).then_inc(o_mm, 1)

    @block.scalar
    def _(act):
        act.wait_ge(a_done, 1)
        act.activation(lc[:, 0:NCMP], lc[:, 0:NCMP], ACT.Exp, bias=sc[:, 0:1], accum_out=sc[:, 1:2]).then_inc(e_done, 1)
        act.wait_ge(a_done, 2)
        act.activation(ls[:, 0:LS], ls[:, 0:LS], ACT.Exp, bias=sc[:, 2:3], accum_out=sc[:, 3:4]).then_inc(e_done, 1)
        act.wait_ge(a_done, 3)
        act.activation(lw[:, 0:LW], lw[:, 0:LW], ACT.Exp, bias=sc[:, 4:5], accum_out=sc[:, 5:6]).then_inc(e_done, 1)
        values_of(act, (5, 7))

    @block.vector
    def _(dve):
        n = [0]

        def chain(ins):
            n[0] += 1
            ins.then_inc(ch, 1)
            dve.wait_ge(ch, n[0])

        chain(dve.memset(qb[:], 0.0))
        dve.wait_ge(c_in, 16 * 7)
        for g in range(G):
            rows = slice(g * HD, (g + 1) * HD)
            q0 = qb[rows].rearrange("p b c -> p (b c)")
            for b in range(NS):
                ins = dve.tensor_copy(q0[:, b * (RW + 8) + g * R:b * (RW + 8) + (g + 1) * R], qs[rows, :, b])
            ins.then_inc(qb_done, 1)
        dve.wait_ge(s_mm, NS)
        dve.wait_ge(b_in, 16 * 2 * NS)
        chain(dve.tensor_copy(lc[:, 0:40], S4[0:RW, 0:40]))
        chain(dve.tensor_tensor(lc[:, 40:NCMP], S4[0:RW, 40:NCMP], b_cmp[:], ALU.add))
        dve.tensor_reduce(sc[:, 0:1], lc[:, 0:NCMP], AX, ALU.max, negate=True).then_inc(a_done, 1)
        dve.wait_ge(e_done, 1)
        chain(dve.reciprocal(sc[:, 6:7], sc[:, 1:2]))
        dve.tensor_scalar(lc[:, 0:NCMP], lc[:, 0:NCMP], sc[:, 6:7], None, ALU.mult).then_inc(g_mm, 1)
        dve.wait_ge(tp_done, 1)
        ssum = keep[:]
        chain(dve.memset(ssum[:, NCMP:NCK], 0.0))
        chain(dve.tensor_copy(ssum[:, 0:NCMP], S5[0:RW, 0:NCMP]))
        chain(dve.tensor_reduce(sel[:, 0], ssum.rearrange("p (s c) -> p s c", c=4), AX, ALU.add))
        chain(dve.tensor_tensor(sel[:, 0, 1:NB], sel[:, 0, 1:NB], ssum.rearrange("p (s c) -> p s c", c=4)[:, 0:NB - 1, 3], ALU.add))
        chain(dve.tensor_reduce(sc[:, 7:8], sel[:, 0, 1:NB - 1], AX, ALU.min))
        chain(dve.memset(sel[:, 1], 0.0))
        chain(dve.tensor_scalar(sel[:, 1, 1:NB - 1], sel[:, 0, 1:NB - 1], sc[:, 7:8], None, ALU.is_le))
        chain(dve.tensor_tensor(sel[:, 1], sel[:, 1], blk[:], ALU.mult))
        chain(dve.tensor_reduce(sc[:, 8:9], sel[:, 1], AX, ALU.max))
        chain(dve.tensor_scalar(sel[:, 2], blk[:], sc[:, 8:9], NEGV, ALU.is_equal, ALU.mult))
        chain(dve.tensor_copy(ls[:, 0:512], S0[0:RW, :]))
        chain(dve.tensor_copy(ls[:, 512:NP_ - P], S1[0:RW, 0:512 - P]))
        chain(dve.tensor_tensor(ls[:, NP_ - P:NP_], S1[0:RW, 512 - P:512], b_far[:, 0:P], ALU.add))
        chain(dve.tensor_tensor(ls[:, NP_:LS], S3[0:RW, 0:1], b_far[:, P:P + 1], ALU.add))
        chain(dve.tensor_tensor(ls[:, 0:NP_].rearrange("p (s c) -> p s c", s=NB), ls[:, 0:NP_].rearrange("p (s c) -> p s c", s=NB),
                                sel[:, 2].rearrange("p (s a) -> p s a", a=1).to_broadcast([RW, NB, NP_ // NB]), ALU.add))
        dve.tensor_reduce(sc[:, 2:3], ls[:, 0:LS], AX, ALU.max, negate=True).then_inc(a_done, 1)
        chain(dve.tensor_copy(lw[:, 0:WIN - P], S2[0:RW, 0:WIN - P]))
        chain(dve.tensor_tensor(lw[:, WIN - P:WIN], S2[0:RW, WIN - P:WIN], b_far[:, 0:P], ALU.add))
        chain(dve.tensor_tensor(lw[:, WIN:LW], S3[0:RW, 1:2], b_far[:, P:P + 1], ALU.add))
        chain(dve.memset(lw[:, 0:1], NEGV))
        dve.tensor_reduce(sc[:, 4:5], lw[:, 0:LW], AX, ALU.max, negate=True).then_inc(a_done, 1)
        chain(dve.tensor_scalar(lc[:, 0:NCMP], lc[:, 0:NCMP], gt[:, 0:1], None, ALU.mult))
        dve.wait_ge(e_done, 2)
        chain(dve.reciprocal(sc[:, 9:10], sc[:, 3:4]))
        chain(dve.tensor_scalar(ls[:, 0:LS], ls[:, 0:LS], sc[:, 9:10], gt[:, 1:2], ALU.mult, ALU.mult))
        dve.wait_ge(e_done, 3)
        chain(dve.reciprocal(sc[:, 10:11], sc[:, 5:6]))
        dve.tensor_scalar(lw[:, 0:LW], lw[:, 0:LW], sc[:, 10:11], gt[:, 2:3], ALU.mult, ALU.mult).then_inc(m_done, 1)
        dve.wait_ge(tp_done, 2)
        dve.tensor_copy(pT[:, 0:8].rearrange("p t r -> p (t r)"), S6[:, 0:8 * RW]).then_inc(te_done, 1)
        dve.tensor_copy(pT[:, 8:12].rearrange("p t r -> p (t r)"), S7[:, 0:4 * RW]).then_inc(te_done, 1)
        dve.tensor_copy(pT[0:NCMP, 12], S7[0:NCMP, 4 * RW:5 * RW]).then_inc(te_done, 1)
        dve.tensor_copy(nT[:], S5[0:1, 128:384].rearrange("p (j n) -> p j n", j=2)[:, :, 0:RW]).then_inc(te_done, 1)
        dve.wait_ge(o_mm, NS)
        for g in range(G):
            rows = slice(g * HD, (g + 1) * HD)
            dve.tensor_copy(oT[rows], S0[rows, 0:RW].rearrange("p (b h) -> p h b", h=8)[:, g * R:(g + 1) * R, :]).then_inc(o_done, 1)


def sample_memory(nc, d, per, ctx, block, bank):
    RW = NS * MH
    RP = 64
    SC = P ** -0.5
    sb, sem = sb_of(nc, ctx, "sme"), sem_of(nc, ctx, "sme", new_phase=False)
    qs = sb("qs", [P, MH, NS])
    qb = sb("qb", [P, RW, RP])
    km = sb("km", [P, 4, MH, NMEM])
    vm = sb("vm", [P, 4, 2, MH, P])
    pr = sb("pr", [RW, NMEM])
    pT = sb("pT", [P, 2, RW])
    sc = sb("sc", [RW, 4])
    oT = sb("oT", [P, MH, NS])
    O, tp, S = bank[1:4]
    c_in, z_done, qb_done = per["soft"][17], sem("z_done"), sem("qb_done")
    k_in = per["soft"][9:13]
    v_in = per["soft"][13:17]
    s_mm, ch, a_done, e_done, p_done, tp_done, te_done, o_mm, o_done, o_out = (
        sem(x) for x in ("s_mm", "ch", "a_done", "e_done", "p_done", "tp_done", "te_done", "o_mm", "o_done", "o_out"))

    @block.gpsimd
    def _(pool):
        pool.dma_start(qs[:], d["zn"][6:10][:, :, NP_:T].rearrange("r p b -> p r b")).then_inc(c_in, 16)
        for b in range(4):
            pool.dma_start(km[:, b], d["mem_kT"][b]).then_inc(k_in[b], 16)
        for b in range(4):
            pool.dma_start(vm[:, b], d["mem_v"][b].rearrange("t p h n -> p t h n")).then_inc(v_in[b], 16)
        for b in range(4, NS):
            pool.wait_ge(s_mm, b - 3)
            pool.dma_start(km[:, b % 4], d["mem_kT"][b]).then_inc(k_in[b % 4], 16)
        for b in range(4, NS):
            pool.wait_ge(o_mm, b - 3)
            pool.dma_start(vm[:, b % 4], d["mem_v"][b].rearrange("t p h n -> p t h n")).then_inc(v_in[b % 4], 16)

    @block.sync
    def _(sp):
        sp.wait_ge(o_done, 1)
        sp.dma_start(d["o_mem"][:, :, NP_:T].rearrange("r p b -> p r b"), oT[:]).then_inc(o_out, 16)
        sp.wait_ge(o_out, 16)

    @block.tensor
    def _(pe):
        pe.wait_ge(qb_done, 1)
        for b in range(NS):
            pe.wait_ge(k_in[b % 4], 16 * (b // 4 + 1))
            for h in range(MH):
                n = b * MH + h
                mm = pe.matmul(S[0:RP, 0:NMEM], qb[:, n, :], km[:, b % 4, h, :], start=(n == 0), stop=(n == RW - 1))
            mm.then_inc(s_mm, 1)
        pe.wait_ge(p_done, 1)
        for t in range(2):
            mm = pe.transpose(tp[:, t * RW:(t + 1) * RW], pr[:, t * P:(t + 1) * P], per["ident"][0:RW, 0:RW])
        mm.then_inc(tp_done, 1)
        pe.wait_ge(te_done, 1)
        for b in range(NS):
            pe.wait_ge(v_in[b % 4], 16 * (b // 4 + 1))
            for h in range(MH):
                n = b * MH + h
                for t in range(2):
                    mm = pe.matmul(O[:, n:n + 1], vm[:, b % 4, t, h, :], pT[:, t, n:n + 1], start=(t == 0), stop=(t == 1))
            mm.then_inc(o_mm, 1)

    @block.scalar
    def _(act):
        act.wait_ge(a_done, 1)
        act.activation(pr[:], S[0:RW, 0:NMEM], ACT.Exp, bias=sc[:, 1:2], scale=SC, accum_out=sc[:, 2:3]).then_inc(e_done, 1)

    @block.vector
    def _(dve):
        dve.memset(qb[:], 0.0).then_inc(z_done, 1)
        dve.wait_ge(z_done, 1)
        dve.wait_ge(c_in, 16)
        q0 = qb[:].rearrange("p n c -> p (n c)")
        for n in range(RW):
            ins = dve.tensor_copy(q0[:, n * (RP + 1):n * (RP + 1) + 1], qs[:, n % MH, n // MH:n // MH + 1])
        ins.then_inc(qb_done, 1)
        dve.wait_ge(s_mm, NS)
        dve.tensor_reduce(sc[:, 0:1], S[0:RW, 0:NMEM], AX, ALU.max).then_inc(ch, 1)
        dve.wait_ge(ch, 1)
        dve.tensor_scalar(sc[:, 1:2], sc[:, 0:1], -SC, None, ALU.mult).then_inc(a_done, 1)
        dve.wait_ge(e_done, 1)
        dve.reciprocal(sc[:, 3:4], sc[:, 2:3]).then_inc(ch, 1)
        dve.wait_ge(ch, 2)
        dve.tensor_scalar(pr[:], pr[:], sc[:, 3:4], None, ALU.mult).then_inc(p_done, 1)
        dve.wait_ge(tp_done, 1)
        dve.tensor_copy(pT[:].rearrange("p t n -> p (t n)"), tp[:, 0:2 * RW]).then_inc(te_done, 1)
        dve.wait_ge(o_mm, NS)
        dve.tensor_copy(oT[:], O[:, 0:RW].rearrange("p (b h) -> p h b", h=MH)).then_inc(o_done, 1)


def load_split(nc, tag, ctx, block, tiles, hi, lo, slots):
    sem = sem_of(nc, ctx, tag, new_phase=False)
    raw = sb_of(nc, ctx, tag)("raw", [P, slots, T])
    t_in = [sem(f"t_in{s}") for s in range(slots)]
    hi_done, lo_done = sem("hi_done"), sem("lo_done")

    @block.sync
    def _(sp):
        for k, t in enumerate(tiles):
            if k >= slots:
                sp.wait_ge(lo_done, k - slots + 1)
            sp.dma_start(raw[:, k % slots], t).then_inc(t_in[k % slots], 16)

    @block.vector
    def _(dve):
        for k in range(len(tiles)):
            dve.wait_ge(t_in[k % slots], 16 * (k // slots + 1))
            dve.tensor_copy(hi[:, k], raw[:, k % slots]).then_inc(hi_done, 1)
            dve.wait_ge(hi_done, k + 1)
            dve.tensor_tensor(lo[:, k], raw[:, k % slots], hi[:, k].bitcast(F32), ALU.subtract).then_inc(lo_done, 1)

    return lambda pe, k: pe.wait_ge(lo_done, k + 1)


def merge(nc, d, ctx, block, x_hi, x_lo, make_x):
    sb, ps, sem = sb_of(nc, ctx, "mrg"), ps_of(nc, ctx, "mrg"), sem_of(nc, ctx, "mrg", new_phase=False)
    raw = sb("raw", [P, 2, KT, P])
    w_hi = sb("w_hi", [P, 2, KT, P], F32R)
    w_lo = sb("w_lo", [P, 2, KT, P], F32R)
    mg = sb("mg", [P, 2, 3, T])
    z = sb("z", [P, 2, T])
    acc = [ps(f"acc{s}", [P, NCH, 512]) for s in range(2)]
    raw_in = [sem("raw_in0"), sem("raw_in1")]
    mg_in = [sem("mg_in0"), sem("mg_in1")]
    z_out = [sem("z_out0"), sem("z_out1")]
    hi_done, lo_done, mm_done, ev_done, sg_done, z_done, ch = (
        sem(x) for x in ("hi_done", "lo_done", "mm_done", "ev_done", "sg_done", "z_done", "ch"))
    GROUPS = [(0, 0, KT, 0), (1, 0, 4, 8), (1, 4, 4, 12), (2, 0, KT, 0), (3, 0, 4, 8), (3, 4, 4, 12)]
    UNIT_DONE = (1, 3, 4, 6)

    def lo_part(pool, s):
        pool.tensor_tensor(w_lo[:, s], raw[:, s], w_hi[:, s].bitcast(F32), ALU.subtract).then_inc(lo_done, 1)

    @block.sync
    def _(sp):
        sp.sem_inc(ev_done, 2)
        for s in range(2):
            sp.dma_start(raw[:, s], d["w_up"][s]).then_inc(raw_in[s], 16)

    @block.scalar
    def _(act):
        for s in range(2):
            act.wait_ge(raw_in[s], 16)
            act.activation(w_hi[:, s], raw[:, s], ACT.Copy).then_inc(hi_done, 1)

    @block.gpsimd
    def _(pool):
        for s in range(2):
            pool.wait_ge(hi_done, s + 1)
            lo_part(pool, s)

    ready = make_x()

    @block.sync
    def _(sp):
        sp.sem_inc(z_out[0], 16)
        sp.sem_inc(z_out[1], 16)
        sp.sem_inc(z_done, 2)
        with sp.Fori(0, KT // 2) as i:
            for m in range(2):
                row = [sp.snap(i * 2 + (U_MG + 8 * b + m)) for b in range(3)]
                sp.wait_ge(z_done, i * 2 + (m + 1))
                for b in range(3):
                    sp.dma_start(mg[:, m, b], d["z"][bass.ds(row[b], 1)].rearrange("a p n -> p (a n)")).then_inc(mg_in[m], 16)
            for u in range(4):
                nxt = sp.snap(i * 4 + (u + 2))
                sp.wait_ge(lo_done, i * 4 + (u + 1))
                sp.dma_start(raw[:, u % 2], d["w_up"][bass.ds(nxt, 1)].rearrange("a p k n -> p (a k) n")).then_inc(raw_in[u % 2], 16)
                if u % 2:
                    cur = sp.snap(i * 2 + u // 2)
                    sp.wait_ge(z_done, i * 2 + (u // 2 + 3))
                    sp.dma_start(d["zm"][bass.ds(cur, 1)].rearrange("a p n -> p (a n)"), z[:, u // 2]).then_inc(z_out[u // 2], 16)
        for s in range(2):
            sp.wait_ge(z_out[s], 16 * (KT // 2 + 1))
            sp.wait_ge(raw_in[s], 16 * (KT + 1))

    @block.scalar
    def _(act):
        with act.Fori(0, KT // 2) as i:
            for u in range(4):
                if u % 2 == 0:
                    m = u // 2
                    act.wait_ge(mg_in[m], i * 48 + 48)
                    act.activation(mg[:, m], mg[:, m], ACT.Sigmoid).then_inc(sg_done, 1)
                act.wait_ge(raw_in[u % 2], i * 32 + (16 * (u // 2) + 32))
                act.wait_ge(mm_done, i * 6 + UNIT_DONE[u])
                act.activation(w_hi[:, u % 2], raw[:, u % 2], ACT.Copy).then_inc(hi_done, 1)

    @block.gpsimd
    def _(pool):
        with pool.Fori(0, KT // 2) as i:
            for u in range(4):
                pool.wait_ge(hi_done, i * 4 + (u + 3))
                lo_part(pool, u % 2)

    @block.tensor
    def _(pe):
        with pe.Fori(0, KT // 2) as i:
            for g, (u, k0, nk, x0) in enumerate(GROUPS):
                pe.wait_ge(lo_done, i * 4 + (u + 1))
                pe.wait_ge(ev_done, i * 6 + (g + 1))
                for k in range(nk):
                    ready(pe, x0 + k)
                    for n, (w, x) in enumerate(((w_hi, x_hi), (w_hi, x_lo), (w_lo, x_hi))):
                        for c in range(NCH):
                            mm = pe.matmul(acc[g % 2][:, c, 0:CW], w[:, u % 2, k0 + k, :], x[:, x0 + k, c * CW:(c + 1) * CW],
                                           start=(k + n == 0), stop=(k == nk - 1 and n == 2))
                mm.then_inc(mm_done, 1)

    @block.vector
    def _(dve):
        with dve.Fori(0, KT // 2) as i:
            for g in range(6):
                m, b = g // 3, g % 3
                a = acc[g % 2][:, :, 0:CW]
                gate = mg[:, m, b].rearrange("p (c n) -> p c n", c=NCH)
                zz = z[:, m].rearrange("p (c n) -> p c n", c=NCH)
                if b == 0:
                    dve.wait_ge(sg_done, i * 2 + (m + 1))
                    dve.wait_ge(z_out[m], i * 16 + 16)
                    dve.wait_ge(mm_done, i * 6 + (g + 1))
                    dve.tensor_tensor(zz, a, gate, ALU.mult).then_inc(ev_done, 1)
                else:
                    dve.wait_ge(mm_done, i * 6 + (g + 1))
                    dve.tensor_tensor(gate, a, gate, ALU.mult).then_inc(ev_done, 1)
                    dve.wait_ge(ev_done, i * 6 + (g + 3))
                    if b == 2:
                        dve.wait_ge(ch, i * 2 + (m + 1))
                    ins = dve.tensor_tensor(zz, zz, gate, ALU.add)
                    ins.then_inc(ch if b == 1 else z_done, 1)


def residual_norm(nc, d, per, ctx, block, ss, h, f_hi, f_lo):
    sb, sem = sb_of(nc, ctx, "res"), sem_of(nc, ctx, "res", new_phase=False)
    zo = sb("zo", [P, 2, T])
    sq = sb("sq", [P, 2, T])
    rstd = sb("rstd", [P, T])
    x_in = sem("x_in")
    z_in = [sem("z_in0"), sem("z_in1")]
    h_done, sq_done, ss_done, rt_done, rs_done, n_done, hi_done, lo_done = (
        sem(x) for x in ("h_done", "sq_done", "ss_done", "rt_done", "rs_done", "n_done", "hi_done", "lo_done"))

    @block.sync
    def _(sp):
        for k in range(KT):
            sp.dma_start(h[:, k], d["xT"][:, k, 0:T]).then_inc(x_in, 16)
        for k in range(KT):
            if k >= 2:
                sp.wait_ge(h_done, k - 1)
            sp.dma_start(zo[:, k % 2], d["zo"][k]).then_inc(z_in[k % 2], 16)

    @block.scalar
    def _(act):
        for k in range(KT):
            act.wait_ge(h_done, k + 1)
            if k >= 2:
                act.wait_ge(ss_done, k - 1)
            act.activation(sq[:, k % 2], h[:, k], ACT.Square).then_inc(sq_done, 1)
        act.wait_ge(ss_done, KT)
        act.activation(rstd[:].rearrange("p (c n) -> p c n", c=NCH), ss[:, :, 0:CW], ACT.Sqrt,
                       bias=per["eps"][:, 0:1], scale=1.0 / D).then_inc(rt_done, 1)
        for k in range(KT):
            act.wait_ge(n_done, k + 1)
            act.activation(f_hi[:, k], sq[:, k % 2], ACT.Copy).then_inc(hi_done, 1)

    @block.tensor
    def _(pe):
        for k in range(KT):
            pe.wait_ge(sq_done, k + 1)
            for c in range(NCH):
                mm = pe.matmul(ss[:, c, 0:CW], per["ones"][:], sq[:, k % 2, c * CW:(c + 1) * CW],
                               start=(k == 0), stop=(k == KT - 1))
            mm.then_inc(ss_done, 1)

    @block.vector
    def _(dve):
        dve.wait_ge(x_in, 16 * KT)
        for k in range(KT):
            dve.wait_ge(z_in[k % 2], 16 * (k // 2 + 1))
            dve.tensor_tensor(h[:, k], h[:, k], zo[:, k % 2], ALU.add).then_inc(h_done, 1)
        dve.wait_ge(rt_done, 1)
        dve.reciprocal(rstd[:], rstd[:]).then_inc(rs_done, 1)
        dve.wait_ge(rs_done, 1)
        for k in range(KT):
            if k >= 2:
                dve.wait_ge(lo_done, k - 1)
            dve.scalar_tensor_tensor(sq[:, k % 2], h[:, k], per["vec"][:, V_FFN + k:V_FFN + k + 1], rstd[:],
                                     ALU.mult, ALU.mult).then_inc(n_done, 1)

    @block.gpsimd
    def _(pool):
        for k in range(KT):
            pool.wait_ge(hi_done, k + 1)
            pool.tensor_tensor(f_lo[:, k], sq[:, k % 2], f_hi[:, k].bitcast(F32), ALU.subtract).then_inc(lo_done, 1)

    return lambda pe, k: pe.wait_ge(lo_done, k + 1)


def ffn(nc, d, ctx, block, acc, h, f_hi, f_lo, make_f):
    NG = 20
    sb, sem = sb_of(nc, ctx, "ffn"), sem_of(nc, ctx, "ffn", new_phase=False)
    raw = sb("raw", [P, 2, KT, P])
    w_hi = sb("w_hi", [P, 2, KT, P], F32R)
    w_lo = sb("w_lo", [P, 2, KT, P], F32R)
    sg = sb("sg", [P, 2, T])
    a = sb("a", [P, 2, T])
    a_hi = sb("a_hi", [P, 2, T], F32R)
    a_lo = sb("a_lo", [P, 2, T], F32R)
    raw_in = [sem("raw_in0"), sem("raw_in1")]
    hi_done, lo_done, mm_done, ev_done, sg_done, ahi_done, alo_done, y_out = (
        sem(x) for x in ("hi_done", "lo_done", "mm_done", "ev_done", "sg_done", "ahi_done", "alo_done", "y_out"))
    UNIT_FREE = (12, 20, NG + 1, NG + 2, NG + 3, NG + 4)

    @block.sync
    def _(sp):
        sp.sem_inc(ev_done, 2)
        for s in range(2):
            sp.dma_start(raw[:, s], d["w_ff"][s]).then_inc(raw_in[s], 16)

    ready = make_f()

    @block.sync
    def _(sp):
        with sp.Fori(0, FFG) as i:
            for u in range(6):
                nxt = sp.snap(i * 6 + (u + 2))
                sp.wait_ge(lo_done, i * 6 + (u + 1))
                sp.dma_start(raw[:, u % 2], d["w_ff"][bass.ds(nxt, 1)].rearrange("a p k n -> p (a k) n")).then_inc(raw_in[u % 2], 16)
        sp.wait_ge(ev_done, FFG * NG + 2)
        for k in range(KT):
            sp.dma_start(d["yT"][k], h[:, k]).then_inc(y_out, 16)
        sp.wait_ge(y_out, 16 * KT)
        for s in range(2):
            sp.wait_ge(raw_in[s], 16 * (3 * FFG + 1))

    @block.scalar
    def _(act):
        with act.Fori(0, FFG) as i:

            def w_part(u):
                act.wait_ge(raw_in[u % 2], i * 48 + (16 * (u // 2) + 16))
                act.wait_ge(mm_done, i * NG + UNIT_FREE[u])
                act.activation(w_hi[:, u % 2], raw[:, u % 2], ACT.Copy).then_inc(hi_done, 1)

            def sigma(j):
                act.wait_ge(mm_done, i * NG + (NG + 2 * j + 1))
                act.activation(sg[:, j].rearrange("p (c n) -> p c n", c=NCH), acc[0][:, :, 0:CW], ACT.Sigmoid).then_inc(sg_done, 1)

            def a_part(j):
                act.wait_ge(ev_done, i * NG + (2 * j + 4))
                act.wait_ge(mm_done, i * NG + (12 + 8 * j))
                act.activation(a_hi[:, j], a[:, j], ACT.Copy).then_inc(ahi_done, 1)

            w_part(0)
            w_part(1)
            sigma(0)
            w_part(2)
            a_part(0)
            w_part(3)
            sigma(1)
            w_part(4)
            a_part(1)
            w_part(5)

    @block.gpsimd
    def _(pool):
        with pool.Fori(0, FFG) as i:

            def w_part(u):
                pool.wait_ge(hi_done, i * 6 + (u + 1))
                pool.tensor_tensor(w_lo[:, u % 2], raw[:, u % 2], w_hi[:, u % 2].bitcast(F32), ALU.subtract).then_inc(lo_done, 1)

            def a_part(j):
                pool.wait_ge(ahi_done, i * 2 + (j + 1))
                pool.tensor_tensor(a_lo[:, j], a[:, j], a_hi[:, j].bitcast(F32), ALU.subtract).then_inc(alo_done, 1)

            w_part(0)
            w_part(1)
            w_part(2)
            a_part(0)
            w_part(3)
            w_part(4)
            a_part(1)
            w_part(5)

    @block.tensor
    def _(pe):
        pe.sem_inc(mm_done, NG)
        with pe.Fori(0, FFG) as i:
            for u in range(4):
                pe.wait_ge(lo_done, i * 6 + (u + 1))
                pe.wait_ge(ev_done, i * NG + (u + 1))
                for k in range(KT):
                    ready(pe, k)
                    for n, (w, x) in enumerate(((w_hi, f_hi), (w_hi, f_lo), (w_lo, f_hi))):
                        for c in range(NCH):
                            mm = pe.matmul(acc[u % 2][:, c, 0:CW], w[:, u % 2, k, :], x[:, k, c * CW:(c + 1) * CW],
                                           start=(k + n == 0), stop=(k == KT - 1 and n == 2))
                mm.then_inc(mm_done, 1)
            for j in range(2):
                pe.wait_ge(lo_done, i * 6 + (5 + j))
                pe.wait_ge(alo_done, i * 2 + (j + 1))
                for m in range(KT):
                    pe.wait_ge(ev_done, i * NG + (4 + 8 * j + m + 1))
                    for n, (w, x) in enumerate(((w_hi, a_hi), (w_hi, a_lo), (w_lo, a_hi))):
                        for c in range(NCH):
                            mm = pe.matmul(acc[m % 2][:, c, 0:CW], w[:, j, m, :], x[:, j, c * CW:(c + 1) * CW],
                                           start=(n == 0), stop=(n == 2))
                    mm.then_inc(mm_done, 1)

    @block.vector
    def _(dve):
        with dve.Fori(0, FFG) as i:
            for j in range(2):
                aj = a[:, j].rearrange("p (c n) -> p c n", c=NCH)
                dve.wait_ge(sg_done, i * 2 + (j + 1))
                dve.wait_ge(mm_done, i * NG + (12 + 8 * j))
                dve.tensor_tensor(aj, acc[0][:, :, 0:CW], sg[:, j].rearrange("p (c n) -> p c n", c=NCH), ALU.mult).then_inc(ev_done, 1)
                dve.wait_ge(ev_done, i * NG + (2 * j + 3))
                dve.wait_ge(mm_done, i * NG + (NG + 2 * j + 2))
                dve.tensor_tensor(aj, acc[1][:, :, 0:CW], aj, ALU.mult).then_inc(ev_done, 1)
            for g in range(16):
                m = g % 8
                dve.wait_ge(mm_done, i * NG + (NG + 5 + g))
                hm = h[:, m].rearrange("p (c n) -> p c n", c=NCH)
                dve.tensor_tensor(hm, acc[m % 2][:, :, 0:CW], hm, ALU.add).then_inc(ev_done, 1)


def outputs(nc, d, block, o):

    @block.gpsimd
    def _(pool):
        for n, src in enumerate((d["z"][U_CMPK], d["z"][U_CMPV], d["zn"][0], d["z"][U_SELV], d["zn"][1], d["z"][U_WINV])):
            pool.dma_start(d["kvT"][n], src).then_inc(o, 16)
        for h in range(MH):
            pool.dma_start(d["memT"][h], d["memn"][h]).then_inc(o, 16)
            pool.dma_start(d["memT"][MH + h], d["memz"][MH + h]).then_inc(o, 16)
        for b in range(NS):
            pool.dma_start(d["win_out"][b, 0:WIN - 1], d["win_in"][b, 1:WIN]).then_inc(o, 16)
        for j, src in enumerate((d["zn"][1], d["z"][U_WINV])):
            pool.dma_start(d["win_out"][:, WIN - 1, j * P:(j + 1) * P].rearrange("b p -> p b"), src[:, NP_:T],
                         allow_slow_non_contiguous=True).then_inc(o, 16)

    @block.sync
    def _(sp):
        sp.wait_ge(o, 16 * 24)


def program(nc, d):
    PHASE_SEMS["last"], PHASE_SEMS["now"] = [], []
    scratch = lambda name, shape: nc.dram_tensor(name, shape, F32, kind="Internal").ap()
    d["z"] = scratch("z", [NU_IN, P, T])
    d["zn"] = scratch("zn", [NHN, P, T])
    d["memz"] = scratch("memz", [2 * MH, P, NMEM])
    d["memn"] = scratch("memn", [MH, P, NMEM])
    d["gate_s"] = scratch("gate_s", [NS * 24, 1])
    d["vtok"] = scratch("vtok", [2, QT, P, P])
    d["memv"] = scratch("memv", [MH, 2, P, P])
    d["o_lru"] = scratch("o_lru", [KT, P, T])
    d["o_nsa"] = scratch("o_nsa", [R, P, T])
    d["o_mem"] = scratch("o_mem", [MH, P, T])
    d["zm"] = scratch("zm", [KT, P, T])
    d["zo"] = scratch("zo", [KT, P, T])
    d["dist"] = scratch("dist", [P, 8, RLEN])
    d["kcT"] = scratch("kcT", [P, (NS + 1) * NCK])
    d["vc"] = scratch("vc", [NCK, NS + 1, P])
    with ExitStack() as ctx:
        sb = sb_of(nc, ctx, "per")
        per = {"ident": sb("ident", [P, P]), "ones": sb("ones", [P, P]), "vec": sb("vec", [P, NV]), "eps": sb("eps", [P, 1]),
               "gate": sb("gate", [P, QT, 24]),
               "soft": [ctx.enter_context(nc.semaphore(f"soft{n}")) for n in range(31)]}
        with ExitStack() as part:
            sbh = sb_of(nc, part, "h")
            h_hi, h_lo = sbh("hi", [P, KT, XC], F32R), sbh("lo", [P, KT, XC], F32R)
            with ExitStack() as own:
                block = own.enter_context(nc.Block())
                bank = own.enter_context(nc.psum_tensor("in_bank", [P, 8, 512], F32))
                start_phase(nc, own, block, "in")

                h_ready = []

                def rows():
                    h_ready.append(normalise(nc, d, per, own, block, bank, h_hi, h_lo))
                    return h_ready[0]

                def tokens():
                    project(nc, "pin", own, block, d["w_in"], U_LX, h_hi, h_lo, 0, NCH, CW, d["z"],
                            [bank[:, 0:3], bank[:, 3:6]], rows)
                    return h_ready[0]

                project(nc, "pmem", own, block, d["w_mem"], 2 * MH, h_hi, h_lo, T, 1, NMEM, d["memz"],
                        [bank[:, 6:7], bank[:, 7:8]], tokens)
            with ExitStack() as own:
                block = own.enter_context(nc.Block())
                start_phase(nc, own, block, "mid")
                bank = own.enter_context(nc.psum_tensor("mid_bank", [P, 8, 512], F32))
                soft = per["soft"][18:30]
                wait_hn = head_norm(nc, "hn", own, block, [bank[:, 0:3], bank[:, 3:6]], d["z"], U_SELK, NHN, T, NCH,
                                    d["mats"], d["gains"], d["zn"])
                wait_hm = head_norm(nc, "hm", own, block, [bank[:, 6:7], bank[:, 7:8]], d["memz"], 0, MH, NMEM, 1,
                                    d["mats_m"], d["gains_m"], d["memn"])

                @block.tensor
                def _(pe):
                    wait_hn(pe)
                    wait_hm(pe)

                distance_bias(nc, d, own, block, bank[:, 6:8], soft[0:2])
                to_tokens(nc, "tm", per, own, block, [bank[:, s, 0:2 * P].rearrange("p (t n) -> p t n", n=P) for s in (4, 5)],
                          soft[2:6], d["memz"], MH, MH, NMEM, d["memv"])
                wait_g = gates(nc, d, per, own, block, bank, soft[6:8], h_hi, h_lo)

                @block.tensor
                def _(pe):
                    wait_g(pe)

                to_tokens(nc, "tv", per, own, block,
                          [bank[:, 2 * s:2 * s + 2].rearrange("p b (t n) -> p (b t) n", n=P) for s in range(2)],
                          soft[8:12], d["z"], U_SELV, 2, NP_, d["vtok"])
            compress(nc, d, per)
            prompt_attention(nc, d, per, h_hi, h_lo)
            merge_gates_and_recurrence(nc, d, h_hi, h_lo)
        with ExitStack() as part:
            bank = [part.enter_context(nc.psum_tensor(f"bank{n}", [P, 512], F32)) for n in range(8)]
            block = part.enter_context(nc.Block())
            start_phase(nc, part, block, "att2")
            sample_attention(nc, d, per, part, block, bank)
            outputs(nc, d, block, per["soft"][30])
            sample_memory(nc, d, per, part, block, bank)
        with ExitStack() as part:
            sbx = sb_of(nc, part, "x")
            x_hi, x_lo = sbx("hi", [P, 16, T], F32R), sbx("lo", [P, 16, T], F32R)
            block = part.enter_context(nc.Block())
            start_phase(nc, part, block, "merge")
            branches = [d["o_lru"][k] for k in range(8)] + [d["o_nsa"][k] for k in range(4)] + [d["o_mem"][k] for k in range(4)]
            merge(nc, d, part, block, x_hi, x_lo, lambda: load_split(nc, "lsx", part, block, branches, x_hi, x_lo, 3))
        with ExitStack() as part:
            sbx = sb_of(nc, part, "m")
            x_hi, x_lo = sbx("hi", [P, KT, T], F32R), sbx("lo", [P, KT, T], F32R)
            block = part.enter_context(nc.Block())
            start_phase(nc, part, block, "out")
            acc = [part.enter_context(nc.psum_tensor(f"wo_acc{s}", [P, NCH, 512], F32)) for s in range(2)]
            project(nc, "pwo", part, block, d["w_o"], KT, x_hi, x_lo, 0, NCH, CW, d["zo"], acc,
                    lambda: load_split(nc, "lsm", part, block, [d["zm"][k] for k in range(KT)], x_hi, x_lo, 8))
        with ExitStack() as part:
            sbx = sb_of(nc, part, "f")
            h = sbx("h", [P, KT, T])
            f_hi, f_lo = sbx("hi", [P, KT, T], F32R), sbx("lo", [P, KT, T], F32R)
            block = part.enter_context(nc.Block())
            start_phase(nc, part, block, "ffn")
            acc = [part.enter_context(nc.psum_tensor(f"ffn_acc{s}", [P, NCH, 512], F32)) for s in range(2)]
            ffn(nc, d, part, block, acc, h, f_hi, f_lo,
                lambda: residual_norm(nc, d, per, part, block, acc[0], h, f_hi, f_lo))



def _bucket(n):
    if n < 16:
        return n
    return min(31, 16 + int(math.log(n / 16) / math.log(8) * 16 + 1e-9))


def _constants():
    f = np.float32
    hot = np.zeros((33, RLEN), f)
    for i in range(RLEN):
        dist = RMAX - i
        if dist < 0:
            hot[32, i] = NEGV
        else:
            hot[_bucket(dist), i] += 1
            hot[31, i] -= 1
    blk64 = np.kron(np.eye(2, dtype=f), np.ones((HD, HD), f))
    one = np.ones((P, P), f)

    def mat(m, eps):
        return np.concatenate([m, np.full((P, 1), eps, f)], 1)

    qi, xi, ui = np.arange(P)[:, None], np.arange(P)[None, :], np.arange(CU)[None, :]
    return {
        "ident": np.eye(P, dtype=f), "ones": one, "hot": hot,
        "mats": np.stack([mat(blk64 / 64, EPS)] * 2 + [mat(blk64, 64 * EPS)] * 4 + [mat(one / 128, EPS)] * 4),
        "mats_m": np.stack([mat(one / 128, EPS)] * 4),
        "avg": mat(blk64 / 64, EPS),
        "wmask": np.where(xi > qi, 0, NEGV).astype(f),
        "cmask": (qi >= 16 * (ui - 56) + 31).astype(f),
        "grp": np.kron(np.eye(16, dtype=f), np.ones((4, 4), f)),
        "blk": np.tile(np.arange(1, 17, dtype=f), (64, 1)),
    }


def _layout(x):
    x = {k: np.asarray(v) for k, v in x.items()}
    c = _constants()

    def fm(a):
        return a.T.reshape(-1, P, a.shape[0]).transpose(1, 0, 2)

    def units(w, cols=None):
        w = w if cols is None else w[:, cols]
        return w.reshape(-1, P, w.shape[1] // P, P).transpose(2, 1, 0, 3)

    def cols8(v):
        return v.reshape(-1, P).T

    w_in = x["w_in"][0]
    zero = np.zeros((2, P, KT, P), np.float32)
    starts = [2560, 2688, 2944, 3200, 2816, 3072]
    cols = [np.arange(s, s + P) for s in starts]
    cols += [np.concatenate([2048 + r * HD + np.arange(HD), 2048 + (R + r) * HD + np.arange(HD)]) for r in range(R)]
    cols += [np.arange(3352 + P * h, 3352 + P * (h + 1)) for h in range(MH)]
    cols += [np.arange(P * m, P * (m + 1)) for m in range(16)]
    cols += [np.arange(3864 + P * m, 3864 + P * (m + 1)) for m in range(24)]
    order = np.concatenate([np.concatenate([r * HD + np.arange(HD), (R + r) * HD + np.arange(HD)]) for r in range(R)])
    ua, ub, um = units(x["w_up_a"][0]), units(x["w_up_b"][0][order]), units(x["w_up_m"][0])
    ubm = np.concatenate([ub, um], 2)
    w_up = np.concatenate([np.stack([ua, ubm], 1).reshape(16, P, KT, P), zero])
    gu = np.stack([units(x["w_ffn_gate"][0]), units(x["w_ffn_up"][0])], 1).reshape(FFG, 4, P, KT, P)
    dn = x["w_ffn_down"][0].reshape(FFG, 2, P, KT, P)
    w_ff = np.concatenate([np.concatenate([gu, dn], 1).reshape(6 * FFG, P, KT, P), zero])
    dup = lambda g: np.concatenate([g, g])[:, None]
    gk = x["g_nsa_k"][0]
    gq, gm = dup(x["g_nsa_q"][0]), x["g_mem_q"][0][:, None]
    pool = x["cache_cmp_kv"][0]
    npool = pool.shape[0]
    sel = x["cache_sel_kv"][0].reshape(npool, P, 2, P)
    win = x["cache_win_kv"][0]
    wk = win.reshape(NS, WIN, 2, P)
    mem = x["cache_mem_kv"][0]
    out = {
        "xT": np.concatenate([fm(x["x_prompt"][0]), fm(x["x_sample"][:, 0]), fm(x["mem_prompt"][0])], 2),
        "vec": np.concatenate([cols8(x["norm_mix"][0]), cols8(x["norm_mem"][0]), cols8(x["norm_ffn"][0]),
                               x["g_mem_k"][0][:, None], cols8(x["pe_cmp_k"][0]), cols8(x["pe_cmp_v"][0])], 1),
        "w_in": np.concatenate([units(w_in, np.concatenate(cols)), zero]), "w_mem": units(x["w_mem_kv"][0]),
        "w_ng": w_in[:, 3328:3352].reshape(KT, P, 24).transpose(1, 0, 2),
        "gains": np.stack([dup(gk[1]), dup(gk[2])] + [gq] * 4 + [gm] * 4),
        "gains_m": np.stack([x["g_mem_k"][0][:, None]] * 4),
        "nm_kc": np.concatenate([c.pop("avg"), dup(gk[0])], 1),
        "rel": np.concatenate([np.repeat(x["rel_bias"][:, :, None], P, 2), np.ones((1, 8, P), np.float32)]),
        "st": np.concatenate([x["state_conv"][0].transpose(2, 1, 0).reshape(KT, P, 3 * NS).transpose(1, 0, 2),
                              fm(x["state_lru_h"][0])], 2),
        "par": np.stack([cols8(v) for v in (*x["conv_w"][0], x["conv_b"][0], x["b_lru_a"][0], x["b_lru_i"][0],
                                            x["lru_lambda"][0])], 2),
        "w_a": x["w_lru_a"][0].reshape(4, 2, P, 256).transpose(0, 2, 1, 3),
        "w_i": x["w_lru_i"][0].reshape(4, 2, P, 256).transpose(0, 2, 1, 3),
        "w_c1": np.stack([x["w_cmp_k1"][0], x["w_cmp_v1"][0]]).reshape(2, 16, P, P).transpose(0, 2, 1, 3),
        "w_c2": np.stack([x["w_cmp_k2"][0], x["w_cmp_v2"][0]]),
        "cmp_pool": pool.reshape(npool, 8, 8, 2, 2, 2, HD).transpose(0, 3, 6, 4, 5, 2, 1).reshape(npool, P, 256),
        "sel_kT": sel[:, :, 0].transpose(0, 2, 1), "sel_v": sel[:, :, 1],
        "winkT": wk[:, :, 0].transpose(0, 2, 1), "win_v": wk[:, :, 1].reshape(NS, WIN // P, P, P),
        "win_in": win.reshape(NS, WIN, 256),
        "mem_kT": mem[:, :, 0].transpose(0, 3, 2, 1), "mem_v": mem[:, :, 1].reshape(NS, 2, P, MH, P),
        "page_table": x["page_table"].reshape(1, NS * PAGES),
        "w_up": w_up, "w_o": units(x["w_o"][0]), "w_ff": w_ff,
    }
    out.update(c)
    return {k: np.ascontiguousarray(v) for k, v in out.items()}


_OUTS = {"yT": (KT, P, T), "kvT": (6, P, T), "memT": (2 * MH, P, NMEM), "win_out": (NS, WIN, 256),
         "hT": (KT, P, 1 + NS), "cvT": (KT, P, 3), "cvsT": (KT, P, 3 * NS)}


def kernel(**inputs):
    import concourse.bacc as _bacc
    from concourse.bass_utils import run_bass_kernel_spmd as _run

    nc = _bacc.Bacc("TRN2", target_bir_lowering=False, num_devices=1)
    arrays, d = {}, {}
    for name, a in _layout(inputs).items():
        arrays[f"in_{name}"] = a
        d[name] = nc.dram_tensor(f"in_{name}", a.shape, mybir.dt.from_np(a.dtype), kind="ExternalInput").ap()
    for name, shape in _OUTS.items():
        d[name] = nc.dram_tensor(f"out_{name}", shape, F32, kind="ExternalOutput").ap()
    program(nc, d)
    r = _run(nc, [arrays], core_ids=[0]).results[0]
    got = {name: np.asarray(r[f"out_{name}"]) for name in _OUTS}

    y = got["yT"].reshape(D, T).T
    kv = got["kvT"].reshape(3, 2, P, T).transpose(0, 3, 1, 2).reshape(3, T, 2, G, HD)
    mem = got["memT"].reshape(2, MH, P, NMEM).transpose(3, 0, 1, 2)
    h = got["hT"].reshape(D, 1 + NS).T
    cv = got["cvT"].reshape(D, 3).T
    cvs = got["cvsT"].reshape(D, 3, NS).transpose(2, 1, 0)
    res = (y[None, :NP_], y[NP_:, None], kv[0][None, None, :NP_], kv[0][None, NP_:, None],
           kv[1][None, None, :NP_], kv[1][None, NP_:, None], kv[2][None, None, NP_ - WIN:NP_],
           got["win_out"].reshape(1, NS, WIN, 2, G, HD), mem[None, None], h[None, 0:1], h[None, 1:], cv[None, None], cvs[None])
    return tuple(np.ascontiguousarray(a) for a in res)
```
